# Optimizing a Trainium2 kernel written in Bass

```python
import math
import jax, jax.numpy as jnp
from jax import lax
import numpy as np
import jax
import jax.numpy as jnp

D_MODEL = 1024
BATCH = 1
SEQ = 256
DEPTH = 2

N_A = DEPTH // 2
N_B = DEPTH - N_A
HEAD_DIM = 64
CHUNK = 128
N_SG = 12
SG_WIDTH = N_SG * HEAD_DIM
DIL_PAIRS = ((128, 1), (512, 4), (2048, 16))
HEADS_PER_DIL = 4
N_DIL_HEADS = HEADS_PER_DIL * len(DIL_PAIRS)
DIL_Q_WIDTH = N_DIL_HEADS * HEAD_DIM
DIL_OUT_WIDTH = HEADS_PER_DIL * HEAD_DIM
N_MEM = 256
MEM_HEADS = 4
MEM_WIDTH = MEM_HEADS * HEAD_DIM
N_EXPERTS = 16
N_EXPERT_GROUPS = 4
EXPERTS_PER_GROUP = N_EXPERTS // N_EXPERT_GROUPS
TOP_K = 2
D_EXPERT = 1024
MOE_BLOCK = 128
ALPHA = (2 * DEPTH) ** 0.25
BETA = (8 * DEPTH) ** -0.25
LN_EPS = 1e-5
ATT_SCALE = 1.0 / math.sqrt(HEAD_DIM)


def layer_norm(x, g, b):
    xf = x.astype(jnp.float32)
    mu = jnp.mean(xf, -1, keepdims=True)
    var = jnp.mean(jnp.square(xf - mu), -1, keepdims=True)
    return ((xf - mu) * lax.rsqrt(var + LN_EPS)).astype(x.dtype) * g + b

def alibi_slopes():
    return 2.0 ** (-8.0 * jnp.arange(1, N_DIL_HEADS + 1, dtype=jnp.float32) / N_DIL_HEADS)

def spatial_gating(u, v, w_s, b_s):
    B, S, G, Dh = v.shape
    vc = v.reshape(B, S // CHUNK, CHUNK, G, Dh)
    causal = jnp.tril(jnp.ones((CHUNK, CHUNK), bool))
    w = jnp.where(causal[None], w_s, 0).astype(v.dtype)
    s = jnp.einsum('gpq,bcqgd->bcpgd', w, vc) + b_s.T[None, None, :, :, None].astype(v.dtype)
    return u * s.reshape(B, S, G, Dh)

def dilated_branch(q, k, v, window, dilation, slopes):
    B, S, H, Dh = q.shape
    steps = window // dilation
    L = S // dilation
    N = B * dilation

    def by_residue(t):
        return t.reshape(B, L, dilation, H, Dh).transpose(0, 2, 3, 1, 4).reshape(N, H, L, Dh)

    qr, kr, vr = by_residue(q), by_residue(k), by_residue(v)
    nb = -(-L // CHUNK)
    pad = nb * CHUNK - L
    qr = jnp.pad(qr, ((0, 0), (0, 0), (0, pad), (0, 0)))
    kr = jnp.pad(kr, ((0, 0), (0, 0), (CHUNK, pad), (0, 0)))
    vr = jnp.pad(vr, ((0, 0), (0, 0), (CHUNK, pad), (0, 0)))
    qb = qr.reshape(N, H, nb, CHUNK, Dh)
    kb = kr.reshape(N, H, nb + 1, CHUNK, Dh)
    vb = vr.reshape(N, H, nb + 1, CHUNK, Dh)
    kband = jnp.concatenate([kb[:, :, :-1], kb[:, :, 1:]], axis=3)
    vband = jnp.concatenate([vb[:, :, :-1], vb[:, :, 1:]], axis=3)
    s = jnp.einsum('nhbqd,nhbkd->nhbqk', qb, kband).astype(jnp.float32) * ATT_SCALE
    iq = jnp.arange(CHUNK)[:, None]
    jk = jnp.arange(2 * CHUNK)[None, :]
    rel = CHUNK + iq - jk
    key_pos = (jnp.arange(nb)[:, None, None] - 1) * CHUNK + jk[None]
    valid = (rel >= 0)[None] & (rel <= steps)[None] & (key_pos >= 0)
    bias = -slopes[:, None, None, None] * (dilation * rel).astype(jnp.float32)[None, None]
    s = jnp.where(valid[None, None], s + bias[None], -jnp.inf)
    m = jnp.max(s, -1, keepdims=True)
    p = jnp.exp(s - m)
    l = jnp.sum(p, -1, keepdims=True)
    o = jnp.einsum('nhbqk,nhbkd->nhbqd', (p / l).astype(v.dtype), vband)
    lse = (m + jnp.log(l))[..., 0]
    o = o.reshape(N, H, nb * CHUNK, Dh)[:, :, :L]
    lse = lse.reshape(N, H, nb * CHUNK)[:, :, :L]
    o = o.reshape(B, dilation, H, L, Dh).transpose(0, 3, 1, 2, 4).reshape(B, S, H, Dh)
    lse = lse.reshape(B, dilation, H, L).transpose(0, 3, 1, 2).reshape(B, S, H)
    return o, lse

def dilated_mixture(q, k, v, slopes):
    outs, lses = [], []
    for g, (window, dilation) in enumerate(DIL_PAIRS):
        hs = slice(g * HEADS_PER_DIL, (g + 1) * HEADS_PER_DIL)
        o, lse = dilated_branch(q[:, :, hs], k[:, :, hs], v[:, :, hs], window, dilation, slopes[hs])
        outs.append(o)
        lses.append(lse)
    O = jnp.stack(outs, 0)
    wts = jax.nn.softmax(jnp.stack(lses, 0), 0)
    return jnp.sum(wts[..., None].astype(O.dtype) * O, 0)

def memory_attention(q, mk, mv):
    s = jnp.einsum('bshd,bmhd->bhsm', q, mk).astype(jnp.float32) * ATT_SCALE
    p = jax.nn.softmax(s, -1).astype(mv.dtype)
    return jnp.einsum('bhsm,bmhd->bshd', p, mv)

def route(h, w_router, b_router):
    T = h.shape[0]
    probs = jax.nn.softmax((h @ w_router).astype(jnp.float32), -1)
    sel = probs + b_router.astype(jnp.float32)
    grp = sel.reshape(T, N_EXPERT_GROUPS, EXPERTS_PER_GROUP)
    grp_score = jnp.sum(lax.top_k(grp, TOP_K)[0], -1)
    g_idx = jnp.argmax(grp_score, -1).astype(jnp.int32)
    in_grp = jnp.take_along_axis(grp, g_idx[:, None, None], axis=1)[:, 0]
    _, local = lax.top_k(in_grp, TOP_K)
    expert = g_idx[:, None] * EXPERTS_PER_GROUP + local.astype(jnp.int32)
    gate = jnp.take_along_axis(probs, expert, 1)
    gate = gate / jnp.sum(gate, -1, keepdims=True)
    return expert, gate

def moe_ffn(h, expert, gate, w_gate, w_up, w_down):
    T, D = h.shape
    n_slots = T * TOP_K
    e_flat = expert.reshape(-1)
    g_flat = gate.reshape(-1)
    tok = jnp.arange(n_slots, dtype=jnp.int32) // TOP_K
    order = jnp.argsort(e_flat)
    e_s, tok_s, g_s = e_flat[order], tok[order], g_flat[order]
    counts = jnp.bincount(e_flat, length=N_EXPERTS)
    starts = jnp.cumsum(counts) - counts
    padded = (counts + MOE_BLOCK - 1) // MOE_BLOCK * MOE_BLOCK
    pad_ends = jnp.cumsum(padded)
    pad_starts = pad_ends - padded
    dest = pad_starts[e_s] + (jnp.arange(n_slots) - starts[e_s])
    n_pad = n_slots + N_EXPERTS * MOE_BLOCK
    n_blocks = n_pad // MOE_BLOCK
    slot_tok = jnp.zeros((n_pad,), jnp.int32).at[dest].set(tok_s)
    slot_gate = jnp.zeros((n_pad,), jnp.float32).at[dest].set(g_s)
    block_start = jnp.arange(n_blocks) * MOE_BLOCK
    block_expert = jnp.minimum(jnp.searchsorted(pad_ends, block_start, side='right'), N_EXPERTS - 1)
    xb = h[slot_tok].reshape(n_blocks, MOE_BLOCK, D)

    def expert_block(args):
        xblk, e = args
        return (jax.nn.silu(xblk @ w_gate[e]) * (xblk @ w_up[e])) @ w_down[e]

    yb = lax.map(expert_block, (xb, block_expert))
    y = yb.reshape(n_pad, D) * slot_gate[:, None].astype(h.dtype)
    return jnp.zeros_like(h).at[slot_tok].add(y)

def _normal(k, shape, scale):
    return jax.random.normal(k, shape, jnp.float32) * scale

def first_inputs(seed: int = 0) -> dict:
    key = jax.random.key(seed)
    ks = jax.random.split(key, 24)
    D = D_MODEL
    return {
        "x": _normal(ks[0], (BATCH, SEQ, D), 1.0),
        "mem": _normal(ks[1], (BATCH, N_MEM, D), 1.0),
        "w_in_a": _normal(ks[2], (N_A, D, 2 * SG_WIDTH + MEM_WIDTH), D ** -0.5),
        "w_out_a": _normal(ks[3], (N_A, SG_WIDTH + MEM_WIDTH, D), (SG_WIDTH + MEM_WIDTH) ** -0.5 * BETA),
        "sg_ln_g": 1.0 + _normal(ks[4], (N_A, SG_WIDTH), 0.02),
        "sg_ln_b": _normal(ks[5], (N_A, SG_WIDTH), 0.02),
        "sg_w": _normal(ks[6], (N_A, N_SG, CHUNK, CHUNK), 0.5 * CHUNK ** -0.5),
        "sg_b": 1.0 + _normal(ks[7], (N_A, N_SG, CHUNK), 0.1),
        "w_in_b": _normal(ks[8], (N_B, D, DIL_Q_WIDTH + MEM_WIDTH), D ** -0.5),
        "w_out_b": _normal(ks[9], (N_B, DIL_OUT_WIDTH + MEM_WIDTH, D), (DIL_OUT_WIDTH + MEM_WIDTH) ** -0.5 * BETA),
        "w_k_shared": _normal(ks[10], (D, DIL_Q_WIDTH), D ** -0.5),
        "w_v_shared": _normal(ks[11], (D, DIL_Q_WIDTH), D ** -0.5 * BETA),
        "w_mem_k": _normal(ks[12], (DEPTH, D, MEM_WIDTH), D ** -0.5),
        "w_mem_v": _normal(ks[13], (DEPTH, D, MEM_WIDTH), D ** -0.5 * BETA),
        "ln1_g": 1.0 + _normal(ks[14], (DEPTH, D), 0.02),
        "ln1_b": _normal(ks[15], (DEPTH, D), 0.02),
        "ln2_g": 1.0 + _normal(ks[16], (DEPTH, D), 0.02),
        "ln2_b": _normal(ks[17], (DEPTH, D), 0.02),
        "w_router": _normal(ks[18], (D, N_EXPERTS), D ** -0.5),
        "b_router": _normal(ks[19], (N_EXPERTS,), 0.01),
        "w_gate": _normal(ks[20], (DEPTH, N_EXPERTS, D, D_EXPERT), D ** -0.5),
        "w_up": _normal(ks[21], (DEPTH, N_EXPERTS, D, D_EXPERT), D ** -0.5),
        "w_down": _normal(ks[22], (DEPTH, N_EXPERTS, D_EXPERT, D), D_EXPERT ** -0.5 * BETA),
    }

def first_block(x, mem, w_in_a, w_out_a, sg_ln_g, sg_ln_b, sg_w, sg_b, w_in_b, w_out_b,
              w_k_shared, w_v_shared, w_mem_k, w_mem_v, ln1_g, ln1_b, ln2_g, ln2_b,
              w_router, b_router, w_gate, w_up, w_down):
    B, S, D = x.shape
    M = mem.shape[1]
    slopes = alibi_slopes()
    k_sh = None
    v_sh = None
    for layer in range(DEPTH):
        mk = (mem @ w_mem_k[layer]).reshape(B, M, MEM_HEADS, HEAD_DIM)
        mv = (mem @ w_mem_v[layer]).reshape(B, M, MEM_HEADS, HEAD_DIM)
        if layer < N_A:
            a = layer
            proj = x @ w_in_a[a]
            u = jax.nn.gelu(proj[..., :SG_WIDTH], approximate=False)
            gv = jax.nn.gelu(proj[..., SG_WIDTH:2 * SG_WIDTH], approximate=False)
            qm = proj[..., 2 * SG_WIDTH:].reshape(B, S, MEM_HEADS, HEAD_DIM)
            gv = layer_norm(gv, sg_ln_g[a], sg_ln_b[a])
            mix = spatial_gating(u.reshape(B, S, N_SG, HEAD_DIM), gv.reshape(B, S, N_SG, HEAD_DIM),
                                 sg_w[a], sg_b[a]).reshape(B, S, SG_WIDTH)
            mo = memory_attention(qm, mk, mv).reshape(B, S, MEM_WIDTH)
            att = jnp.concatenate([mix, mo], -1) @ w_out_a[a]
        else:
            bl = layer - N_A
            if bl == 0:
                k_sh = (x @ w_k_shared).reshape(B, S, N_DIL_HEADS, HEAD_DIM)
                v_sh = (x @ w_v_shared).reshape(B, S, N_DIL_HEADS, HEAD_DIM)
            proj = x @ w_in_b[bl]
            q = proj[..., :DIL_Q_WIDTH].reshape(B, S, N_DIL_HEADS, HEAD_DIM)
            qm = proj[..., DIL_Q_WIDTH:].reshape(B, S, MEM_HEADS, HEAD_DIM)
            mix = dilated_mixture(q, k_sh, v_sh, slopes).reshape(B, S, DIL_OUT_WIDTH)
            mo = memory_attention(qm, mk, mv).reshape(B, S, MEM_WIDTH)
            att = jnp.concatenate([mix, mo], -1) @ w_out_b[bl]
        x = layer_norm(ALPHA * x + att, ln1_g[layer], ln1_b[layer])
        h = x.reshape(B * S, D)
        expert, gate = route(h, w_router, b_router)
        ffn = moe_ffn(h, expert, gate, w_gate[layer], w_up[layer], w_down[layer]).reshape(B, S, D)
        x = layer_norm(ALPHA * x + ffn, ln2_g[layer], ln2_b[layer])
    return x


DEPTH_2 = 1

GRID_W = 64
MEM_LEN = 256
N_BRANCHES = 3
RET_HEADS = 4
RET_QK_DIM = 128
RET_V_DIM = 256
RET_CHUNK = 128
ROPE_BASE = 10000.0
NA_HEADS = 8
NA_HEAD_DIM = 64
NA_ROWS = 8
NA_COLS = 16
XA_HEADS = 4
XA_HEAD_DIM = 128
MOE_GROUPS = 4
MOE_EXPERTS_PER_GROUP = 4
MOE_TOP_K = 2
MOE_D_FF = 512
RMS_EPS = 1e-6
GN_EPS = 1e-5

RET_QK_WIDTH = RET_HEADS * RET_QK_DIM
RET_V_WIDTH = RET_HEADS * RET_V_DIM
NA_WIDTH = NA_HEADS * NA_HEAD_DIM
XA_WIDTH = XA_HEADS * XA_HEAD_DIM
IN_SPLITS = (RET_QK_WIDTH, RET_QK_WIDTH, RET_V_WIDTH, RET_V_WIDTH, NA_WIDTH, NA_WIDTH, NA_WIDTH, XA_WIDTH, N_BRANCHES * D_MODEL)
IN_WIDTH = 2 * RET_QK_WIDTH + 2 * RET_V_WIDTH + 3 * NA_WIDTH + XA_WIDTH + N_BRANCHES * D_MODEL


def _rmsnorm(x, g):
    xf = x.astype(jnp.float32)
    y = xf * lax.rsqrt(jnp.mean(xf * xf, axis=-1, keepdims=True) + RMS_EPS)
    return (y * g.astype(jnp.float32)).astype(x.dtype)

def _rope(a):
    seq, dh = a.shape[1], a.shape[-1]
    half = dh // 2
    inv_freq = ROPE_BASE ** (-jnp.arange(half, dtype=jnp.float32) / half)
    ang = jnp.arange(seq, dtype=jnp.float32)[:, None] * inv_freq[None, :]
    cos = jnp.cos(ang)[None, :, None, :]
    sin = jnp.sin(ang)[None, :, None, :]
    a1, a2 = a[..., :half], a[..., half:]
    return jnp.concatenate([a1 * cos - a2 * sin, a1 * sin + a2 * cos], axis=-1)

def _retention_one_direction(q, k, v, log_gamma, strict):
    b, h, s, dk = q.shape
    dv = v.shape[-1]
    c = RET_CHUNK
    n = s // c
    qc = q.reshape(b, h, n, c, dk)
    kc = k.reshape(b, h, n, c, dk)
    vc = v.reshape(b, h, n, c, dv)
    pos = jnp.arange(c, dtype=jnp.float32)
    diff = pos[:, None] - pos[None, :]
    mask = (diff > 0) if strict else (diff >= 0)
    decay = jnp.where(mask[None], jnp.exp(jnp.where(mask, diff, 0.0)[None] * log_gamma[:, None, None]), 0.0)
    scores = jnp.einsum('bhnid,bhnjd->bhnij', qc, kc) * decay[None, :, None]
    y_inner = jnp.einsum('bhnij,bhnje->bhnie', scores, vc)
    k_decay = jnp.exp((c - 1 - pos)[None, :] * log_gamma[:, None])
    q_decay = jnp.exp((pos + 1)[None, :] * log_gamma[:, None])
    chunk_decay = jnp.exp(c * log_gamma)[None, :, None, None]
    kv = jnp.einsum('bhnjd,hj,bhnje->bhnde', kc, k_decay, vc)

    def step(state, kv_chunk):
        return state * chunk_decay + kv_chunk, state

    _, prev = lax.scan(step, jnp.zeros((b, h, dk, dv), jnp.float32), jnp.moveaxis(kv, 2, 0))
    prev = jnp.moveaxis(prev, 0, 2)
    y_cross = jnp.einsum('bhnid,hi,bhnde->bhnie', qc, q_decay, prev)
    return (y_inner + y_cross).reshape(b, h, s, dv)

def _retention_branch(rq, rk, rv, rg, dec_f, dec_b, gn_gain, w_o):
    b, s, _ = rq.shape
    q = _rope(rq.reshape(b, s, RET_HEADS, RET_QK_DIM).astype(jnp.float32)) * (RET_QK_DIM ** -0.5)
    k = _rope(rk.reshape(b, s, RET_HEADS, RET_QK_DIM).astype(jnp.float32))
    v = rv.reshape(b, s, RET_HEADS, RET_V_DIM).astype(jnp.float32)
    q, k, v = q.transpose(0, 2, 1, 3), k.transpose(0, 2, 1, 3), v.transpose(0, 2, 1, 3)
    lg_f = jax.nn.log_sigmoid(dec_f.astype(jnp.float32))
    lg_b = jax.nn.log_sigmoid(dec_b.astype(jnp.float32))
    y_fwd = _retention_one_direction(q, k, v, lg_f, False)
    y_bwd = jnp.flip(_retention_one_direction(jnp.flip(q, 2), jnp.flip(k, 2), jnp.flip(v, 2), lg_b, True), 2)
    y = y_fwd + y_bwd
    mu = jnp.mean(y, axis=-1, keepdims=True)
    var = jnp.mean(jnp.square(y - mu), axis=-1, keepdims=True)
    y = (y - mu) * lax.rsqrt(var + GN_EPS)
    y = y.transpose(0, 2, 1, 3).reshape(b, s, RET_V_WIDTH) * gn_gain.astype(jnp.float32)
    return (jax.nn.silu(rg) * y.astype(rg.dtype)) @ w_o

def _neighbourhood_attention(nq, nk, nv, rpb):
    b, s, _ = nq.shape
    rows_n = s // GRID_W
    w = GRID_W
    kr = min(NA_ROWS, rows_n)
    kc = NA_COLS

    def to_grid(a):
        return a.reshape(b, rows_n, w, NA_HEADS, NA_HEAD_DIM).transpose(0, 3, 1, 2, 4)

    qg, kg, vg = to_grid(nq), to_grid(nk), to_grid(nv)
    rows = jnp.arange(rows_n)
    row_start = jnp.clip(rows - kr // 2, 0, rows_n - kr)
    row_idx = row_start[:, None] + jnp.arange(kr)[None, :]
    cols = jnp.arange(w)
    col_start = jnp.clip(cols - kc // 2, 0, w - kc)
    col_off = cols[None, :] - col_start[:, None]
    col_mask = (col_off >= 0) & (col_off < kc)
    k_rows = jnp.take(kg, row_idx, axis=2)
    v_rows = jnp.take(vg, row_idx, axis=2)
    sc = jnp.einsum('bhrqd,bhrwkd->bhrqwk', qg, k_rows).astype(jnp.float32) * (NA_HEAD_DIM ** -0.5)
    rel_r = row_idx - rows[:, None] + (NA_ROWS - 1)
    rel_c = jnp.clip(cols[None, :] - cols[:, None], -(kc - 1), kc - 1) + (kc - 1)
    bias = rpb[:, rel_r[:, None, :, None], rel_c[None, :, None, :]].astype(jnp.float32)
    sc = jnp.where(col_mask[:, None, :], sc + bias, -jnp.inf)
    p = jax.nn.softmax(sc, axis=(-2, -1)).astype(vg.dtype)
    o = jnp.einsum('bhrqwk,bhrwkd->bhrqd', p, v_rows)
    return o.transpose(0, 2, 3, 1, 4).reshape(b, s, NA_WIDTH)

def _memory_cross_attention(xq, mem_n, w_kv):
    b, s, _ = xq.shape
    m = mem_n.shape[1]
    mk, mv = jnp.split(mem_n @ w_kv, 2, axis=-1)
    q = xq.reshape(b, s, XA_HEADS, XA_HEAD_DIM)
    k = mk.reshape(b, m, XA_HEADS, XA_HEAD_DIM)
    v = mv.reshape(b, m, XA_HEADS, XA_HEAD_DIM)
    sc = jnp.einsum('bshd,bmhd->bhsm', q, k).astype(jnp.float32) * (XA_HEAD_DIM ** -0.5)
    p = jax.nn.softmax(sc, axis=-1).astype(v.dtype)
    return jnp.einsum('bhsm,bmhd->bshd', p, v).reshape(b, s, XA_WIDTH)

def _hierarchical_moe(h, w_rg, b_rg, w_re, b_re, w_gate, w_up, w_down):
    b, s, d = h.shape
    t = h.reshape(b * s, d)
    g_n, e_n = MOE_GROUPS, MOE_EXPERTS_PER_GROUP
    grp_p = jax.nn.softmax((t @ w_rg + b_rg).astype(jnp.float32), axis=-1)
    grp_w, grp_idx = lax.top_k(grp_p, 1)
    exp_logits = (t @ w_re + b_re).astype(jnp.float32).reshape(-1, g_n, e_n)
    in_grp = jnp.take_along_axis(exp_logits, grp_idx[:, :, None], axis=1)[:, 0]
    top_w, top_idx = lax.top_k(jax.nn.softmax(in_grp, axis=-1), MOE_TOP_K)
    top_w = top_w / jnp.sum(top_w, axis=-1, keepdims=True) * grp_w
    exp_w = jnp.sum(jax.nn.one_hot(top_idx, e_n, dtype=jnp.float32) * top_w[..., None], axis=1)
    combine = (jax.nn.one_hot(grp_idx[:, 0], g_n, dtype=jnp.float32)[:, :, None] * exp_w[:, None, :]).astype(t.dtype)
    out = jnp.zeros_like(t)
    for g in range(g_n):
        a = jnp.einsum('td,edf->tef', t, w_gate[g])
        u = jnp.einsum('td,edf->tef', t, w_up[g])
        hid = jax.nn.silu(a) * u * combine[:, g, :, None]
        out = out + jnp.einsum('tef,efd->td', hid, w_down[g])
    return out.reshape(b, s, d)

def second_inputs(seed: int = 0) -> dict:
    key = jax.random.key(seed)
    ks = jax.random.split(key, 24)
    f32 = jnp.float32
    d = D_MODEL
    n_l = DEPTH_2
    g_n, e_n, f_n = MOE_GROUPS, MOE_EXPERTS_PER_GROUP, MOE_D_FF

    def nrm(k, shape, fan_in):
        return jax.random.normal(k, shape, f32) * (fan_in ** -0.5)

    def gain(k, shape):
        return 1.0 + 0.02 * jax.random.normal(k, shape, f32)

    base_gamma = 1.0 - 2.0 ** (-5.0 - jnp.arange(RET_HEADS, dtype=f32))
    base_logit = jnp.log(base_gamma) - jnp.log1p(-base_gamma)
    return {
        'x': jax.random.normal(ks[0], (BATCH, SEQ, d), f32),
        'mem': jax.random.normal(ks[1], (BATCH, MEM_LEN, d), f32),
        'g_mix': gain(ks[2], (n_l, d)),
        'w_in': nrm(ks[3], (n_l, d, IN_WIDTH), d),
        'ret_decay_fwd': base_logit[None] + 0.05 * jax.random.normal(ks[4], (n_l, RET_HEADS), f32),
        'ret_decay_bwd': base_logit[None] + 0.05 * jax.random.normal(ks[5], (n_l, RET_HEADS), f32),
        'ret_norm_gain': gain(ks[6], (n_l, RET_V_WIDTH)),
        'w_ret_o': nrm(ks[7], (n_l, RET_V_WIDTH, d), RET_V_WIDTH),
        'na_rpb': 0.1 * jax.random.normal(ks[8], (n_l, NA_HEADS, 2 * NA_ROWS - 1, 2 * NA_COLS - 1), f32),
        'w_na_o': nrm(ks[9], (n_l, NA_WIDTH, d), NA_WIDTH),
        'g_mem': gain(ks[10], (n_l, d)),
        'w_mem_kv': nrm(ks[11], (n_l, d, 2 * XA_WIDTH), d),
        'w_xa_o': nrm(ks[12], (n_l, XA_WIDTH, d), XA_WIDTH),
        'w_out': nrm(ks[13], (n_l, d, d), d),
        'g_ffn': gain(ks[14], (n_l, d)),
        'w_router_group': nrm(ks[15], (n_l, d, g_n), d),
        'b_router_group': 0.01 * jax.random.normal(ks[16], (n_l, g_n), f32),
        'w_router_expert': nrm(ks[17], (n_l, d, g_n * e_n), d),
        'b_router_expert': 0.01 * jax.random.normal(ks[18], (n_l, g_n * e_n), f32),
        'w_exp_gate': nrm(ks[19], (n_l, g_n, e_n, d, f_n), d),
        'w_exp_up': nrm(ks[20], (n_l, g_n, e_n, d, f_n), d),
        'w_exp_down': nrm(ks[21], (n_l, g_n, e_n, f_n, d), f_n),
        'g_final': gain(ks[22], (d,)),
    }

def second_block(x, mem, g_mix, w_in, ret_decay_fwd, ret_decay_bwd, ret_norm_gain, w_ret_o, na_rpb, w_na_o, g_mem, w_mem_kv, w_xa_o, w_out, g_ffn, w_router_group, b_router_group, w_router_expert, b_router_expert, w_exp_gate, w_exp_up, w_exp_down, g_final):
    split_points = [int(p) for p in np.cumsum(np.array(IN_SPLITS))[:-1]]
    for l in range(DEPTH_2):
        h = _rmsnorm(x, g_mix[l])
        rq, rk, rv, rg, nq, nk, nv, xq, gate_logits = jnp.split(h @ w_in[l], split_points, axis=-1)
        y_ret = _retention_branch(rq, rk, rv, rg, ret_decay_fwd[l], ret_decay_bwd[l], ret_norm_gain[l], w_ret_o[l])
        y_na = _neighbourhood_attention(nq, nk, nv, na_rpb[l]) @ w_na_o[l]
        y_xa = _memory_cross_attention(xq, _rmsnorm(mem, g_mem[l]), w_mem_kv[l]) @ w_xa_o[l]
        g_ret, g_na, g_xa = jnp.split(jax.nn.sigmoid(gate_logits), N_BRANCHES, axis=-1)
        x = x + (g_ret * y_ret + g_na * y_na + g_xa * y_xa) @ w_out[l]
        x = x + _hierarchical_moe(_rmsnorm(x, g_ffn[l]), w_router_group[l], b_router_group[l], w_router_expert[l], b_router_expert[l], w_exp_gate[l], w_exp_up[l], w_exp_down[l])
    return _rmsnorm(x, g_final)


def setup_inputs(seed=0):
    out = dict(first_inputs(seed))
    for name, value in second_inputs(seed + 1).items():
        if name != "x":
            out[name + "_2"] = value
    return out


def reference(
    x, mem, w_in_a, w_out_a, sg_ln_g, sg_ln_b, sg_w, sg_b, w_in_b, w_out_b, w_k_shared,
    w_v_shared, w_mem_k, w_mem_v, ln1_g, ln1_b, ln2_g, ln2_b, w_router, b_router, w_gate, w_up,
    w_down, mem_2, g_mix_2, w_in_2, ret_decay_fwd_2, ret_decay_bwd_2, ret_norm_gain_2,
    w_ret_o_2, na_rpb_2, w_na_o_2, g_mem_2, w_mem_kv_2, w_xa_o_2, w_out_2, g_ffn_2,
    w_router_group_2, b_router_group_2, w_router_expert_2, b_router_expert_2, w_exp_gate_2,
    w_exp_up_2, w_exp_down_2, g_final_2,
):
    x = first_block(
        x, mem, w_in_a, w_out_a, sg_ln_g, sg_ln_b, sg_w, sg_b, w_in_b, w_out_b, w_k_shared,
        w_v_shared, w_mem_k, w_mem_v, ln1_g, ln1_b, ln2_g, ln2_b, w_router, b_router, w_gate,
        w_up, w_down,
    )
    return second_block(
        x, mem_2, g_mix_2, w_in_2, ret_decay_fwd_2, ret_decay_bwd_2, ret_norm_gain_2, w_ret_o_2,
        na_rpb_2, w_na_o_2, g_mem_2, w_mem_kv_2, w_xa_o_2, w_out_2, g_ffn_2, w_router_group_2,
        b_router_group_2, w_router_expert_2, b_router_expert_2, w_exp_gate_2, w_exp_up_2,
        w_exp_down_2, g_final_2,
    )


_drawn_inputs = setup_inputs


def setup_inputs(seed=0):
    import zlib

    import numpy as np

    out = dict(_drawn_inputs(seed))
    spreads = {}
    factors = {'sg_ln_g': 8.0,
     'sg_ln_b': 2.734,
     'ret_norm_gain_2': 37.502,
     'na_rpb_2': 21.359,
     'g_mem_2': 8.0,
     'b_router_expert_2': 64.0,
     'g_final_2': 8.733,
     'g_ffn_2': 6.824,
     'b_router_group_2': 7.82}
    for name, (base, spread) in spreads.items():
        noise = np.random.default_rng([zlib.crc32(name.encode()), seed]).standard_normal(out[name].shape)
        drawn = base * np.exp(spread * noise) if base else spread * noise
        out[name] = jnp.asarray(drawn.astype(out[name].dtype))
    for name, factor in factors.items():
        out[name] = (out[name] * factor).astype(out[name].dtype)
    return out
```

```python
import math

import numpy as np

import concourse.bass as bass
from concourse import mybir
from concourse.alu_op_type import AluOpType as ALU

F32 = mybir.dt.float32
I32 = mybir.dt.int32
ACT = mybir.ActivationFunctionType
AX = mybir.AxisListType

P = 128
T, D = 256, 1024
TC, DC = T // P, D // P
DEPTH = 2
ALPHA = (2 * DEPTH) ** 0.25
LN_EPS, GN_EPS, RMS_EPS = 1e-5, 1e-5, 1e-6
HD = 64
N_SG, SGW = 12, 768
MEMW, MEM_HEADS = 256, 4
DILS = (1, 4, 16)
STEPS = 128
DIL_HEADS = 4
N_EXP, N_GRP, PER_GRP = 16, 4, 4
RET_HEADS, RET_QK, RET_V = 4, 128, 256
NA_HEADS, NA_ROWS, NA_COLS, GRID_W = 8, 8, 16, 64
XA_HEADS = 4
BIG = 1e30

RING = 6
CHUNK = 4096
BANKS = 4

C_IDENT, C_FLIP, C_BEFORE, C_ONES, C_IOTA = 0, 128, 256, 384, 512
C_RANK, C_NAMASK, C_MHALF = 640, 672, 736
C_N = 744


def constants():
    c = np.zeros((P, C_N), np.float32)
    c[:, C_IDENT:C_IDENT + P] = np.eye(P)
    flip = np.zeros((P, P))
    for r in range(2):
        for x in range(GRID_W):
            flip[r * GRID_W + x, r * GRID_W + GRID_W - 1 - x] = 1
    c[:, C_FLIP:C_FLIP + P] = flip
    c[:, C_BEFORE:C_BEFORE + P] = np.triu(np.ones((P, P)), 1)
    c[:, C_ONES:C_ONES + P] = 1
    c[:, C_IOTA:C_IOTA + P] = np.arange(P)[None]
    c[:, C_RANK:C_RANK + 32] = np.tile(np.arange(3, -1, -1), 8)[None]
    col = GRID_W - 1 - np.arange(P) % GRID_W
    start = np.clip(col - NA_COLS // 2, 0, GRID_W - NA_COLS)
    off = np.arange(GRID_W)[None] - start[:, None]
    c[:, C_NAMASK:C_NAMASK + GRID_W] = np.where((off >= 0) & (off < NA_COLS), 0, -BIG)
    c[:, C_MHALF:C_MHALF + 8] = -0.5
    i = np.arange(T)[:, None]
    j = np.arange(T)[None]
    rel = np.stack([np.where((j <= i) & ((i - j) % d == 0) & ((i - j) // d <= STEPS), i - j, BIG) for d in DILS])
    dist = rel.reshape(3, TC, P, T).transpose(2, 0, 1, 3).reshape(P, 3 * TC * T)
    fwd = np.maximum(j - i, 0).reshape(TC, P, T).transpose(1, 0, 2).reshape(P, TC * T)
    bwd = np.maximum(i - j, 0).reshape(TC, P, T).transpose(1, 0, 2).reshape(P, TC * T)
    half = RET_QK // 2
    inv = np.float32(10000.0) ** (-np.arange(half, dtype=np.float32) / np.float32(half))
    ang = np.arange(T, dtype=np.float32)[:, None] * inv[None].astype(np.float32)
    rope = [f(ang).reshape(TC, P, half).transpose(1, 0, 2).reshape(P, TC * half) for f in (np.cos, np.sin)]
    return {
        "const": c,
        "dist": np.ascontiguousarray(dist.astype(np.float32)),
        "later": np.ascontiguousarray(np.concatenate([fwd, bwd] + rope, 1).astype(np.float32)),
    }


SLOPES = [float(np.float32(2.0) ** np.float32(-8.0 * k / 12)) for k in range(1, 13)]

W_N = 15616
L0 = dict(memN=0, cat=0, memT=2048, sgw=4096, swT=5632, bsN=7168, bsT=7296, u=7424, gv=8960, qmT=10496)
W_P, W_PT = 11008, 12544
L1 = dict(dist=8192, qT=1536, kT=3072, v=4608, qmT=6144, cat=6656)
W_TAB, W_MEM2 = 8192, 11264
W_P2, W_PT2, W_COMB = 11264, 11776, 12288
XA = dict(H=0, memT=2048, mkT=4096, mv=5120, qT=6144, o=7168, oT=0, gate=2048)
NA = dict(qT=4096, kT=5120, v=6144, o=7168, oT=0, gate=2048)
RET = dict(q=0, k=1024, qT=2048, kT=3072, v=4096, rg=6144, D=8192, sd=10240, tmp=11264, y=0, yT=4096, gate=2048)
W_AB, W_ROPE = 14336, 15360
MOE = dict(xeT=0, h=1024, hT=2048, silu=3072, y=4096, pick=5120, pickg=5376, pickT=5632, acc=5888)

NORM_ORDER = ["gv", "ln1_0", "ln2_0", "ln1_1", "ln2_1", "mix", "mem", "gn", "ffn", "final"]
NORM_AT = {name: 2 * (n + 1) for n, name in enumerate(NORM_ORDER)}


def build(nc, a, out):
    from contextlib import ExitStack
    with ExitStack() as ctx:
        def sb(name, shape, dt=F32):
            return ctx.enter_context(nc.sbuf_tensor(name, shape, dt))

        ring = sb("ring", [P, RING, CHUNK])
        x = sb("x", [P, TC, D])
        xT = sb("xT", [P, DC, T])
        mkv = sb("mkv", [P, DEPTH, 2, 512])
        prm = sb("prm", [P, 2, 2, D])
        con = sb("con", [P, C_N])
        work = sb("work", [P, W_N])
        wr = sb("wr", [P, DC, 16])
        wr2 = sb("wr2", [P, DC, 20])
        br = sb("br", [P, TC, 16])
        br2 = sb("br2", [P, TC, 20])
        dec = sb("dec", [P, 8])
        stats = sb("stats", [P, 8, 6])
        mv8 = sb("mv8", [P, 8, 2])
        var8 = sb("var8", [P, 8])
        rstd = sb("rstd", [P, 8])
        att_mx = sb("att_mx", [P, 64])
        att_nm = sb("att_nm", [P, 64])
        att_sum = sb("att_sum", [P, 64])
        att_rec = sb("att_rec", [P, 64])
        rt = sb("rt", [P, 16, 32])
        rsm = sb("rsm", [P, 16, 8])
        sel = sb("sel", [P, TC, N_EXP])
        gates = sb("gates", [P, TC, N_EXP])
        slot_main = sb("slot_main", [P, TC, N_EXP + 2])
        slot_more = sb("slot_more", [P, TC, N_EXP + 2])
        fullest = sb("fullest", [P, 1], I32)
        fullest_f = sb("fullest_f", [P, 1])
        lg = sb("lg", [P, 10, 8])

        psum = [ctx.enter_context(nc.psum_tensor(f"bank{i}", [P, 512], F32)) for i in range(8)]
        RB = {"v": psum[0:4], "a": psum[4:8]}

        sems = {}

        def S(name):
            if name not in sems:
                sems[name] = ctx.enter_context(nc.semaphore(name))
            return sems[name]

        def W(at, *shape):
            n = int(np.prod(shape))
            ap = work[:, at:at + n]
            if len(shape) == 1:
                return ap
            names = "abc"[:len(shape)]
            return ap.rearrange(f"p ({' '.join(names)}) -> p {' '.join(names)}", **dict(zip(names, shape)))

        ident = con[:, C_IDENT:C_IDENT + P]
        flip = con[:, C_FLIP:C_FLIP + P]
        before = con[:, C_BEFORE:C_BEFORE + P]
        ones = con[:, C_ONES:C_ONES + P]
        iota = con[:, C_IOTA:C_IOTA + P]
        rank0 = con[:, C_RANK:C_RANK + 32].rearrange("p (g e) -> p g e", e=4)
        namask = con[:, C_NAMASK:C_NAMASK + GRID_W]
        mhalf = con[:, C_MHALF:C_MHALF + 8]

        block = ctx.enter_context(nc.Block())

        def cols(w, c0, n):
            return w[:, c0:c0 + n].rearrange("(c p) n -> p c n", p=P)

        def rows(w, r0, n):
            return w[r0:r0 + n, :].rearrange("(c p) n -> p c n", p=P)

        w_in_a, w_out_a = a["w_in_a"][0], a["w_out_a"][0]
        w_in_b, w_out_b = a["w_in_b"][0], a["w_out_b"][0]
        w2 = a["w_in_2"][0]
        stream_0 = [[(0, cols(a["w_mem_k"][l], 0, 256)), (2048, cols(a["w_mem_v"][l], 0, 256))] for l in range(2)]
        stream_0 += [[(0, cols(w_in_a, SGW, 512))], [(0, cols(w_in_a, SGW + 512, 512))],
                     [(0, cols(w_in_a, 0, 512))], [(0, cols(w_in_a, 512, 256))],
                     [(0, cols(w_out_a, 0, 512))], [(0, cols(w_out_a, 512, 512))]]
        stream_1 = [[(0, cols(w_in_b, 0, 512))], [(0, cols(w_in_b, 512, 512))],
                    [(0, cols(a["w_k_shared"], 0, 512))], [(0, cols(a["w_v_shared"], 0, 512))],
                    [(0, cols(a["w_k_shared"], 512, 256)), (2048, cols(a["w_v_shared"], 512, 256))],
                    [(0, rows(w_out_b, 0, 512))]]
        O_RQ, O_RK, O_RV, O_RG, O_NQ, O_NK, O_NV, O_XQ, O_G = 0, 512, 1024, 2048, 3072, 3584, 4096, 4608, 5120
        stream_2 = [[(0, cols(a["w_mem_kv_2"][0], 0, 512))], [(0, cols(a["w_mem_kv_2"][0], 512, 512))],
                    [(0, cols(w2, O_XQ, 512))],
                    [(0, cols(w2, O_G + 2048, 512))], [(0, cols(w2, O_G + 2560, 512))],
                    [(0, rows(a["w_xa_o_2"][0], 0, 512))],
                    [(0, cols(w2, O_NQ, 512))], [(0, cols(w2, O_NK, 512))], [(0, cols(w2, O_NV, 512))],
                    [(0, cols(w2, O_G + 1024, 512))], [(0, cols(w2, O_G + 1536, 512))],
                    [(0, rows(a["w_na_o_2"][0], 0, 512))],
                    [(0, cols(w2, O_RQ, 512))], [(0, cols(w2, O_RK, 512))],
                    [(0, cols(w2, O_RV, 512))], [(0, cols(w2, O_RV + 512, 512))],
                    [(0, cols(w2, O_RG, 512))], [(0, cols(w2, O_RG + 512, 512))],
                    [(0, cols(w2, O_G, 512))], [(0, cols(w2, O_G + 512, 512))],
                    [(0, cols(a["w_ret_o_2"][0], 0, 512))], [(0, cols(a["w_ret_o_2"][0], 512, 512))],
                    [(0, cols(a["w_out_2"][0], 0, 512))], [(0, cols(a["w_out_2"][0], 512, 512))]]

        class Phase:
            def __init__(self, tag, wg, wu, wd, halves, n0, slots, more):
                self.tag, self.wg, self.wu, self.wd, self.halves = tag, wg, wu, wd, halves
                self.n0, self.slots, self.more = n0, slots, more
                self.iters = N_EXP if halves == 2 else N_EXP // 2
                self.units, self.chunks = 2 * self.iters, 6 * self.iters
                self.ub = self.b16 = self.b17 = self.b18 = self.landed_before = 0

            def after(self, others):
                self.ub = sum(o.units for o in others)
                self.b16, self.b17, self.b18 = ((N_EXP + k) * len(others) for k in range(3))
                self.landed_before = 16 * sum(o.iters for o in others)

            def sem(self, name):
                return S(("more_" if self.more else "moe_") + name)

            def skip(self, eng, names):
                totals = dict(gathered=2 * (N_EXP + 1), gate=self.units, up=self.units, scattered=4 * (N_EXP + 1), turned=self.units,
                              pick_turned=N_EXP, down=self.units, xe_a=N_EXP + 1, xe_v=N_EXP + 1, silu=self.units, hT=self.units,
                              pickT=N_EXP + 1, y_a=N_EXP + 1, y_v=N_EXP + 1, pick=2 * (N_EXP + 2), h=self.units, pickg=2 * N_EXP,
                              added=4 * (N_EXP + 1))
                for name in names.split():
                    eng.sem_inc(self.sem(name), totals[name])

        phases, extras = [], []
        n_at = 0
        starts = []
        for tag, stream, halves, suffix in (("0", stream_0, 2, ""), ("1", stream_1, 2, ""), ("2", stream_2, 1, "_2")):
            starts.append(n_at)
            n_at += len(stream)
            if halves == 2:
                wg, wu, wd = (a[k][int(tag)] for k in ("w_gate", "w_up", "w_down"))
            else:
                wg, wu, wd = (a[k][0].rearrange("g e r c -> (g e) r c") for k in ("w_exp_gate_2", "w_exp_up_2", "w_exp_down_2"))
            ph = Phase(tag, wg, wu, wd, halves, n_at, slot_main, False)
            ph.after(phases)
            phases.append(ph)
            more = Phase(tag, wg, wu, wd, halves, 0, slot_more, True)
            more.after(extras)
            extras.append(more)
            n_at += ph.chunks
        n_all = n_at

        landed, count = {}, [0] * RING

        def note(n, parts):
            count[n % RING] += 16 * parts
            landed[n] = count[n % RING]

        for s0, stream, ph in zip(starts, (stream_0, stream_1, stream_2), phases):
            for k, parts in enumerate(stream):
                note(s0 + k, len(parts))
            for k in range(ph.chunks):
                note(ph.n0 + k, 1)

        freed = {}

        @block.tensor
        def _(pe):
            taken = {"v": 0, "a": 0}
            emptied = {"v": [], "a": []}
            made = {}

            def bank(r, product=None, by=None):
                j = taken[r]
                taken[r] += 1
                if j >= BANKS:
                    pe.wait_ge(*emptied[r][j - BANKS])
                if by is None:
                    key = product + "_" + r
                    made[key] = made.get(key, 0) + 1
                    by = (S(key), made[key])
                emptied[r].append(by)
                return RB[r][j % BANKS]

            def full(r, ins):
                ins.then_inc(S(r + "_full"), 1)
                return (S(r + "_full"), taken[r])

            def wait_made(product):
                for r in "va":
                    if product + "_" + r in made:
                        pe.wait_ge(S(product + "_" + r), made[product + "_" + r])

            def chunk(n):
                pe.wait_ge(S(f"slot{n % RING}"), landed[n])
                return ring[:, n % RING, :]

            def turn(src, tiles, product):
                for j in range(tiles // 2):
                    r = "va"[j % 2]
                    b = bank(r, product)
                    for cc in range(2):
                        for t in range(TC):
                            ins = pe.transpose(b[:, cc * T + t * P:cc * T + (t + 1) * P],
                                               src[:, t, (2 * j + cc) * P:(2 * j + cc + 1) * P], ident)
                    full(r, ins)

            def gemm(b, cols_at, lhsT, rhs, k):
                for c in range(k):
                    ins = pe.matmul(b[:, cols_at[0]:cols_at[1]], lhsT=lhsT(c), rhs=rhs(c), start=(c == 0), stop=(c == k - 1))
                return ins

            def nat(w, act, k, n, r, product, pack=False):
                for t in range(TC):
                    if t == 0 or not pack:
                        b = bank(r, product)
                    at = (t * n, (t + 1) * n) if pack else (0, n)
                    ins = gemm(b, at, lambda c: act[:, c, t * P:(t + 1) * P], lambda c: w[:, c, :], k)
                    if not pack or t == TC - 1:
                        done = full(r, ins)
                return done

            def turned(w, act, k, tiles, r, product):
                for j in range(tiles // 2):
                    b = bank(r, product)
                    for cc in range(2):
                        f = (2 * j + cc) * P
                        ins = gemm(b, (cc * T, (cc + 1) * T), lambda c: w[:, c, f:f + P], lambda c: act[:, c, :], k)
                    done = full(r, ins)
                return done

            def as_cols(n, at=0, width=512):
                return chunk(n)[:, at:at + 8 * width].rearrange("p (c n) -> p c n", c=8)

            def as_rows(n):
                return chunk(n).rearrange("p (c n) -> p c n", c=4)

            att = {"i": 0, "sc": 0}

            def attention(q, keys, v, nk, dv, n_tasks, bias=None, tables=False):
                i0 = att["i"]
                att["i"] += n_tasks

                def scores(i):
                    h, t = divmod(i, TC)
                    ks = keys(h)
                    for first in range(0, len(ks), 2):
                        mine = ks[first:first + 2]
                        if tables:
                            att["sc"] += len(mine)
                            b = bank("v", by=(S("att_sc"), att["sc"]))
                        else:
                            b = bank("v", by=(S("att_p"), i0 + i + 1))
                        for g, kk in enumerate(mine):
                            o = b[:, g * T:(g + 1) * T]
                            if bias is not None:
                                pe.matmul(o, lhsT=flip, rhs=bias(h, t), start=True, stop=False)
                            ins = pe.matmul(o, lhsT=q(h, t, first + g), rhs=kk, start=(bias is None), stop=True)
                        full("v", ins)

                def turn_weights(i):
                    pe.wait_ge(S("att_p"), i0 + i + 1)
                    p = W(p_at, 2, nk * P)
                    for first in range(0, nk, 4):
                        m = min(4, nk - first)
                        b = bank("a", "att_pT")
                        for k in range(m):
                            ins = pe.transpose(b[:, k * P:(k + 1) * P], p[:, i % 2, (first + k) * P:(first + k + 1) * P], ident)
                        full("a", ins)
                    upto[i] = made["att_pT_a"]

                def values(i):
                    h = i // TC
                    pe.wait_ge(S("att_pT_a"), upto[i])
                    pT = W(pT_at, 2, nk * P)
                    b = bank("v", by=(S("att_o"), i0 + i + 1))
                    for k in range(nk):
                        ins = pe.matmul(b[:, 0:dv], lhsT=pT[:, i % 2, k * P:(k + 1) * P], rhs=v(h, k),
                                        start=(k == 0), stop=(k == nk - 1))
                    full("v", ins)

                upto = {}
                for i in range(n_tasks + 3):
                    if i < n_tasks:
                        scores(i)
                    if 2 <= i < n_tasks + 2:
                        turn_weights(i - 2)
                    if i >= 3:
                        values(i - 3)
                pe.wait_ge(S("att_o"), att["i"])

            def route(w, n, k):
                b = bank("v", by=(S("logits_read"), k))
                for t in range(TC):
                    ins = gemm(b, (t * n, (t + 1) * n), lambda c: xT[:, c, t * P:(t + 1) * P], lambda c: w[:, c, :], DC)
                full("v", ins)
                pe.wait_ge(S("chosen"), k)
                b = bank("v", by=(S("slots"), k))
                pe.matmul(b[:, 0:16], lhsT=before, rhs=sel[:, 0, :], start=True, stop=True)
                pe.matmul(b[:, 16:32], lhsT=ones, rhs=sel[:, 0, :], start=True, stop=False)
                pe.matmul(b[:, 16:32], lhsT=before, rhs=sel[:, 1, :], start=False, stop=True)
                pe.matmul(b[:, 32:48], lhsT=ones, rhs=sel[:, 0, :], start=True, stop=False)
                ins = pe.matmul(b[:, 32:48], lhsT=ones, rhs=sel[:, 1, :], start=False, stop=True)
                full("v", ins)

            def drain():
                for r in "va":
                    for by in emptied[r][-BANKS:]:
                        pe.wait_ge(*by)

            def experts(ph):
                sem, ub, b16, b17, b18 = ph.sem, ph.ub, ph.b16, ph.b17, ph.b18
                g_bank, u_bank = (psum[0], psum[2]), (psum[1], psum[3])
                y_bank, t_bank = (psum[4], psum[5]), (psum[6], psum[7])
                xeT, h, hT = W(MOE["xeT"], 8, P), W(MOE["h"], 2, 512), W(MOE["hT"], 2, 4, P)
                y, pick, pickg, pickT = W(MOE["y"], D), W(MOE["pick"], TC, P), W(MOE["pickg"], TC, P), W(MOE["pickT"], T)

                def gather(e):
                    pe.wait_ge(sem("pick"), e * 2 + (b18 + 1) * 2)
                    for half in range(2):
                        for c in range(4):
                            for t in range(TC):
                                ins = pe.matmul(t_bank[half][:, c * P:(c + 1) * P], lhsT=x[:, t, (4 * half + c) * P:(4 * half + c + 1) * P],
                                                rhs=pick[:, t, :], start=(t == 0), stop=(t == TC - 1))
                        ins.then_inc(sem("gathered"), 1)

                def scatter(e):
                    pe.wait_ge(sem("y_a"), e + (b17 + 1))
                    pe.wait_ge(sem("y_v"), e + (b17 + 1))
                    pe.wait_ge(sem("pickT"), e + (b17 + 1))
                    for t in range(TC):
                        for half in range(2):
                            if t == 1:
                                pe.wait_ge(sem("added"), e * 4 + (4 * b17 + half + 1))
                            pe.matmul(t_bank[half][:], lhsT=pickT[:, t * P:(t + 1) * P], rhs=y[:, half * 512:(half + 1) * 512],
                                      start=True, stop=True).then_inc(sem("scattered"), 1)

                def unit(it, k):
                    first, last = (k == 0, k == 1) if ph.halves == 2 else (True, True)
                    u = it * 2 + (k + ub)
                    e = it if ph.halves == 2 else it * 2 + k
                    for which, (bk, name) in enumerate(((g_bank, "gate"), (u_bank, "up"))):
                        n = ph.n0 + 3 * k + which
                        pe.wait_ge(land(ph, n), it * 16 + landed_first(ph, n))
                        w = ring[:, n % RING, :].rearrange("p (c n) -> p c n", c=8)
                        if which == 0 and first:
                            pe.wait_ge(sem("xe_a"), e + (b17 + 1))
                            pe.wait_ge(sem("xe_v"), e + (b17 + 1))
                        ins = gemm(bk[k], (0, 512), lambda c: xeT[:, c, :], lambda c: w[:, c, :], DC)
                        ins.then_inc(sem(name), 1)
                    if first:
                        scatter(e)
                    if last:
                        pe.wait_ge(sem("added"), e * 4 + (4 * b17 + 4))
                        gather(e + 1)
                        pe.wait_ge(sem("xe_a"), e + (b17 + 2))
                    else:
                        pe.wait_ge(sem("added"), e * 4 + (4 * b17 + 3))
                    pe.wait_ge(sem("h"), u + 1)
                    for f in range(4):
                        ins = pe.transpose(t_bank[0][:, f * P:(f + 1) * P], h[:, k, f * P:(f + 1) * P], ident)
                    ins.then_inc(sem("turned"), 1)
                    if last:
                        pe.wait_ge(sem("xe_v"), e + (b17 + 2))
                        pe.wait_ge(sem("pickg"), e * 2 + (2 * b16 + 2))
                        for t in range(TC):
                            ins = pe.transpose(t_bank[1][:, t * P:(t + 1) * P], pickg[:, t, :], ident)
                        ins.then_inc(sem("pick_turned"), 1)
                    n = ph.n0 + 3 * k + 2
                    pe.wait_ge(land(ph, n), it * 16 + landed_first(ph, n))
                    pe.wait_ge(sem("hT"), u + 1)
                    w = ring[:, n % RING, :].rearrange("p (c n) -> p c n", c=4)
                    for half in range(2):
                        for c in range(4):
                            ins = pe.matmul(y_bank[half][:], lhsT=hT[:, k, c, :], rhs=w[:, c, half * 512:(half + 1) * 512],
                                            start=(first and c == 0), stop=(last and c == 3))
                    ins.then_inc(sem("down"), 1)

                gather(0)
                with pe.Fori(0, ph.iters) as it:
                    unit(it, 0)
                    unit(it, 1)
                scatter(N_EXP)

            def land(ph, n):
                return S(("more_slot" if ph.more else "slot") + str(n % RING))

            def landed_first(ph, n):
                return 16 + ph.landed_before if ph.more else landed[n]

            def expert_layer(k):
                drain()
                experts(phases[k])
                for m in range(phases[k].chunks - 6, phases[k].chunks):
                    n = phases[k].n0 + m
                    name = ("gate", "up", "down")[m % 3]
                    freed[n] = (phases[k].sem(name), phases[k].ub + m // 3 + 1)
                fills = pe.value_load(fullest[0:1, 0:1])
                with pe.If(fills > P):
                    experts(extras[k])
                with pe.Else():
                    extras[k].skip(pe, "gathered gate up scattered turned pick_turned down")
                pe.wait_ge(S("experts_done"), k + 1)

            n = 0
            pe.wait_ge(S("con_in"), 16)
            pe.wait_ge(S("mem_in"), 16)
            turn(W(L0["memN"], TC, D), DC, "memT")
            wait_made("memT")
            memT = W(L0["memT"], DC, T)
            for l in range(DEPTH):
                turned(as_cols(n, 0, 256), memT, DC, 2, "v", "mkv")
                freed[n] = nat(as_cols(n, 2048, 256), memT, DC, 256, "a", "mkv", pack=True)
                n += 1
            pe.wait_ge(S("x_in"), 16)
            turn(x, DC, "xT")
            wait_made("xT")
            freed[n] = nat(as_cols(n), xT, DC, 512, "a", "gv"); n += 1
            w = as_cols(n)
            nat(w[:, :, 0:256], xT, DC, 256, "a", "gv", pack=True)
            freed[n] = turned(w[:, :, 256:512], xT, DC, 2, "v", "qm"); n += 1
            freed[n] = nat(as_cols(n), xT, DC, 512, "a", "u"); n += 1
            freed[n] = nat(as_cols(n, 0, 256), xT, DC, 256, "a", "u", pack=True); n += 1
            pe.wait_ge(S("sg_causal"), 1)
            sgw = W(L0["sgw"], N_SG, P)
            for j in range(3):
                b = bank("v", "sw")
                for g in range(4):
                    ins = pe.transpose(b[:, g * P:(g + 1) * P], sgw[:, 4 * j + g, :], ident)
                full("v", ins)
            b = bank("v", "sw")
            full("v", pe.transpose(b[:, 0:N_SG], W(L0["bsN"], P)[0:N_SG, :], ident[0:N_SG, 0:N_SG]))
            qmT = W(L0["qmT"], 2, T)
            wait_made("qm")
            wait_made("mkv")

            def mem_attention(qT, l):
                mk = mkv[:, l, 0, :].rearrange("p (c m) -> p c m", c=2)
                mv = mkv[:, l, 1, :].rearrange("p (c n) -> p c n", c=2)

                def hp(h):
                    return slice(HD * (h % 2), HD * (h % 2) + HD)
                attention(lambda h, t, g: qT[hp(h), h // 2, t * P:(t + 1) * P], lambda h: [mk[hp(h), h // 2, :]],
                          lambda h, k: mv[:, k, h * HD:(h + 1) * HD], 2, HD, 2 * MEM_HEADS)

            p_at, pT_at = W_P, W_PT
            mem_attention(qmT, 0)
            gv, swT = W(L0["gv"], TC, SGW), W(L0["swT"], N_SG, P)
            wait_made("sw")
            pe.wait_ge(S("norm"), NORM_AT["gv"])
            for j in range(3):
                b = bank("v", by=(S("mix"), 4 * (j + 1)))
                for g in range(4):
                    hh = 4 * j + g
                    ins = pe.matmul(b[:, g * P:(g + 1) * P].rearrange("p (c d) -> p c d", c=2), lhsT=swT[:, hh, :],
                                    rhs=gv[:, :, hh * HD:(hh + 1) * HD], start=True, stop=True)
                full("v", ins)
            pe.wait_ge(S("mix"), N_SG)
            turn(W(L0["cat"], TC, D), DC, "xT")
            wait_made("xT")
            for half in range(2):
                freed[n] = nat(as_cols(n), xT, DC, 512, "v", "z"); n += 1
            pe.wait_ge(S("norm"), NORM_AT["ln1_0"])
            turn(x, DC, "xT")
            wait_made("xT")
            pe.wait_ge(S("wr_in"), 16)
            route(wr, 16, 1)
            expert_layer(0)
            n += phases[0].chunks

            pe.wait_ge(S("norm"), NORM_AT["ln2_0"])
            turn(x, DC, "xT")
            wait_made("xT")
            freed[n] = turned(as_cols(n), xT, DC, 4, "v", "qkv"); n += 1
            w = as_cols(n)
            turned(w[:, :, 0:256], xT, DC, 2, "a", "qkv")
            freed[n] = turned(w[:, :, 256:512], xT, DC, 2, "a", "qkv"); n += 1
            freed[n] = turned(as_cols(n), xT, DC, 4, "v", "qkv"); n += 1
            freed[n] = nat(as_cols(n), xT, DC, 512, "a", "qkv"); n += 1
            turned(as_cols(n, 0, 256), xT, DC, 2, "v", "qkv")
            freed[n] = nat(as_cols(n, 2048, 256), xT, DC, 256, "a", "qkv", pack=True); n += 1
            wait_made("qkv")
            qT, kT, v = W(L1["qT"], 6, T), W(L1["kT"], 6, T), W(L1["v"], TC, SGW)

            def pair(g, h):
                hh = g * DIL_HEADS + h
                return slice(HD * (hh % 2), HD * (hh % 2) + HD), hh // 2

            def dil_q(h, t, g):
                r, tile = pair(g, h)
                return qT[r, tile, t * P:(t + 1) * P]

            def dil_k(h):
                return [kT[pair(g, h)[0], pair(g, h)[1], :] for g in range(3)]

            def dil_v(h, k):
                hh = (k // 2) * DIL_HEADS + h
                return v[:, k % 2, hh * HD:(hh + 1) * HD]

            attention(dil_q, dil_k, dil_v, 6, HD, 2 * DIL_HEADS, tables=True)
            mem_attention(W(L1["qmT"], 2, T), 1)
            turn(W(L1["cat"], TC, 512), 4, "xT")
            wait_made("xT")
            w = as_rows(n)
            for half in range(2):
                freed[n] = nat(w[:, :, half * 512:(half + 1) * 512], xT, 4, 512, "v", "z")
            n += 1
            pe.wait_ge(S("norm"), NORM_AT["ln1_1"])
            turn(x, DC, "xT")
            wait_made("xT")
            route(wr, 16, 2)
            expert_layer(1)
            n += phases[1].chunks

            p_at, pT_at = W_P2, W_PT2
            pe.wait_ge(S("norm"), NORM_AT["mix"])
            turn(W(XA["H"], TC, D), DC, "xT")
            pe.wait_ge(S("norm"), NORM_AT["mem"])
            turn(W(W_MEM2, TC, D), DC, "memT")
            wait_made("memT")
            memT = W(XA["memT"], DC, T)
            freed[n] = turned(as_cols(n), memT, DC, 4, "v", "xa"); n += 1
            freed[n] = nat(as_cols(n), memT, DC, 512, "a", "xa"); n += 1
            wait_made("xT")
            freed[n] = turned(as_cols(n), xT, DC, 4, "v", "xa"); n += 1
            wait_made("xa")
            qT, kT, v = W(XA["qT"], 4, T), W(XA["mkT"], 4, T), W(XA["mv"], TC, 512)
            attention(lambda h, t, g: qT[:, h, t * P:(t + 1) * P], lambda h: [kT[:, h, :]],
                      lambda h, k: v[:, k, h * P:(h + 1) * P], 2, P, 2 * XA_HEADS)

            def join(o, oT, k):
                nonlocal n
                for half in range(2):
                    freed[n] = nat(as_cols(n), xT, DC, 512, "a", "gate"); n += 1
                turn(o, k, "oT")
                wait_made("oT")
                wait_made("gate")
                if k == 4:
                    w = as_rows(n)
                    for half in range(2):
                        freed[n] = nat(w[:, :, half * 512:(half + 1) * 512], oT, 4, 512, "v", "joined")
                    n += 1
                else:
                    for half in range(2):
                        freed[n] = nat(as_cols(n), oT, DC, 512, "v", "joined"); n += 1

            join(W(XA["o"], TC, 512), W(XA["oT"], 4, T), 4)

            freed[n] = turned(as_cols(n), xT, DC, 4, "v", "na"); n += 1
            freed[n] = turned(as_cols(n), xT, DC, 4, "a", "na"); n += 1
            freed[n] = nat(as_cols(n), xT, DC, 512, "a", "na"); n += 1
            wait_made("na")
            pe.wait_ge(S("na_table"), 1)
            qT, kT, v = W(NA["qT"], 4, T), W(NA["kT"], 4, T), W(NA["v"], TC, 512)
            table = W(W_TAB, NA_HEADS, 6 * GRID_W)

            def na_rows(h):
                return slice(HD * (h % 2), HD * (h % 2) + HD)

            attention(lambda h, t, g: qT[na_rows(h), h // 2, t * P:(t + 1) * P], lambda h: [kT[na_rows(h), h // 2, :]],
                      lambda h, k: v[:, k, h * HD:(h + 1) * HD], 2, HD, 2 * NA_HEADS,
                      bias=lambda h, t: table[:, h, (1 - t) * P:(1 - t) * P + T])
            join(W(NA["o"], TC, 512), W(NA["oT"], 4, T), 4)

            wait_made("joined")
            freed[n] = nat(as_cols(n), xT, DC, 512, "v", "rope"); n += 1
            freed[n] = nat(as_cols(n), xT, DC, 512, "v", "rope"); n += 1
            for half in range(2):
                freed[n] = nat(as_cols(n), xT, DC, 512, "a", "rv"); n += 1
            for half in range(2):
                freed[n] = nat(as_cols(n), xT, DC, 512, "a", "rg"); n += 1
            wait_made("rope")
            turn(W(RET["q"], TC, 512), 4, "rqk")
            turn(W(RET["k"], TC, 512), 4, "rqk")
            wait_made("rqk")
            wait_made("rv")
            qT, kT, v, sd = W(RET["qT"], 4, T), W(RET["kT"], 4, T), W(RET["v"], TC, D), W(RET["sd"], 2, TC, T)
            for h in range(RET_HEADS + 1):
                if h < RET_HEADS:
                    b = bank("v", by=(S("ret_sd"), h + 1))
                    for j in range(TC):
                        ins = pe.matmul(b[:, j * T:(j + 1) * T], lhsT=kT[:, h, j * P:(j + 1) * P], rhs=qT[:, h, :], start=True, stop=True)
                    full("v", ins)
                if h >= 1:
                    g = h - 1
                    pe.wait_ge(S("ret_sd"), g + 1)
                    b = bank("a", "ret_y")
                    for i in range(TC):
                        for j in range(TC):
                            ins = pe.matmul(b[:, i * RET_V:(i + 1) * RET_V], lhsT=sd[:, g % 2, j, i * P:(i + 1) * P],
                                            rhs=v[:, j, g * RET_V:(g + 1) * RET_V], start=(j == 0), stop=(j == TC - 1))
                    full("a", ins)
            pe.wait_ge(S("norm"), NORM_AT["gn"])
            join(W(RET["y"], TC, D), W(RET["yT"], DC, T), DC)
            wait_made("joined")
            turn(W(W_COMB, TC, D), DC, "xT")
            wait_made("xT")
            for half in range(2):
                freed[n] = nat(as_cols(n), xT, DC, 512, "v", "z"); n += 1
            pe.wait_ge(S("norm"), NORM_AT["ffn"])
            turn(x, DC, "xT")
            wait_made("xT")
            pe.wait_ge(S("wr2_in"), 32)
            route(wr2, 20, 3)
            expert_layer(2)

        @block.scalar
        def _(act):
            took = [0]
            counted = {}

            def bank():
                took[0] += 1
                act.wait_ge(S("a_full"), took[0])
                return RB["a"][(took[0] - 1) % BANKS]

            def step(ins):
                counted["act_step"] = counted.get("act_step", 0) + 1
                ins.then_inc(S("act_step"), 1)
                act.wait_ge(S("act_step"), counted["act_step"])

            def empty(dst, product, func=ACT.Copy, n=512, scale=None):
                b = bank()
                src = b[:, 0:n]
                if len(dst.shape) == 3:
                    src = src.rearrange("p (a b) -> p a b", a=dst.shape[1])
                kw = {} if scale is None else {"scale": scale}
                act.activation(dst, src, func, **kw).then_inc(S(product + "_a"), 1)

            def turn(dst, tiles, product):
                for j in range(1, tiles // 2, 2):
                    empty(dst[:, 2 * j:2 * j + 2, :], product)

            def nat(dst, n, product, func=ACT.Copy, pack=False):
                if pack:
                    empty(dst, product, func)
                else:
                    for t in range(TC):
                        empty(dst[:, t, :], product, func, n)

            att = {"i": 0}

            def attention(nk, n_tasks, scale, p_at, pT_at, tables=False):
                i0 = att["i"]
                att["i"] += n_tasks
                p, pT = W(p_at, 2, nk * P), W(pT_at, 2, nk * P)
                for i in range(n_tasks + 2):
                    if i >= 2:
                        for first in range(0, nk, 4):
                            m = min(4, nk - first) * P
                            empty(pT[:, i % 2, first * P:first * P + m], "att_pT", n=m)
                    if i < n_tasks:
                        act.wait_ge(S("att_nm"), i0 + i + 1)
                        I = i0 + i
                        if tables:
                            src = p[:, i % 2, :]
                        else:
                            src = score_bank(i0 + i)
                        act.activation(p[:, i % 2, :], src, ACT.Exp, bias=att_nm[:, I:I + 1], scale=scale,
                                       accum_out=att_sum[:, I:I + 1]).then_inc(S("att_p"), 1)

            def score_bank(i):
                return RB["v"][score_at[i] % BANKS][:, 0:T]

            score_at = {}
            v_jobs = 0

            def plan(before, i0, n_tasks):
                j = before
                for i in range(n_tasks + 3):
                    if i < n_tasks:
                        score_at[i0 + i] = j
                        j += 1
                    if i >= 3:
                        j += 1
                return j

            def routed(k):
                act.wait_ge(S("logit_max"), k)
                e, lgt, nm, sm = rt[:, 1, :], rt[:, 0, :], rsm[:, 0, :], rsm[:, 1, :]
                if k < 3:
                    for c in range(TC):
                        act.activation(e[:, c * 16:(c + 1) * 16], lgt[:, c * 16:(c + 1) * 16], ACT.Exp, bias=nm[:, c:c + 1],
                                       accum_out=sm[:, c:c + 1]).then_inc(S("logit_exp"), 1)
                else:
                    act.activation(rt[:, 3, :], rt[:, 2, :], ACT.Exp).then_inc(S("logit_exp"), 1)
                    act.activation(rsm[:, 3, :], rsm[:, 2, :], ACT.Exp).then_inc(S("logit_exp"), 1)

            def experts(ph):
                sem, ub, b16, b17 = ph.sem, ph.ub, ph.b16, ph.b17
                xeT, hT, silu = W(MOE["xeT"], 2, 512), W(MOE["hT"], 2, 512), W(MOE["silu"], 2, 512)
                y, pickT = W(MOE["y"], 2, 512), W(MOE["pickT"], T)

                def gathered(e):
                    act.wait_ge(sem("gathered"), e * 2 + (2 * b17 + 1))
                    act.copy(xeT[:, 0, :], psum[6][:]).then_inc(sem("xe_a"), 1)

                gathered(0)
                with act.Fori(0, ph.iters) as it:
                    for k in range(2):
                        last = k == 1 or ph.halves == 1
                        u = it * 2 + (k + ub)
                        e = it if ph.halves == 2 else it * 2 + k
                        act.wait_ge(sem("gate"), u + 1)
                        act.activation(silu[:, k, :], psum[2 * k][:], ACT.Silu).then_inc(sem("silu"), 1)
                        if last:
                            gathered(e + 1)
                        act.wait_ge(sem("turned"), u + 1)
                        act.copy(hT[:, k, :], psum[6][:]).then_inc(sem("hT"), 1)
                        if last:
                            act.wait_ge(sem("pick_turned"), e + (b16 + 1))
                            act.copy(pickT, psum[7][:, 0:T]).then_inc(sem("pickT"), 1)
                            act.wait_ge(sem("down"), u + 1)
                            act.copy(y[:, 0, :], psum[4][:]).then_inc(sem("y_a"), 1)

            def expert_layer(k):
                experts(phases[k])
                act.wait_ge(S("slots"), k + 1)
                fills = act.value_load(fullest[0:1, 0:1])
                with act.If(fills > P):
                    experts(extras[k])
                with act.Else():
                    extras[k].skip(act, "xe_a silu hT pickT y_a")

            turn(W(L0["memT"], DC, T), DC, "memT"); v_jobs += 2
            for l in range(DEPTH):
                nat(mkv[:, l, 1, :], 256, "mkv", pack=True); v_jobs += 1
            turn(xT, DC, "xT"); v_jobs += 2
            gv, u = W(L0["gv"], TC, SGW), W(L0["u"], TC, SGW)
            nat(gv[:, :, 0:512], 512, "gv", ACT.Gelu)
            nat(gv[:, :, 512:SGW], 256, "gv", ACT.Gelu, pack=True); v_jobs += 1
            nat(u[:, :, 0:512], 512, "u", ACT.Gelu)
            nat(u[:, :, 512:SGW], 256, "u", ACT.Gelu, pack=True)
            v_jobs += 4
            v_jobs = plan(v_jobs, att["i"], 8)
            attention(2, 8, HD ** -0.5, W_P, W_PT)
            v_jobs += 3
            turn(xT, DC, "xT"); v_jobs += 2
            v_jobs += 4
            turn(xT, DC, "xT"); v_jobs += 2
            routed(1); v_jobs += 2
            expert_layer(0)
            turn(xT, DC, "xT"); v_jobs += 2
            qT, kT, v = W(L1["qT"], 6, T), W(L1["kT"], 6, T), W(L1["v"], TC, SGW)
            v_jobs += 5
            empty(qT[:, 4:6, :], "qkv")
            empty(W(L1["qmT"], 2, T), "qkv")
            nat(v[:, :, 0:512], 512, "qkv")
            nat(v[:, :, 512:SGW], 256, "qkv", pack=True)
            attention(6, 8, HD ** -0.5, W_P, W_PT, tables=True)
            v_jobs += 3 * 8
            v_jobs = plan(v_jobs, att["i"], 8)
            attention(2, 8, HD ** -0.5, W_P, W_PT)
            turn(xT, 4, "xT"); v_jobs += 1
            v_jobs += 4
            turn(xT, DC, "xT"); v_jobs += 2
            routed(2); v_jobs += 2
            expert_layer(1)
            squares = [0]

            def square(src, junk, n_norm):
                for c in range(TC):
                    act.activation(junk[:, c, :], src[:, c, :], ACT.Square, accum_out=var8[:, c:c + 1]).then_inc(S("var"), 1)

            act.wait_ge(S("norm"), NORM_AT["ln2_1"])
            square(x, W(XA["H"], TC, D), "mix")
            act.wait_ge(S("mem2_in"), 16)
            act.wait_ge(S("rstd"), 1 + NORM_ORDER.index("mix"))
            square(W(W_MEM2, TC, D), W(XA["memT"], TC, D), "mem")
            turn(xT, DC, "xT"); v_jobs += 2
            turn(W(XA["memT"], DC, T), DC, "memT"); v_jobs += 2
            nat(W(XA["mv"], TC, 512), 512, "xa"); v_jobs += 4
            v_jobs = plan(v_jobs, att["i"], 8)
            attention(2, 8, P ** -0.5, W_P2, W_PT2)

            def join(oT, k, gate_at):
                nonlocal v_jobs
                gate = W(gate_at, TC, D)
                for half in range(2):
                    nat(gate[:, :, half * 512:(half + 1) * 512], 512, "gate", ACT.Sigmoid)
                turn(oT, k, "oT")
                v_jobs += k // 4 + 4

            join(W(XA["oT"], 4, T), 4, XA["gate"])
            v_jobs += 2
            kT, v = W(NA["kT"], 4, T), W(NA["v"], TC, 512)
            empty(kT[:, 0:2, :], "na")
            empty(kT[:, 2:4, :], "na")
            nat(v, 512, "na")
            v_jobs = plan(v_jobs, att["i"], 16)
            attention(2, 16, 1.0, W_P2, W_PT2)
            join(W(NA["oT"], 4, T), 4, NA["gate"])
            act.wait_ge(S("dec_in"), 32)
            act.activation(lg[:, 0, :], dec[:], ACT.Abs).then_inc(S("dec_abs"), 1)
            act.wait_ge(S("dec_abs"), 1)
            act.activation(lg[:, 1, :], lg[:, 0, :], ACT.Exp, scale=-1.0).then_inc(S("dec_exp"), 1)
            Dm = W(RET["D"], RET_HEADS, TC * T)
            act.wait_ge(S("ret_e"), RET_HEADS)
            for h in range(RET_HEADS):
                act.activation(Dm[:, h, :], Dm[:, h, :], ACT.Exp).then_inc(S("ret_d"), 1)
            v, rg, y = W(RET["v"], TC, D), W(RET["rg"], TC, D), W(RET["y"], TC, D)
            for half in range(2):
                nat(v[:, :, half * 512:(half + 1) * 512], 512, "rv")
            for half in range(2):
                nat(rg[:, :, half * 512:(half + 1) * 512], 512, "rg", ACT.Silu)
            turn(W(RET["qT"], 4, T), 4, "rqk")
            turn(W(RET["kT"], 4, T), 4, "rqk")
            for h in range(RET_HEADS):
                empty(y[:, :, h * RET_V:(h + 1) * RET_V], "ret_y")
            join(W(RET["yT"], DC, T), DC, RET["gate"])
            turn(xT, DC, "xT")
            act.wait_ge(S("z_v"), 12)
            square(x, W(RET["y"], TC, D), "ffn")
            turn(xT, DC, "xT")
            routed(3)
            expert_layer(2)
            act.wait_ge(S("resid"), 2)
            square(x, W(MOE["xeT"], TC, D), "final")

        @block.vector
        def _(dve):
            took = [0]
            counted = {"dve_step": 0, "rstd": 0, "att": 0, "sc": 0}

            def bank():
                took[0] += 1
                dve.wait_ge(S("v_full"), took[0])
                return RB["v"][(took[0] - 1) % BANKS]

            def step(ins):
                counted["dve_step"] += 1
                ins.then_inc(S("dve_step"), 1)
                dve.wait_ge(S("dve_step"), counted["dve_step"])

            def steps(todo):
                for ins in todo:
                    counted["dve_step"] += 1
                    ins.then_inc(S("dve_step"), 1)
                dve.wait_ge(S("dve_step"), counted["dve_step"])

            def empty(dst, product, n=512):
                b = bank()
                src = b[:, 0:n]
                if len(dst.shape) == 3:
                    src = src.rearrange("p (a b) -> p a b", a=dst.shape[1])
                dve.tensor_copy(dst, src).then_inc(S(product + "_v"), 1)

            def turn(dst, tiles, product):
                for j in range(0, tiles // 2, 2):
                    empty(dst[:, 2 * j:2 * j + 2, :], product)

            def turned(dst, tiles, product):
                for j in range(tiles // 2):
                    empty(dst[:, 2 * j:2 * j + 2, :], product)

            def wait_rstd():
                counted["rstd"] += 1
                dve.wait_ge(S("rstd"), counted["rstd"])

            def moments(srcs, cuts):
                for n, src in enumerate(srcs):
                    w = src.shape[-1] // cuts
                    steps(dve.bn_stats(stats[:, c, :], src[:, c * w:(c + 1) * w]) for c in range(cuts))
                    dve.bn_aggr(mv8[:, n, :], stats[:, 0:cuts, :]).then_inc(S("moments"), 1)
                    counted["moments"] = counted.get("moments", 0) + 1
                    dve.wait_ge(S("moments"), counted["moments"])
                dve.tensor_copy(var8[:, 0:len(srcs)], mv8[:, 0:len(srcs), 1]).then_inc(S("var"), 2)

            def layer_norm(buf, width, cuts, slot):
                moments([buf[:, c, :] for c in range(TC)], cuts)
                wait_rstd()
                g, b = prm[:, slot, 0, 0:width], prm[:, slot, 1, 0:width]
                steps(dve.scalar_tensor_tensor(out=buf[:, c, :], in0=buf[:, c, :], scalar=mv8[:, c, 0:1], in1=g,
                                               op0=ALU.subtract, op1=ALU.mult) for c in range(TC))
                for c in range(TC):
                    dve.scalar_tensor_tensor(out=buf[:, c, :], in0=buf[:, c, :], scalar=rstd[:, c:c + 1], in1=b,
                                             op0=ALU.mult, op1=ALU.add).then_inc(S("norm"), 1)

            def rms_norm(src, dst, g):
                wait_rstd()
                for c in range(TC):
                    dve.scalar_tensor_tensor(out=dst[:, c, :], in0=src[:, c, :], scalar=rstd[:, c:c + 1], in1=g,
                                             op0=ALU.mult, op1=ALU.mult).then_inc(S("norm"), 1)

            def attention(nk, dv, n_tasks, scale, outs, p_at=None, t_slopes=None, dist=None):
                i0 = counted["att"]
                counted["att"] += n_tasks

                def peak(i):
                    I = i0 + i
                    if t_slopes is None:
                        src = bank()[:, 0:nk * P]
                    else:
                        h, t = divmod(i, TC)
                        sc = W(p_at, 2, nk * P)[:, i % 2, :]
                        if i >= 2:
                            dve.wait_ge(S("att_pT_a"), counted["pT0"] + 2 * (i - 1))
                        for g in range(3):
                            if g != 1:
                                b = bank()
                            dve.scalar_tensor_tensor(out=sc[:, g * T:(g + 1) * T], in0=dist[:, g, t, :], scalar=t_slopes(g, h),
                                                     in1=b[:, (g % 2) * T:(g % 2 + 1) * T],
                                                     op0=ALU.mult, op1=ALU.add).then_inc(S("att_sc"), 1)
                        counted["sc"] += 3
                        dve.wait_ge(S("att_sc"), counted["sc"])
                        src = sc
                    step(dve.tensor_reduce(att_mx[:, I:I + 1], src, AX.X, ALU.max))
                    dve.tensor_scalar(att_nm[:, I:I + 1], att_mx[:, I:I + 1], -scale, None, ALU.mult).then_inc(S("att_nm"), 1)

                def result(i):
                    I = i0 + i
                    b = bank()
                    step(dve.reciprocal(att_rec[:, I:I + 1], att_sum[:, I:I + 1]))
                    dve.tensor_scalar(outs(i // TC, i % TC), b[:, 0:dv], att_rec[:, I:I + 1], None, ALU.mult).then_inc(S("att_o"), 1)

                for i in range(n_tasks + 3):
                    if i < n_tasks:
                        peak(i)
                    if i >= 3:
                        result(i - 3)

            def residual(half, t):
                b = bank()
                xs = x[:, t, half * 512:(half + 1) * 512]
                return b, xs

            def rank4(v, r):
                step(dve.tensor_copy(r, rank0[:, 0:r.shape[1], :]))
                ge = rt[:, 15, 0:4 * r.shape[1]].rearrange("p (g e) -> p g e", e=4)
                for s in range(1, 4):
                    step(dve.tensor_tensor(ge[:, :, 0:4 - s], v[:, :, 0:4 - s], v[:, :, s:4], ALU.is_ge))
                    step(dve.tensor_tensor(r[:, :, s:4], r[:, :, s:4], ge[:, :, 0:4 - s], ALU.add))
                    step(dve.tensor_tensor(r[:, :, 0:4 - s], r[:, :, 0:4 - s], ge[:, :, 0:4 - s], ALU.subtract))

            def groups(ap, n=8):
                return ap.rearrange("p (g e) -> p g e", e=4)

            def spread(ap):
                return ap.unsqueeze(2).to_broadcast([P, 8, 4])

            selg = sel[:].rearrange("p c (g e) -> p (c g) e", e=4)

            def slots(k):
                b = bank()
                s2 = sel[:].rearrange("p c e -> p (c e)")
                step(dve.scalar_tensor_tensor(out=rt[:, 12, :], in0=b[:, 0:32], scalar=1.0, in1=s2, op0=ALU.add, op1=ALU.mult))
                r = rt[:, 12, :].rearrange("p (c e) -> p c e", c=TC)
                step(dve.tensor_reduce(fullest_f[:], b[:, 32:48], AX.X, ALU.max))
                steps([dve.tensor_scalar(slot_main[:, :, 0:N_EXP], r, -1.0, None, ALU.add),
                       dve.tensor_scalar(slot_more[:, :, 0:N_EXP], r, -1.0 - P, None, ALU.add),
                       dve.memset(slot_main[:, :, N_EXP:], -1.0), dve.memset(slot_more[:, :, N_EXP:], -1.0)])
                dve.tensor_copy(fullest[:], fullest_f[:]).then_inc(S("slots"), 1)
                dve.wait_ge(S("slots"), k)

            def route_1(k):
                b = bank()
                lgt, e, nm, sm = rt[:, 0, :], rt[:, 1, :], rsm[:, 0, 0:2], rsm[:, 1, 0:2]
                dve.tensor_copy(lgt, b[:, 0:32]).then_inc(S("logits_read"), 1)
                dve.wait_ge(S("logits_read"), k)
                step(dve.tensor_reduce(rsm[:, 2, 0:2], lgt.rearrange("p (c e) -> p c e", c=TC), AX.X, ALU.max))
                dve.tensor_scalar(nm, rsm[:, 2, 0:2], -1.0, None, ALU.mult).then_inc(S("logit_max"), 1)
                dve.wait_ge(S("logit_exp"), 2 * k)
                step(dve.reciprocal(rsm[:, 3, 0:2], sm))
                probs, score, r, two = rt[:, 2, :], rt[:, 3, :], groups(rt[:, 4, :]), rt[:, 5, :]
                steps(dve.tensor_scalar(probs[:, c * 16:(c + 1) * 16], e[:, c * 16:(c + 1) * 16], rsm[:, 3, c:c + 1], None, ALU.mult)
                      for c in range(TC))
                if k == 1:
                    dve.wait_ge(S("br_in"), 32)
                step(dve.tensor_tensor(score, probs, br[:].rearrange("p c e -> p (c e)"), ALU.add))
                rank4(groups(score), r)
                step(dve.tensor_scalar(groups(two), r, 2.0, None, ALU.is_lt))
                step(dve.tensor_tensor(rt[:, 6, :], score, two, ALU.mult))
                step(dve.tensor_reduce(rsm[:, 4, :], groups(rt[:, 6, :]), AX.X, ALU.add))
                rg = rsm[:, 5, :].rearrange("p (c g) -> p c g", c=TC)
                rank4(rsm[:, 4, :].rearrange("p (c g) -> p c g", c=TC), rg)
                step(dve.tensor_scalar(rsm[:, 6, :], rsm[:, 5, :], 1.0, None, ALU.is_lt))
                dve.tensor_tensor(selg, groups(two), spread(rsm[:, 6, :]), ALU.mult).then_inc(S("chosen"), 1)
                dve.wait_ge(S("chosen"), k)
                s2 = sel[:].rearrange("p c e -> p (c e)")
                step(dve.tensor_tensor(rt[:, 7, :], probs, s2, ALU.mult))
                step(dve.tensor_reduce(rsm[:, 7, 0:2], rt[:, 7, :].rearrange("p (c e) -> p c e", c=TC), AX.X, ALU.add))
                step(dve.reciprocal(rsm[:, 8, 0:2], rsm[:, 7, 0:2]))
                steps(dve.tensor_scalar(gates[:, c, :], rt[:, 7, c * 16:(c + 1) * 16], rsm[:, 8, c:c + 1], None, ALU.mult) for c in range(TC))
                slots(k)

            def route_2(k):
                b = bank()
                full = rt[:, 8:10, 0:20]
                dve.wait_ge(S("br2_in"), 64)
                dve.tensor_tensor(full, b[:, 0:40].rearrange("p (c e) -> p c e", c=TC), br2[:], ALU.add).then_inc(S("logits_read"), 1)
                dve.wait_ge(S("logits_read"), k)
                lgrp, lexp = full[:, :, 0:4], full[:, :, 4:20].rearrange("p c (g e) -> p c g e", e=4)
                steps([dve.tensor_reduce(rsm[:, 0, 0:2], lgrp, AX.X, ALU.max),
                       dve.tensor_reduce(rsm[:, 1, :].rearrange("p (c g) -> p c g", c=TC), lexp, AX.X, ALU.max)])
                todo = []
                for c in range(TC):
                    todo.append(dve.tensor_scalar(rsm[:, 2, 4 * c:4 * c + 4], lgrp[:, c, :], rsm[:, 0, c:c + 1], None, ALU.subtract))
                    todo.append(dve.tensor_tensor(groups(rt[:, 2, 16 * c:16 * c + 16]), lexp[:, c],
                                                  rsm[:, 1, 4 * c:4 * c + 4].unsqueeze(2).to_broadcast([P, 4, 4]), ALU.subtract))
                steps(todo)
                dve.sem_inc(S("logit_max"), 1)
                dve.wait_ge(S("logit_exp"), 6)
                e, r, two = rt[:, 3, :], groups(rt[:, 4, :]), rt[:, 5, :]
                rank4(groups(e), r)
                step(dve.tensor_scalar(groups(two), r, 2.0, None, ALU.is_lt))
                rg = rsm[:, 5, :].rearrange("p (c g) -> p c g", c=TC)
                rank4(rsm[:, 2, :].rearrange("p (c g) -> p c g", c=TC), rg)
                step(dve.tensor_scalar(rsm[:, 6, :], rsm[:, 5, :], 1.0, None, ALU.is_lt))
                dve.tensor_tensor(selg, groups(two), spread(rsm[:, 6, :]), ALU.mult).then_inc(S("chosen"), 1)
                dve.wait_ge(S("chosen"), k)
                s2 = sel[:].rearrange("p c e -> p (c e)")
                step(dve.tensor_tensor(rt[:, 7, :], e, s2, ALU.mult))
                steps([dve.tensor_reduce(rsm[:, 7, 0:2], rt[:, 7, :].rearrange("p (c e) -> p c e", c=TC), AX.X, ALU.add),
                       dve.tensor_reduce(rsm[:, 8, 0:2], rsm[:, 3, :].rearrange("p (c g) -> p c g", c=TC), AX.X, ALU.add)])
                steps([dve.reciprocal(rsm[:, 9, 0:2], rsm[:, 7, 0:2]), dve.reciprocal(rsm[:, 10, 0:2], rsm[:, 8, 0:2])])
                steps(dve.tensor_scalar(gates[:, c, :], rt[:, 7, c * 16:(c + 1) * 16], rsm[:, 9, c:c + 1], rsm[:, 10, c:c + 1],
                                        ALU.mult, ALU.mult) for c in range(TC))
                slots(k)

            def experts(ph):
                sem, ub, b17 = ph.sem, ph.ub, ph.b17
                xeT, h, silu = W(MOE["xeT"], 2, 512), W(MOE["h"], 2, 512), W(MOE["silu"], 2, 512)
                y, pick, pickg, pickT = W(MOE["y"], 2, 512), W(MOE["pick"], TC, P), W(MOE["pickg"], TC, P), W(MOE["pickT"], T)
                acc = W(MOE["acc"], TC, 2, 512)

                def mark(e):
                    for c in range(TC):
                        dve.tensor_scalar(pick[:, c, :], iota, ph.slots[:, c, bass.ds(e, 1)], None, ALU.is_equal).then_inc(sem("pick"), 1)

                def mark_gated(e):
                    for c in range(TC):
                        dve.tensor_scalar(pickg[:, c, :], iota, ph.slots[:, c, bass.ds(e, 1)], gates[:, c, bass.ds(e, 1)],
                                          ALU.is_equal, ALU.mult).then_inc(sem("pickg"), 1)

                def gathered(e):
                    dve.wait_ge(sem("gathered"), e * 2 + (2 * b17 + 2))
                    dve.tensor_copy(xeT[:, 1, :], psum[7][:]).then_inc(sem("xe_v"), 1)

                def add(e):
                    for t in range(TC):
                        for half in range(2):
                            dve.wait_ge(sem("scattered"), e * 4 + (4 * b17 + 2 * t + half + 1))
                            dve.tensor_tensor(acc[:, t, half, :], acc[:, t, half, :], psum[6 + half][:], ALU.add).then_inc(sem("added"), 1)

                for c in range(TC):
                    dve.tensor_scalar(pick[:, c, :], iota, ph.slots[:, c, 0:1], None, ALU.is_equal).then_inc(sem("pick"), 1)
                dve.memset(y[:, 0, :], 0.0).then_inc(sem("y_a"), 1)
                dve.memset(y[:, 1, :], 0.0).then_inc(sem("y_v"), 1)
                dve.memset(pickT, 0.0).then_inc(sem("pickT"), 1)
                if not ph.more:
                    step(dve.memset(W(MOE["acc"], TC * D), 0.0))
                gathered(0)
                for c in range(TC):
                    dve.tensor_scalar(pick[:, c, :], iota, ph.slots[:, c, 1:2], None, ALU.is_equal).then_inc(sem("pick"), 1)
                with dve.Fori(0, ph.iters) as it:
                    for k in range(2):
                        first, last = (k == 0, k == 1) if ph.halves == 2 else (True, True)
                        u = it * 2 + (k + ub)
                        e = it if ph.halves == 2 else it * 2 + k
                        dve.wait_ge(sem("up"), u + 1)
                        dve.wait_ge(sem("silu"), u + 1)
                        dve.tensor_tensor(h[:, k, :], silu[:, k, :], psum[2 * k + 1][:], ALU.mult).then_inc(sem("h"), 1)
                        if first:
                            add(e)
                            mark_gated(e)
                        if last:
                            gathered(e + 1)
                            mark(e + 2)
                            dve.wait_ge(sem("down"), u + 1)
                            dve.tensor_copy(y[:, 1, :], psum[5][:]).then_inc(sem("y_v"), 1)
                add(N_EXP)
                dve.wait_ge(sem("added"), 4 * (b17 + N_EXP + 1))

            def expert_layer(k):
                experts(phases[k])
                fills = dve.value_load(fullest[0:1, 0:1])
                with dve.If(fills > P):
                    experts(extras[k])
                with dve.Else():
                    extras[k].skip(dve, "pick xe_v h pickg added y_v")
                dve.sem_inc(S("experts_done"), 1)
                acc = W(MOE["acc"], TC, D)
                for c in range(TC):
                    if k < 2:
                        ins = dve.scalar_tensor_tensor(out=x[:, c, :], in0=x[:, c, :], scalar=ALPHA, in1=acc[:, c, :], op0=ALU.mult, op1=ALU.add)
                        step(ins)

            turn(W(L0["memT"], DC, T), DC, "memT")
            for l in range(DEPTH):
                empty(mkv[:, l, 0, :], "mkv")
            turn(xT, DC, "xT")
            empty(W(L0["qmT"], 2 * T), "qm")
            swT, bsT = W(L0["swT"], N_SG * P), W(L0["bsT"], 16)
            for j in range(3):
                empty(swT[:, j * 512:(j + 1) * 512], "sw")
            empty(bsT[:, 0:N_SG], "sw", N_SG)
            dve.wait_ge(S("gv_a"), 3)
            dve.wait_ge(S("prm0_in"), 32)
            gv = W(L0["gv"], TC, SGW)
            cat = W(L0["cat"], TC, D)
            attention(2, HD, 8, HD ** -0.5, lambda h, t: cat[:, t, SGW + h * HD:SGW + (h + 1) * HD])
            layer_norm(gv, SGW, 2, 0)
            dve.wait_ge(S("u_a"), 3)
            dve.wait_ge(S("sw_v"), 4)
            u = W(L0["u"], TC, SGW)
            for j in range(3):
                b = bank()
                for g in range(4):
                    hh = 4 * j + g
                    c = slice(hh * HD, (hh + 1) * HD)
                    dve.scalar_tensor_tensor(out=cat[:, :, c], in0=b[:, g * P:(g + 1) * P].rearrange("p (c d) -> p c d", c=2),
                                             scalar=bsT[:, hh:hh + 1], in1=u[:, :, c], op0=ALU.add, op1=ALU.mult).then_inc(S("mix"), 1)
            turn(xT, DC, "xT")
            zs = [0]

            def add_residual(scale):
                for half in range(2):
                    for t in range(TC):
                        b, xs = residual(half, t)
                        if scale == 1.0:
                            ins = dve.tensor_tensor(xs, xs, b[:], ALU.add)
                        else:
                            ins = dve.scalar_tensor_tensor(out=xs, in0=xs, scalar=scale, in1=b[:], op0=ALU.mult, op1=ALU.add)
                        ins.then_inc(S("z_v"), 1)
                        zs[0] += 1
                dve.wait_ge(S("z_v"), zs[0])

            add_residual(ALPHA)
            dve.wait_ge(S("prm1_in"), 32)
            layer_norm(x, D, 2, 1)
            turn(xT, DC, "xT")
            route_1(1)
            expert_layer(0)
            dve.wait_ge(S("prm0_in"), 64)
            layer_norm(x, D, 2, 0)
            turn(xT, DC, "xT")
            qT, kT = W(L1["qT"], 6, T), W(L1["kT"], 6, T)
            turned(qT[:, 0:4, :], 4, "qkv")
            turned(kT[:, 0:4, :], 4, "qkv")
            empty(kT[:, 4:6, :], "qkv")
            cat = W(L1["cat"], TC, 512)
            dve.wait_ge(S("dist_in"), 16)
            counted["pT0"] = counted["att"]
            attention(6, HD, 8, HD ** -0.5, lambda h, t: cat[:, t, h * HD:(h + 1) * HD], p_at=W_P,
                      t_slopes=lambda g, h: -SLOPES[g * DIL_HEADS + h] * HD ** 0.5, dist=W(L1["dist"], 3, TC * T)
                      .rearrange("p g (t k) -> p g t k", t=TC))
            attention(2, HD, 8, HD ** -0.5, lambda h, t: cat[:, t, 256 + h * HD:256 + (h + 1) * HD])
            turn(xT, 4, "xT")
            add_residual(ALPHA)
            dve.wait_ge(S("prm1_in"), 64)
            layer_norm(x, D, 2, 1)
            turn(xT, DC, "xT")
            route_1(2)
            expert_layer(1)
            dve.wait_ge(S("prm0_in"), 96)
            layer_norm(x, D, 2, 0)
            dve.wait_ge(S("prm1_in"), 96)
            rms_norm(x, W(XA["H"], TC, D), prm[:, 1, 0, :])
            mem2 = W(W_MEM2, TC, D)
            rms_norm(mem2, mem2, prm[:, 1, 1, :])
            turn(xT, DC, "xT")
            turn(W(XA["memT"], DC, T), DC, "memT")
            turned(W(XA["mkT"], 4, T), 4, "xa")
            turned(W(XA["qT"], 4, T), 4, "xa")
            o = W(XA["o"], TC, 512)
            attention(2, P, 8, P ** -0.5, lambda h, t: o[:, t, h * P:(h + 1) * P])
            comb = W(W_COMB, TC, D)
            joins = [0]

            def join(oT, k, gate_at):
                turn(oT, k, "oT")
                gate = W(gate_at, TC, D)
                joins[0] += 1
                dve.wait_ge(S("gate_a"), 4 * joins[0])
                for half in range(2):
                    for t in range(TC):
                        cs = slice(half * 512, (half + 1) * 512)
                        b = bank()
                        if joins[0] == 1:
                            dve.tensor_tensor(comb[:, t, cs], b[:], gate[:, t, cs], ALU.mult).then_inc(S("joined_v"), 1)
                        else:
                            step(dve.tensor_tensor(gate[:, t, cs], b[:], gate[:, t, cs], ALU.mult))
                            dve.tensor_tensor(comb[:, t, cs], comb[:, t, cs], gate[:, t, cs], ALU.add).then_inc(S("joined_v"), 1)
                dve.wait_ge(S("joined_v"), 4 * joins[0])

            join(W(XA["oT"], 4, T), 4, XA["gate"])
            qT = W(NA["qT"], 4, T)
            for j in range(2):
                b = bank()
                dve.tensor_scalar(qT[:, 2 * j:2 * j + 2, :], b[:].rearrange("p (a b) -> p a b", a=2), HD ** -0.5, None, ALU.mult).then_inc(S("na_v"), 1)
            o = W(NA["o"], TC, 512)
            attention(2, HD, 16, 1.0, lambda h, t: o[:, t, h * HD:(h + 1) * HD])
            join(W(NA["oT"], 4, T), 4, NA["gate"])
            dve.wait_ge(S("dec_exp"), 1)
            z, s, s2, acc, ls = lg[:, 1, :], lg[:, 2, :], lg[:, 3, :], lg[:, 4, :], lg[:, 5, :]
            step(dve.tensor_scalar(s2, z, 2.0, None, ALU.add))
            step(dve.reciprocal(acc, s2))
            step(dve.tensor_tensor(s, z, acc, ALU.mult))
            step(dve.tensor_tensor(s2, s, s, ALU.mult))
            step(dve.tensor_scalar(acc, s2, 1.0 / 17, 1.0 / 15, ALU.mult, ALU.add))
            for k in range(13, 0, -2):
                step(dve.tensor_tensor(acc, acc, s2, ALU.mult))
                step(dve.tensor_scalar(acc, acc, 1.0 / k, None, ALU.add))
            step(dve.tensor_tensor(acc, acc, s, ALU.mult))
            step(dve.tensor_scalar(ls, dec[:], 0.0, None, ALU.min))
            step(dve.scalar_tensor_tensor(out=ls, in0=acc, scalar=-2.0, in1=ls, op0=ALU.mult, op1=ALU.add))
            Dm = W(RET["D"], RET_HEADS, TC * T)
            AB = W(W_AB, 2, TC * T)
            dve.wait_ge(S("later_in"), 16)
            steps(dve.tensor_scalar(Dm[:, h, :], AB[:, 0, :], ls[:, h:h + 1], None, ALU.mult) for h in range(RET_HEADS))
            for h in range(RET_HEADS):
                dve.scalar_tensor_tensor(out=Dm[:, h, :], in0=AB[:, 1, :], scalar=ls[:, 4 + h:5 + h], in1=Dm[:, h, :],
                                         op0=ALU.mult, op1=ALU.add).then_inc(S("ret_e"), 1)
            rope = W(W_ROPE, 2, TC * 64)
            tmp = W(RET["tmp"], 4, RET_HEADS * 64)
            for name in "qk":
                dst = W(RET[name], TC, 512)
                for t in range(TC):
                    b = bank()[:].rearrange("p (h s d) -> p h s d", h=4, s=2)
                    cos, sin = (rope[:, f, t * 64:(t + 1) * 64].unsqueeze(1).to_broadcast([P, 4, 64]) for f in range(2))
                    ts = [tmp[:, n, :].rearrange("p (h d) -> p h d", h=4) for n in range(4)]
                    steps([dve.tensor_tensor(ts[0], b[:, :, 0, :], cos, ALU.mult), dve.tensor_tensor(ts[1], b[:, :, 1, :], sin, ALU.mult),
                           dve.tensor_tensor(ts[2], b[:, :, 0, :], sin, ALU.mult), dve.tensor_tensor(ts[3], b[:, :, 1, :], cos, ALU.mult)])
                    dd = dst[:, t, :].rearrange("p (h s d) -> p h s d", h=4, s=2)
                    step(dve.tensor_tensor(dd[:, :, 0, :], ts[0], ts[1], ALU.subtract))
                    dve.tensor_tensor(dd[:, :, 1, :], ts[2], ts[3], ALU.add).then_inc(S("rope_v"), 1)
                    counted["rope"] = counted.get("rope", 0) + 1
                    dve.wait_ge(S("rope_v"), counted["rope"])
            turn(W(RET["qT"], 4, T), 4, "rqk")
            turn(W(RET["kT"], 4, T), 4, "rqk")
            sd = W(RET["sd"], 2, TC * T)
            dve.wait_ge(S("ret_d"), RET_HEADS)
            for h in range(RET_HEADS):
                b = bank()
                if h >= 2:
                    dve.wait_ge(S("ret_y_a"), h - 1)
                dve.scalar_tensor_tensor(out=sd[:, h % 2, :], in0=b[:], scalar=RET_QK ** -0.5, in1=Dm[:, h, :],
                                         op0=ALU.mult, op1=ALU.mult).then_inc(S("ret_sd"), 1)
            y, rg = W(RET["y"], TC, D), W(RET["rg"], TC, D)
            dve.wait_ge(S("ret_y_a"), RET_HEADS)
            cells = [(t, h) for t in range(TC) for h in range(RET_HEADS)]
            moments([y[:, t, h * RET_V:(h + 1) * RET_V] for t, h in cells], 1)
            wait_rstd()
            steps(dve.tensor_scalar(y[:, t, h * RET_V:(h + 1) * RET_V], y[:, t, h * RET_V:(h + 1) * RET_V], mv8[:, n, 0:1], rstd[:, n:n + 1],
                                    ALU.subtract, ALU.mult) for n, (t, h) in enumerate(cells))
            dve.wait_ge(S("prm0_in"), 128)
            steps(dve.tensor_tensor(y[:, t, :], y[:, t, :], prm[:, 0, 0, :], ALU.mult) for t in range(TC))
            dve.wait_ge(S("rg_a"), 4)
            for t in range(TC):
                dve.tensor_tensor(y[:, t, :], y[:, t, :], rg[:, t, :], ALU.mult).then_inc(S("norm"), 1)
            join(W(RET["yT"], DC, T), DC, RET["gate"])
            turn(xT, DC, "xT")
            add_residual(1.0)
            keep = comb
            steps(dve.tensor_copy(keep[:, c, :], x[:, c, :]) for c in range(TC))
            rms_norm(keep, x, prm[:, 0, 1, :])
            turn(xT, DC, "xT")
            route_2(3)
            expert_layer(2)
            acc = W(MOE["acc"], TC, D)
            for c in range(TC):
                dve.tensor_tensor(x[:, c, :], keep[:, c, :], acc[:, c, :], ALU.add).then_inc(S("resid"), 1)
            dve.wait_ge(S("prm1_in"), 112)
            dve.wait_ge(S("resid"), 2)
            rms_norm(x, x, prm[:, 1, 0, :])

        @block.gpsimd
        def _(pool):
            def bc(v):
                return v.partition_broadcast(P)

            pool.dma_start(wr[:], a["w_router"].rearrange("(c p) n -> p c n", p=P)).then_inc(S("wr_in"), 16)
            pool.dma_start(W(L0["bsN"], P)[0:N_SG, :], a["sg_b"][0]).then_inc(S("sgb_in"), 16)
            loads = [
                [(0, SGW, a["sg_ln_g"][0]), (1, SGW, a["sg_ln_b"][0])],
                [(0, D, a["ln1_g"][0]), (1, D, a["ln1_b"][0])],
                [(0, D, a["ln2_g"][0]), (1, D, a["ln2_b"][0])],
                [(0, D, a["ln1_g"][1]), (1, D, a["ln1_b"][1])],
                [(0, D, a["ln2_g"][1]), (1, D, a["ln2_b"][1])],
                [(0, D, a["g_mix_2"][0]), (1, D, a["g_mem_2"][0])],
                [(0, D, a["ret_norm_gain_2"][0]), (1, D, a["g_ffn_2"][0])],
                [(0, D, a["g_final_2"])],
            ]
            last_use = ["gv", "ln1_0", "ln2_0", "ln1_1", "ln2_1", "mem"]

            def load(k):
                if k >= 2:
                    pool.wait_ge(S("norm"), NORM_AT[last_use[k - 2]])
                for which, width, src in loads[k]:
                    pool.dma_start(prm[:, k % 2, which, 0:width], bc(src)).then_inc(S(f"prm{k % 2}_in"), 16)

            load(0)
            load(1)
            for c in range(TC):
                pool.dma_start(br[:, c, :], bc(a["b_router"])).then_inc(S("br_in"), 16)
                pool.dma_start(br2[:, c, 0:4], bc(a["b_router_group_2"][0])).then_inc(S("br2_in"), 16)
                pool.dma_start(br2[:, c, 4:20], bc(a["b_router_expert_2"][0])).then_inc(S("br2_in"), 16)
            pool.dma_start(wr2[:, :, 0:4], a["w_router_group_2"][0].rearrange("(c p) n -> p c n", p=P)).then_inc(S("wr2_in"), 16)
            pool.dma_start(wr2[:, :, 4:20], a["w_router_expert_2"][0].rearrange("(c p) n -> p c n", p=P)).then_inc(S("wr2_in"), 16)
            pool.dma_start(dec[:, 0:4], bc(a["ret_decay_fwd_2"][0])).then_inc(S("dec_in"), 16)
            pool.dma_start(dec[:, 4:8], bc(a["ret_decay_bwd_2"][0])).then_inc(S("dec_in"), 16)
            pool.dma_start(W(W_AB, W_N - W_AB), a["later"]).then_inc(S("later_in"), 16)
            pool.wait_ge(S("sgw_in"), 16)
            pool.wait_ge(S("sgb_in"), 16)
            sgw = W(L0["sgw"], N_SG, P)
            pool.affine_select(out=sgw, in_=sgw, compare_op=ALU.is_ge, fill=0.0, base=0,
                               pattern=[[0, N_SG], [-1, P]], channel_multiplier=1).then_inc(S("sg_causal"), 1)
            pool.wait_ge(S("con_in"), 16)
            done = [0]

            def root(n, eps, scale=None):
                done[0] += 1
                pool.wait_ge(S("var"), 2 * done[0])
                if scale is None:
                    pool.tensor_scalar(var8[:, 0:n], var8[:, 0:n], eps, None, ALU.add).then_inc(S("var_eps"), 1)
                else:
                    pool.tensor_scalar(var8[:, 0:n], var8[:, 0:n], scale, eps, ALU.mult, ALU.add).then_inc(S("var_eps"), 1)
                pool.wait_ge(S("var_eps"), done[0])
                if done[0] >= 2:
                    pool.wait_ge(S("norm"), 2 * (done[0] - 1))
                pool.tensor_tensor(rstd[:, 0:n], var8[:, 0:n], mhalf[:, 0:n], ALU.pow).then_inc(S("rstd"), 1)

            root(2, LN_EPS)
            root(2, LN_EPS)
            pool.wait_ge(S("norm"), NORM_AT["ln1_0"])
            pool.dma_start(W(L1["dist"], 3 * TC * T), a["dist"]).then_inc(S("dist_in"), 16)
            load(2)
            load(3)
            root(2, LN_EPS)
            root(2, LN_EPS)
            pool.wait_ge(S("norm"), NORM_AT["ln1_1"])
            pool.dma_start(W(W_MEM2, TC, D), a["mem_2"][0].rearrange("(c p) n -> p c n", p=P)).then_inc(S("mem2_in"), 16)
            rpb = a["na_rpb_2"]
            n_r, n_c = 2 * NA_ROWS - 1, 2 * NA_COLS - 1
            table = W(W_TAB, NA_HEADS, 6, GRID_W)
            for r in range(2):
                for h in range(NA_HEADS):
                    src = bass.AP(rpb.tensor, (h * n_r + 5 - r) * n_c + NA_COLS - 1 - (GRID_W - 1),
                                  [[1, GRID_W], [n_c, 6], [1, GRID_W]])
                    pool.dma_start(table[r * GRID_W:(r + 1) * GRID_W, h], src).then_inc(S("rpb_in"), 16)
            load(4)
            load(5)
            pool.wait_ge(S("rpb_in"), 16 * 2 * NA_HEADS)
            flat = W(W_TAB, NA_HEADS * 6, GRID_W)
            pool.tensor_tensor(flat, flat, namask.unsqueeze(1).to_broadcast([P, NA_HEADS * 6, GRID_W]), ALU.add).then_inc(S("na_table"), 1)
            root(2, LN_EPS)
            root(2, RMS_EPS, 1.0 / D)
            load(6)
            root(2, RMS_EPS, 1.0 / D)
            load(7)
            root(8, GN_EPS)
            root(2, RMS_EPS, 1.0 / D)
            root(2, RMS_EPS, 1.0 / D)

        @block.sync
        def _(sp):
            sp.dma_start(con[:], a["const"]).then_inc(S("con_in"), 16)
            sp.dma_start(W(L0["memN"], TC, D), a["mem"][0].rearrange("(c p) n -> p c n", p=P)).then_inc(S("mem_in"), 16)

            def fill(n, parts):
                if n >= RING:
                    sp.wait_ge(*freed[n - RING])
                for at, src in parts:
                    dst = ring[:, n % RING, at:at + src.shape[1] * src.shape[2]].rearrange("p (c n) -> p c n", c=src.shape[1])
                    sp.dma_start(dst, src).then_inc(S(f"slot{n % RING}"), 16)

            def expert_chunk(ph, it, k, which):
                e, half = (it, k) if ph.halves == 2 else (it * 2 + k, 0)
                w = (ph.wg, ph.wu, ph.wd)[which]
                if which < 2:
                    return w[e, :, half * 512:(half + 1) * 512].rearrange("(c p) n -> p c n", p=P)
                return w[e, half * 512:(half + 1) * 512, :].rearrange("(c p) n -> p c n", p=P)

            def expert_fills(ph):
                for k in range(2):
                    for which in range(3):
                        n = ph.n0 + 3 * k + which
                        src = expert_chunk(ph, 0, k, which)
                        if not ph.more:
                            fill(n, [(0, src)])
                        else:
                            dst = ring[:, n % RING, :].rearrange("p (c n) -> p c n", c=src.shape[1])
                            sp.dma_start(dst, src).then_inc(S(f"more_slot{n % RING}"), 16)
                with sp.Fori(1, ph.iters) as it:
                    for k in range(2):
                        for which in range(3):
                            n = ph.n0 + 3 * k + which
                            src = expert_chunk(ph, it, k, which)
                            dst = ring[:, n % RING, :].rearrange("p (c n) -> p c n", c=src.shape[1])
                            sp.wait_ge(ph.sem(("gate", "up", "down")[which]), it * 2 + (k - 1 + ph.ub))
                            sp.dma_start(dst, src).then_inc(S(("more_slot" if ph.more else "slot") + str(n % RING)), 16)

            for k, (s0, stream) in enumerate(zip(starts, (stream_0, stream_1, stream_2))):
                for m, parts in enumerate(stream):
                    fill(s0 + m, parts)
                    if k == 0 and m == 1:
                        sp.dma_start(x[:], a["x"][0].rearrange("(c p) n -> p c n", p=P)).then_inc(S("x_in"), 16)
                        sp.dma_start(W(L0["sgw"], N_SG, P), a["sg_w"][0].rearrange("g p q -> p g q")).then_inc(S("sgw_in"), 16)
                ph, more = phases[k], extras[k]
                expert_fills(ph)
                sp.wait_ge(S("slots"), k + 1)
                fills = sp.value_load(fullest[0:1, 0:1])
                with sp.If(fills > P):
                    for m in range(ph.chunks - RING, ph.chunks):
                        sp.wait_ge(*freed[ph.n0 + m])
                    expert_fills(more)
                    sp.wait_ge(more.sem("down"), more.ub + more.units)
                with sp.Else():
                    for m in range(RING):
                        sp.sem_inc(S(f"more_slot{m}"), 16 * more.iters)
            sp.wait_ge(S("norm"), NORM_AT["final"])
            sp.dma_start(out[0].rearrange("(c p) n -> p c n", p=P), x[:]).then_inc(S("stored"), 16)
            sp.wait_ge(S("stored"), 16)


_INS = ["x", "mem", "w_in_a", "w_out_a", "sg_ln_g", "sg_ln_b", "sg_w", "sg_b", "w_in_b", "w_out_b", "w_k_shared",
        "w_v_shared", "w_mem_k", "w_mem_v", "ln1_g", "ln1_b", "ln2_g", "ln2_b", "w_router", "b_router", "w_gate", "w_up",
        "w_down", "mem_2", "g_mix_2", "w_in_2", "ret_decay_fwd_2", "ret_decay_bwd_2", "ret_norm_gain_2",
        "w_ret_o_2", "na_rpb_2", "w_na_o_2", "g_mem_2", "w_mem_kv_2", "w_xa_o_2", "w_out_2", "g_ffn_2",
        "w_router_group_2", "b_router_group_2", "w_router_expert_2", "b_router_expert_2", "w_exp_gate_2",
        "w_exp_up_2", "w_exp_down_2", "g_final_2"]


def kernel(**inputs):
    import concourse.bacc as _bacc
    from concourse.bass_utils import run_bass_kernel_spmd as _run

    nc = _bacc.Bacc("TRN2", target_bir_lowering=False, num_devices=1)
    arrays, args = {}, {}
    for name, value in [(n, inputs[n]) for n in _INS] + list(constants().items()):
        v = np.ascontiguousarray(value)
        arrays[f"in_{name}_dram"] = v
        args[name] = nc.dram_tensor(f"in_{name}_dram", v.shape, mybir.dt.from_np(v.dtype), kind="ExternalInput").ap()
    out = nc.dram_tensor("out_0_dram", (1, T, D), F32, kind="ExternalOutput").ap()
    build(nc, args, out)
    r = _run(nc, [arrays], core_ids=[0])
    return r.results[0]["out_0_dram"]
```

```python
import math

import numpy as np

import concourse.bass as bass
from concourse import mybir
from concourse.alu_op_type import AluOpType as ALU

F32 = mybir.dt.float32
F32R = mybir.dt.float32r
I32 = mybir.dt.int32
ACT = mybir.ActivationFunctionType
AX = mybir.AxisListType

P = 128
T, D = 256, 1024
TC, DC = T // P, D // P
DEPTH = 2
ALPHA = (2 * DEPTH) ** 0.25
LN_EPS, GN_EPS, RMS_EPS = 1e-5, 1e-5, 1e-6
HD = 64
N_SG, SGW = 12, 768
MEMW, MEM_HEADS = 256, 4
DILS = (1, 4, 16)
STEPS = 128
DIL_HEADS = 4
N_EXP, N_GRP, PER_GRP = 16, 4, 4
RET_HEADS, RET_QK, RET_V = 4, 128, 256
NA_HEADS, NA_ROWS, NA_COLS, GRID_W = 8, 8, 16, 64
XA_HEADS = 4
BIG = 1e30

RING = 3
CHUNK = 4096
PIECE = CHUNK // 2
RAW = 2 * RING
SPLIT = 3
CAP = P // 2
MORE = T // CAP - 1
AHEAD = 2
BANKS = 4

C_IDENT, C_FLIP, C_BEFORE, C_ONES, C_IOTA = 0, 128, 256, 384, 512
C_RANK, C_NAMASK, C_MHALF, C_STACK = 640, 672, 736, 744
C_N = 808


def constants():
    c = np.zeros((P, C_N), np.float32)
    c[:, C_IDENT:C_IDENT + P] = np.eye(P)
    flip = np.zeros((P, P))
    for r in range(2):
        for x in range(GRID_W):
            flip[r * GRID_W + x, r * GRID_W + GRID_W - 1 - x] = 1
    c[:, C_FLIP:C_FLIP + P] = flip
    c[:, C_BEFORE:C_BEFORE + P] = np.triu(np.ones((P, P)), 1)
    c[:, C_ONES:C_ONES + P] = 1
    c[:, C_IOTA:C_IOTA + P] = np.arange(P)[None] % CAP
    c[:, C_STACK:C_STACK + CAP] = np.arange(P)[:, None] % CAP == np.arange(CAP)[None]
    c[:, C_RANK:C_RANK + 32] = np.tile(np.arange(3, -1, -1), 8)[None]
    col = GRID_W - 1 - np.arange(P) % GRID_W
    start = np.clip(col - NA_COLS // 2, 0, GRID_W - NA_COLS)
    off = np.arange(GRID_W)[None] - start[:, None]
    c[:, C_NAMASK:C_NAMASK + GRID_W] = np.where((off >= 0) & (off < NA_COLS), 0, -BIG)
    c[:, C_MHALF:C_MHALF + 8] = -0.5
    i = np.arange(T)[:, None]
    j = np.arange(T)[None]
    rel = np.stack([np.where((j <= i) & ((i - j) % d == 0) & ((i - j) // d <= STEPS), i - j, BIG) for d in DILS])
    dist = rel.reshape(3, TC, P, T).transpose(2, 0, 1, 3).reshape(P, 3 * TC * T)
    fwd = np.maximum(j - i, 0).reshape(TC, P, T).transpose(1, 0, 2).reshape(P, TC * T)
    bwd = np.maximum(i - j, 0).reshape(TC, P, T).transpose(1, 0, 2).reshape(P, TC * T)
    half = RET_QK // 2
    inv = np.float32(10000.0) ** (-np.arange(half, dtype=np.float32) / np.float32(half))
    ang = np.arange(T, dtype=np.float32)[:, None] * inv[None].astype(np.float32)
    rope = [f(ang).reshape(TC, P, half).transpose(1, 0, 2).reshape(P, TC * half) for f in (np.cos, np.sin)]
    return {
        "const": c,
        "dist": np.ascontiguousarray(dist.astype(np.float32)),
        "later": np.ascontiguousarray(np.concatenate([fwd, bwd] + rope, 1).astype(np.float32)),
    }


SLOPES = [float(np.float32(2.0) ** np.float32(-8.0 * k / 12)) for k in range(1, 13)]

W_N = 15616
L0 = dict(memN=0, cat=0, memT=2048, sgw=4096, swT=5632, bsN=7168, bsT=7296, u=7424, gv=8960, qmT=10496)
W_P, W_PT = 11008, 12544
L1 = dict(dist=8192, qT=1536, kT=3072, v=4608, qmT=6144, cat=6656)
W_TAB, W_MEM2 = 8192, 11264
W_P2, W_PT2, W_COMB = 11264, 11776, 12288
XA = dict(H=0, memT=2048, mkT=4096, mv=5120, qT=6144, o=7168, oT=0, gate=2048)
NA = dict(qT=4096, kT=5120, v=6144, o=7168, oT=0, gate=2048)
RET = dict(q=0, k=1024, qT=2048, kT=3072, v=4096, rg=6144, D=8192, sd=10240, tmp=11264, y=0, yT=4096, gate=2048)
W_AB, W_ROPE = 14336, 15360
MOE = dict(hT=0, g=1024, u=1536, silu=2048, h=2304, y=2560, pick=3584, pickg=3712, pickT=3968, acc=4224)

NORM_ORDER = ["gv", "ln1_0", "ln2_0", "ln1_1", "ln2_1", "mix", "mem", "gn", "ffn", "final"]
NORM_AT = {name: 2 * (n + 1) for n, name in enumerate(NORM_ORDER)}


def build(nc, a, out):
    from contextlib import ExitStack
    with ExitStack() as ctx:
        def sb(name, shape, dt=F32):
            return ctx.enter_context(nc.sbuf_tensor(name, shape, dt))

        ring = sb("ring", [P, RING, CHUNK])
        raw = ring[:].rearrange("p r (h n) -> p (r h) n", h=2)
        w_hi = sb("w_hi", [P, SPLIT, PIECE], F32R)
        w_lo = sb("w_lo", [P, SPLIT, PIECE], F32R)
        x = sb("x", [P, TC, D])
        xT_at = nc.sbuf_base
        xT = sb("xT", [P, DC, T])
        xe = nc.alloc_sbuf_tensor_at("xe", [P, 2, DC, P], F32R, offset=xT_at)
        mkv = sb("mkv", [P, DEPTH, 2, 512])
        prm = sb("prm", [P, 2, 2, D])
        con = sb("con", [P, C_N])
        work_at = nc.sbuf_base
        work = sb("work", [P, W_N])
        hT = nc.alloc_sbuf_tensor_at("hT", [P, 2, 4, P], F32R, offset=work_at + 4 * MOE["hT"])
        wr = sb("wr", [P, DC, 16])
        wr2 = sb("wr2", [P, DC, 20])
        br = sb("br", [P, TC, 16])
        br2 = sb("br2", [P, TC, 20])
        dec = sb("dec", [P, 8])
        stats = sb("stats", [P, 8, 6])
        mv8 = sb("mv8", [P, 8, 2])
        var8 = sb("var8", [P, 8])
        rstd = sb("rstd", [P, 8])
        att_mx = sb("att_mx", [P, 64])
        att_nm = sb("att_nm", [P, 64])
        att_sum = sb("att_sum", [P, 64])
        att_rec = sb("att_rec", [P, 64])
        rt = sb("rt", [P, 16, 32])
        rsm = sb("rsm", [P, 16, 8])
        sel = sb("sel", [P, TC, N_EXP])
        gates = sb("gates", [P, TC, N_EXP])
        slot_main = sb("slot_main", [P, TC, N_EXP])
        slot_more = sb("slot_more", [P, TC, N_EXP])
        fullest = sb("fullest", [P, 1], I32)
        fullest_f = sb("fullest_f", [P, 1])
        lg = sb("lg", [P, 10, 8])

        psum_all = ctx.enter_context(nc.psum_tensor("psum", [P, 8, 512], F32))
        psum = [psum_all[:, i, :] for i in range(8)]
        RB = {"v": psum[0:4], "a": psum[4:8]}

        sems = {}

        def S(name):
            if name not in sems:
                sems[name] = ctx.enter_context(nc.semaphore(name))
            return sems[name]

        def W(at, *shape):
            n = int(np.prod(shape))
            ap = work[:, at:at + n]
            if len(shape) == 1:
                return ap
            names = "abc"[:len(shape)]
            return ap.rearrange(f"p ({' '.join(names)}) -> p {' '.join(names)}", **dict(zip(names, shape)))

        ident = con[:, C_IDENT:C_IDENT + P]
        flip = con[:, C_FLIP:C_FLIP + P]
        before = con[:, C_BEFORE:C_BEFORE + P]
        ones = con[:, C_ONES:C_ONES + P]
        iota = con[:, C_IOTA:C_IOTA + P]
        stack = con[:, C_STACK:C_STACK + CAP]
        rank0 = con[:, C_RANK:C_RANK + 32].rearrange("p (g e) -> p g e", e=4)
        namask = con[:, C_NAMASK:C_NAMASK + GRID_W]
        mhalf = con[:, C_MHALF:C_MHALF + 8]

        block = ctx.enter_context(nc.Block())

        def cols(w, c0, n):
            return w[:, c0:c0 + n].rearrange("(c p) n -> p c n", p=P)

        def rows(w, r0, n):
            return w[r0:r0 + n, :].rearrange("(c p) n -> p c n", p=P)

        w_in_a, w_out_a = a["w_in_a"][0], a["w_out_a"][0]
        w_in_b, w_out_b = a["w_in_b"][0], a["w_out_b"][0]
        w2 = a["w_in_2"][0]
        stream_0 = [[(0, cols(a["w_mem_k"][l], 0, 256)), (2048, cols(a["w_mem_v"][l], 0, 256))] for l in range(2)]
        stream_0 += [[(0, cols(w_in_a, SGW, 512))], [(0, cols(w_in_a, SGW + 512, 512))],
                     [(0, cols(w_in_a, 0, 512))], [(0, cols(w_in_a, 512, 256))],
                     [(0, cols(w_out_a, 0, 512))], [(0, cols(w_out_a, 512, 512))]]
        stream_1 = [[(0, cols(w_in_b, 0, 512))], [(0, cols(w_in_b, 512, 512))],
                    [(0, cols(a["w_k_shared"], 0, 512))], [(0, cols(a["w_v_shared"], 0, 512))],
                    [(0, cols(a["w_k_shared"], 512, 256)), (2048, cols(a["w_v_shared"], 512, 256))],
                    [(0, rows(w_out_b, 0, 512))]]
        O_RQ, O_RK, O_RV, O_RG, O_NQ, O_NK, O_NV, O_XQ, O_G = 0, 512, 1024, 2048, 3072, 3584, 4096, 4608, 5120
        stream_2 = [[(0, cols(w2, O_XQ, 512))],
                    [(0, cols(a["w_mem_kv_2"][0], 0, 512))], [(0, cols(a["w_mem_kv_2"][0], 512, 512))],
                    [(0, cols(w2, O_G + 2048, 512))], [(0, cols(w2, O_G + 2560, 512))],
                    [(0, rows(a["w_xa_o_2"][0], 0, 512))],
                    [(0, cols(w2, O_NQ, 512))], [(0, cols(w2, O_NK, 512))], [(0, cols(w2, O_NV, 512))],
                    [(0, cols(w2, O_G + 1024, 512))], [(0, cols(w2, O_G + 1536, 512))],
                    [(0, rows(a["w_na_o_2"][0], 0, 512))],
                    [(0, cols(w2, O_RQ, 512))], [(0, cols(w2, O_RK, 512))],
                    [(0, cols(w2, O_RV, 512))], [(0, cols(w2, O_RV + 512, 512))],
                    [(0, cols(w2, O_RG, 512))], [(0, cols(w2, O_RG + 512, 512))],
                    [(0, cols(w2, O_G, 512))], [(0, cols(w2, O_G + 512, 512))],
                    [(0, cols(a["w_ret_o_2"][0], 0, 512))], [(0, cols(a["w_ret_o_2"][0], 512, 512))],
                    [(0, cols(a["w_out_2"][0], 0, 512))], [(0, cols(a["w_out_2"][0], 512, 512))]]

        def plus(a, b):
            return a + b if not isinstance(a, int) else b + a

        class Pass:
            def __init__(self, wg, wu, wd, halves, n0, slots, before, more):
                self.wg, self.wu, self.wd, self.halves, self.n0 = wg, wu, wd, halves, n0
                self.slots, self.more = slots, more
                self.units = N_EXP * halves
                self.iters = self.units // 4
                self.lead = 1 if halves == 2 else 2
                U, E = self.units, N_EXP
                self.per = dict(hi=6 * U, lo=6 * U, used=6 * U, gu=2 * U, t_full=U, silu=U, h=U, h_hi=U, h_lo=U,
                                pick=2 * E, gathered=E, xe_hi=E, xe_lo=E, pickg=2 * E, pick_turned=E,
                                pickT=E + 1, y=E + 1, scattered=4 * (E + 1), added=4 * (E + 1), shift=1, piece=16 * U)
                times = MORE if more else 1
                self.before = {k: sum(o.per[k] for o in before) * times for k in self.per}

            def sem(self, name):
                return S(("more_" if self.more else "moe_") + name)

            def base(self, p):
                return {k: self.before[k] if p is None else p * self.per[k] + self.before[k] for k in self.per}

            def skip(self, eng, names):
                for name in names.split():
                    eng.sem_inc(self.sem(name), MORE * self.per[name])

            def expert(self, it, k):
                return it * 2 + k // 2 if self.halves == 2 else it * 4 + k

            def there_is(self, e):
                return not isinstance(e, int) or e < N_EXP

            def first(self, k):
                return self.halves == 1 or k % 2 == 0

            def last(self, k):
                return self.halves == 1 or k % 2 == 1

            def buffer(self, k):
                return (k // 2 if self.halves == 2 else k) % 2

            def slot(self, idx):
                return (2 * self.n0 + idx) % RAW

            def landed(self, eng, it, k, q, B):
                if k is None:
                    eng.wait_ge(self.sem("piece%d" % self.slot(q)), plus(16, B["piece"]))
                else:
                    eng.wait_ge(self.sem("piece%d" % self.slot(4 + q)), plus(it * 64 + 16 * (k + (4 + q) // 6 + 1), B["piece"]))

            def run(self, eng, step):
                with eng.Fori(0, self.iters - 1) as it:
                    for k in range(4):
                        step(it, k, True, True)
                for k in range(4):
                    step(self.iters - 1, k, k < 3, k < 2)

            def passes(self, eng, one):
                if not self.more:
                    one(self, None)
                else:
                    with eng.Fori(0, MORE) as p:
                        one(self, p)

        phases, extras = [], []
        n_at = 0
        starts = []
        for tag, stream, halves, suffix in (("0", stream_0, 2, ""), ("1", stream_1, 2, ""), ("2", stream_2, 1, "_2")):
            starts.append(n_at)
            n_at += len(stream)
            if halves == 2:
                wg, wu, wd = (a[k][int(tag)] for k in ("w_gate", "w_up", "w_down"))
            else:
                wg, wu, wd = (a[k][0].rearrange("g e r c -> (g e) r c") for k in ("w_exp_gate_2", "w_exp_up_2", "w_exp_down_2"))
            ph = Pass(wg, wu, wd, halves, n_at, slot_main, phases, False)
            extras.append(Pass(wg, wu, wd, halves, 0, slot_more, extras, True))
            phases.append(ph)
            n_at += 3 * ph.units

        landed, count = {}, [0] * RING

        def note(n, parts):
            count[n % RING] += 16 * parts
            landed[n] = count[n % RING]

        for s0, stream in zip(starts, (stream_0, stream_1, stream_2)):
            for k, parts in enumerate(stream):
                note(s0 + k, len(parts))

        freed = {}

        @block.tensor
        def _(pe):
            taken = {"v": 0, "a": 0}
            emptied = {"v": [], "a": []}
            made = {}

            def bank(r, product=None, by=None):
                j = taken[r]
                taken[r] += 1
                if j >= BANKS:
                    pe.wait_ge(*emptied[r][j - BANKS])
                if by is None:
                    key = product + "_" + r
                    made[key] = made.get(key, 0) + 1
                    by = (S(key), made[key])
                emptied[r].append(by)
                return RB[r][j % BANKS]

            def full(r, ins):
                ins.then_inc(S(r + "_full"), 1)
                return (S(r + "_full"), taken[r])

            def wait_made(product):
                for r in "va":
                    if product + "_" + r in made:
                        pe.wait_ge(S(product + "_" + r), made[product + "_" + r])

            def chunk(n):
                pe.wait_ge(S(f"slot{n % RING}"), landed[n])
                return ring[:, n % RING, :]

            def turn(src, tiles, product, norm=None):
                for t in range(TC):
                    if norm is not None:
                        pe.wait_ge(S("norm"), NORM_AT[norm] - TC + 1 + t)
                    for j in range(tiles // 4):
                        r = "va"[(t * (tiles // 4) + j) % 2]
                        b = bank(r, product)
                        for c in range(4):
                            ins = pe.transpose(b[:, c * P:(c + 1) * P], src[:, t, (4 * j + c) * P:(4 * j + c + 1) * P], ident)
                        full(r, ins)

            def gemm(b, cols_at, lhsT, rhs, k):
                for c in range(k):
                    ins = pe.matmul(b[:, cols_at[0]:cols_at[1]], lhsT=lhsT(c), rhs=rhs(c), start=(c == 0), stop=(c == k - 1))
                return ins

            def nat(w, act, k, n, r, product, pack=False):
                for t in range(TC):
                    if t == 0 or not pack:
                        b = bank(r, product)
                    at = (t * n, (t + 1) * n) if pack else (0, n)
                    ins = gemm(b, at, lambda c: act[:, c, t * P:(t + 1) * P], lambda c: w[:, c, :], k)
                    if not pack or t == TC - 1:
                        done = full(r, ins)
                return done

            def turned(w, act, k, tiles, r, product):
                for j in range(tiles // 2):
                    b = bank(r, product)
                    for cc in range(2):
                        f = (2 * j + cc) * P
                        ins = gemm(b, (cc * T, (cc + 1) * T), lambda c: w[:, c, f:f + P], lambda c: act[:, c, :], k)
                    done = full(r, ins)
                return done

            def as_cols(n, at=0, width=512):
                return chunk(n)[:, at:at + 8 * width].rearrange("p (c n) -> p c n", c=8)

            def as_rows(n):
                return chunk(n).rearrange("p (c n) -> p c n", c=4)

            att = {"i": 0, "sc": 0}

            def attention(q, keys, v, nk, dv, n_tasks, bias=None, tables=False):
                i0 = att["i"]
                att["i"] += n_tasks

                def scores(i):
                    h, t = divmod(i, TC)
                    ks = keys(h)
                    for first in range(0, len(ks), 2):
                        mine = ks[first:first + 2]
                        if tables:
                            att["sc"] += len(mine)
                            b = bank("v", by=(S("att_sc"), att["sc"]))
                        else:
                            b = bank("v", by=(S("att_p"), i0 + i + 1))
                        for g, kk in enumerate(mine):
                            o = b[:, g * T:(g + 1) * T]
                            if bias is not None:
                                pe.matmul(o, lhsT=flip, rhs=bias(h, t), start=True, stop=False)
                            ins = pe.matmul(o, lhsT=q(h, t, first + g), rhs=kk, start=(bias is None), stop=True)
                        full("v", ins)

                def turn_weights(i):
                    pe.wait_ge(S("att_p"), i0 + i + 1)
                    p = W(p_at, 2, nk * P)
                    for first in range(0, nk, 4):
                        m = min(4, nk - first)
                        b = bank("a", "att_pT")
                        for k in range(m):
                            ins = pe.transpose(b[:, k * P:(k + 1) * P], p[:, i % 2, (first + k) * P:(first + k + 1) * P], ident)
                        full("a", ins)
                    upto[i] = made["att_pT_a"]

                def values(i):
                    h = i // TC
                    pe.wait_ge(S("att_pT_a"), upto[i])
                    pT = W(pT_at, 2, nk * P)
                    b = bank("v", by=(S("att_o"), i0 + i + 1))
                    for k in range(nk):
                        ins = pe.matmul(b[:, 0:dv], lhsT=pT[:, i % 2, k * P:(k + 1) * P], rhs=v(h, k),
                                        start=(k == 0), stop=(k == nk - 1))
                    full("v", ins)

                upto = {}
                for i in range(n_tasks + 3):
                    if i < n_tasks:
                        scores(i)
                    if 2 <= i < n_tasks + 2:
                        turn_weights(i - 2)
                    if i >= 3:
                        values(i - 3)
                pe.wait_ge(S("att_o"), att["i"])

            def route(w, n, k):
                b = bank("v", by=(S("logits_read"), k))
                for t in range(TC):
                    ins = gemm(b, (t * n, (t + 1) * n), lambda c: xT[:, c, t * P:(t + 1) * P], lambda c: w[:, c, :], DC)
                full("v", ins)
                pe.wait_ge(S("chosen"), k)
                b = bank("v", by=(S("slots"), k))
                pe.matmul(b[:, 0:16], lhsT=before, rhs=sel[:, 0, :], start=True, stop=True)
                pe.matmul(b[:, 16:32], lhsT=ones, rhs=sel[:, 0, :], start=True, stop=False)
                pe.matmul(b[:, 16:32], lhsT=before, rhs=sel[:, 1, :], start=False, stop=True)
                pe.matmul(b[:, 32:48], lhsT=ones, rhs=sel[:, 0, :], start=True, stop=False)
                ins = pe.matmul(b[:, 32:48], lhsT=ones, rhs=sel[:, 1, :], start=False, stop=True)
                full("v", ins)

            def drain():
                for r in "va":
                    for by in emptied[r][-BANKS:]:
                        pe.wait_ge(*by)

            def experts(ph, p):
                sem, B, lead = ph.sem, ph.base(p), ph.lead
                g_bank, u_bank, y_bank, t_bank, x_bank = psum[0:2], psum[2:4], psum[4:6], psum[6], psum[7]
                g, u_, y = W(MOE["g"], 4, P), W(MOE["u"], 4, P), W(MOE["y"], 2, 512)
                pick, pickg, pickT = W(MOE["pick"], TC, CAP), W(MOE["pickg"], TC, P), W(MOE["pickT"], TC, P)

                def gather(e):
                    pe.wait_ge(sem("pick"), plus(e * 2 + 2, B["pick"]))
                    for c in range(DC):
                        for t in range(TC):
                            ins = pe.matmul(x_bank[:, c * CAP:(c + 1) * CAP], lhsT=x[:, t, c * P:(c + 1) * P], rhs=pick[:, t, :],
                                            start=(t == 0), stop=(t == TC - 1))
                    ins.then_inc(sem("gathered"), 1)

                def scatter(e, j):
                    if j == 0:
                        pe.wait_ge(sem("y"), plus(e + 1, B["y"]))
                        pe.wait_ge(sem("pickT"), plus(e + 1, B["pickT"]))
                        if ph.there_is(e + (lead - 1)):
                            pe.wait_ge(sem("xe_lo"), plus(e + lead, B["xe_lo"]))
                        to = x_bank
                    elif isinstance(e, int) and e == N_EXP:
                        to = psum[j]
                    else:
                        pe.wait_ge(sem("added"), plus(e * 4 + j, B["added"]))
                        to = x_bank
                    pe.matmul(to, lhsT=pickT[:, j // 2, :], rhs=y[:, j % 2, :], start=True, stop=True).then_inc(sem("scattered"), 1)

                def split_wait(it, k, q):
                    if k is None:
                        pe.wait_ge(sem("lo"), plus(q + 1, B["lo"]))
                        return q % SPLIT
                    pe.wait_ge(sem("lo"), plus(it * 24 + (6 * k + 4 + q + 1), B["lo"]))
                    return (4 + q) % SPLIT

                def up(it, k, q, to, buf, half):
                    sl = split_wait(it, k, q)
                    for c in range(4):
                        for part in (w_hi, w_lo):
                            ins = pe.matmul(to, lhsT=xe[:, buf, 4 * half + c, :], rhs=part[:, sl, c * 512:(c + 1) * 512],
                                            start=(half == 0 and c == 0 and part is w_hi), stop=(half == 1 and c == 3 and part is w_lo))
                    ins.then_inc(sem("used"), 1)

                def step(it, k, more1, more2):
                    first, last = ph.first(k), ph.last(k)
                    e = ph.expert(it, k)
                    pe.wait_ge(sem("gu"), plus(it * 8 + (2 * k + 2), B["gu"]))
                    for i, src in enumerate((g, u_)):
                        for c in range(4):
                            at = (4 * i + c) * CAP
                            ins = pe.matmul(t_bank[:, at:at + CAP], lhsT=src[:, c, :], rhs=stack, start=True, stop=True)
                    ins.then_inc(sem("t_full"), 1)
                    nk = (k + 1) % 2
                    buf = ph.buffer(k + 1)
                    for q in range(4):
                        if first:
                            scatter(e, q)
                        if more1:
                            if q == 0 and ph.first(k + 1):
                                pe.wait_ge(sem("xe_lo"), plus(ph.expert(it, k + 1) + 1, B["xe_lo"]))
                            up(it, k, q, (g_bank if q < 2 else u_bank)[nk], buf, q % 2)
                    if first:
                        pe.wait_ge(sem("added"), plus(e * 4 + 4, B["added"]))
                        if ph.there_is(e + lead):
                            gather(e + lead)
                    pe.wait_ge(sem("h_lo"), plus(it * 4 + (k + 1), B["h_lo"]))
                    for half in range(2):
                        sl = split_wait(it, k, (4 if more1 else 0) + half)
                        for c in range(2):
                            for part in (w_hi, w_lo):
                                for n2 in range(2):
                                    ins = pe.matmul(y_bank[n2], lhsT=hT[:, k % 2, 2 * half + c, :],
                                                    rhs=part[:, sl, c * D + n2 * 512:c * D + (n2 + 1) * 512],
                                                    start=(first and half == 0 and c == 0 and part is w_hi),
                                                    stop=(last and half == 1 and c == 1 and part is w_lo))
                        ins.then_inc(sem("used"), 1)
                    if first:
                        pe.wait_ge(sem("pickg"), plus(e * 2 + 2, B["pickg"]))
                        if ph.there_is(e + lead):
                            pe.wait_ge(sem("xe_lo"), plus(e + (lead + 1), B["xe_lo"]))
                        for t in range(TC):
                            ins = pe.transpose(x_bank[:, t * P:(t + 1) * P], pickg[:, t, :], ident)
                        ins.then_inc(sem("pick_turned"), 1)

                gather(0)
                pe.wait_ge(sem("xe_lo"), plus(1, B["xe_lo"]))
                for q in range(4):
                    if q == 2 and lead == 2:
                        gather(1)
                    up(None, None, q, (g_bank if q < 2 else u_bank)[0], 0, q % 2)
                ph.run(pe, step)
                for j in range(4):
                    scatter(N_EXP, j)
                pe.wait_ge(sem("added"), plus(4 * (N_EXP + 1), B["added"]))

            def expert_layer(k):
                drain()
                ph = phases[k]
                ph.passes(pe, experts)
                for m in range(RING):
                    freed[ph.n0 + 3 * ph.units - RING + m] = (ph.sem("lo"), ph.before["lo"] + ph.per["lo"] - RAW + 2 * m + 2)
                fills = pe.value_load(fullest[0:1, 0:1])
                with pe.If(fills > CAP):
                    extras[k].passes(pe, experts)
                with pe.Else():
                    extras[k].skip(pe, "used t_full gathered pick_turned scattered")

            n = 0
            pe.wait_ge(S("con_in"), 16)
            pe.wait_ge(S("mem_in"), 16)
            turn(W(L0["memN"], TC, D), DC, "memT")
            wait_made("memT")
            memT = W(L0["memT"], DC, T)
            for l in range(DEPTH):
                turned(as_cols(n, 0, 256), memT, DC, 2, "v", "mkv")
                freed[n] = nat(as_cols(n, 2048, 256), memT, DC, 256, "a", "mkv", pack=True)
                n += 1
            pe.wait_ge(S("x_in"), 16)
            turn(x, DC, "xT")
            wait_made("xT")
            freed[n] = nat(as_cols(n), xT, DC, 512, "a", "gv"); n += 1
            w = as_cols(n)
            nat(w[:, :, 0:256], xT, DC, 256, "a", "gv", pack=True)
            freed[n] = turned(w[:, :, 256:512], xT, DC, 2, "v", "qm"); n += 1
            freed[n] = nat(as_cols(n), xT, DC, 512, "a", "u"); n += 1
            freed[n] = nat(as_cols(n, 0, 256), xT, DC, 256, "a", "u", pack=True); n += 1
            pe.wait_ge(S("sg_causal"), 1)
            sgw = W(L0["sgw"], N_SG, P)
            for j in range(3):
                b = bank("v", "sw")
                for g in range(4):
                    ins = pe.transpose(b[:, g * P:(g + 1) * P], sgw[:, 4 * j + g, :], ident)
                full("v", ins)
            b = bank("v", "sw")
            full("v", pe.transpose(b[:, 0:N_SG], W(L0["bsN"], P)[0:N_SG, :], ident[0:N_SG, 0:N_SG]))
            qmT = W(L0["qmT"], 2, T)
            wait_made("qm")
            wait_made("mkv")

            def mem_attention(qT, l):
                mk = mkv[:, l, 0, :].rearrange("p (c m) -> p c m", c=2)
                mv = mkv[:, l, 1, :].rearrange("p (c n) -> p c n", c=2)

                def hp(h):
                    return slice(HD * (h % 2), HD * (h % 2) + HD)
                attention(lambda h, t, g: qT[hp(h), h // 2, t * P:(t + 1) * P], lambda h: [mk[hp(h), h // 2, :]],
                          lambda h, k: mv[:, k, h * HD:(h + 1) * HD], 2, HD, 2 * MEM_HEADS)

            p_at, pT_at = W_P, W_PT
            mem_attention(qmT, 0)
            gv, swT = W(L0["gv"], TC, SGW), W(L0["swT"], N_SG, P)
            wait_made("sw")
            pe.wait_ge(S("norm"), NORM_AT["gv"])
            for j in range(3):
                b = bank("v", by=(S("mix"), 4 * (j + 1)))
                for g in range(4):
                    hh = 4 * j + g
                    ins = pe.matmul(b[:, g * P:(g + 1) * P].rearrange("p (c d) -> p c d", c=2), lhsT=swT[:, hh, :],
                                    rhs=gv[:, :, hh * HD:(hh + 1) * HD], start=True, stop=True)
                full("v", ins)
            pe.wait_ge(S("mix"), N_SG)
            turn(W(L0["cat"], TC, D), DC, "xT")
            wait_made("xT")
            for half in range(2):
                freed[n] = nat(as_cols(n), xT, DC, 512, "v", "z"); n += 1
            turn(x, DC, "xT", "ln1_0")
            wait_made("xT")
            pe.wait_ge(S("wr_in"), 16)
            route(wr, 16, 1)
            expert_layer(0)
            n += 3 * phases[0].units

            turn(x, DC, "xT", "ln2_0")
            wait_made("xT")
            freed[n] = turned(as_cols(n), xT, DC, 4, "v", "qkv"); n += 1
            w = as_cols(n)
            turned(w[:, :, 0:256], xT, DC, 2, "a", "qkv")
            freed[n] = turned(w[:, :, 256:512], xT, DC, 2, "a", "qkv"); n += 1
            freed[n] = turned(as_cols(n), xT, DC, 4, "v", "qkv"); n += 1
            freed[n] = nat(as_cols(n), xT, DC, 512, "a", "qkv"); n += 1
            turned(as_cols(n, 0, 256), xT, DC, 2, "v", "qkv")
            freed[n] = nat(as_cols(n, 2048, 256), xT, DC, 256, "a", "qkv", pack=True); n += 1
            wait_made("qkv")
            qT, kT, v = W(L1["qT"], 6, T), W(L1["kT"], 6, T), W(L1["v"], TC, SGW)

            def pair(g, h):
                hh = g * DIL_HEADS + h
                return slice(HD * (hh % 2), HD * (hh % 2) + HD), hh // 2

            def dil_q(h, t, g):
                r, tile = pair(g, h)
                return qT[r, tile, t * P:(t + 1) * P]

            def dil_k(h):
                return [kT[pair(g, h)[0], pair(g, h)[1], :] for g in range(3)]

            def dil_v(h, k):
                hh = (k // 2) * DIL_HEADS + h
                return v[:, k % 2, hh * HD:(hh + 1) * HD]

            attention(dil_q, dil_k, dil_v, 6, HD, 2 * DIL_HEADS, tables=True)
            mem_attention(W(L1["qmT"], 2, T), 1)
            turn(W(L1["cat"], TC, 512), 4, "xT")
            wait_made("xT")
            w = as_rows(n)
            for half in range(2):
                freed[n] = nat(w[:, :, half * 512:(half + 1) * 512], xT, 4, 512, "v", "z")
            n += 1
            turn(x, DC, "xT", "ln1_1")
            wait_made("xT")
            route(wr, 16, 2)
            expert_layer(1)
            n += 3 * phases[1].units

            p_at, pT_at = W_P2, W_PT2
            turn(W(XA["H"], TC, D), DC, "xT", "mix")
            wait_made("xT")
            freed[n] = turned(as_cols(n), xT, DC, 4, "v", "xa"); n += 1
            turn(W(W_MEM2, TC, D), DC, "memT", "mem")
            wait_made("memT")
            memT = W(XA["memT"], DC, T)
            freed[n] = turned(as_cols(n), memT, DC, 4, "v", "xa"); n += 1
            freed[n] = nat(as_cols(n), memT, DC, 512, "a", "xa"); n += 1
            wait_made("xa")
            qT, kT, v = W(XA["qT"], 4, T), W(XA["mkT"], 4, T), W(XA["mv"], TC, 512)
            attention(lambda h, t, g: qT[:, h, t * P:(t + 1) * P], lambda h: [kT[:, h, :]],
                      lambda h, k: v[:, k, h * P:(h + 1) * P], 2, P, 2 * XA_HEADS)

            def join(o, oT, k):
                nonlocal n
                for half in range(2):
                    freed[n] = nat(as_cols(n), xT, DC, 512, "a", "gate"); n += 1
                turn(o, k, "oT")
                wait_made("oT")
                wait_made("gate")
                if k == 4:
                    w = as_rows(n)
                    for half in range(2):
                        freed[n] = nat(w[:, :, half * 512:(half + 1) * 512], oT, 4, 512, "v", "joined")
                    n += 1
                else:
                    for half in range(2):
                        freed[n] = nat(as_cols(n), oT, DC, 512, "v", "joined"); n += 1

            join(W(XA["o"], TC, 512), W(XA["oT"], 4, T), 4)

            freed[n] = turned(as_cols(n), xT, DC, 4, "v", "na"); n += 1
            freed[n] = turned(as_cols(n), xT, DC, 4, "a", "na"); n += 1
            freed[n] = nat(as_cols(n), xT, DC, 512, "a", "na"); n += 1
            wait_made("na")
            pe.wait_ge(S("na_table"), 1)
            qT, kT, v = W(NA["qT"], 4, T), W(NA["kT"], 4, T), W(NA["v"], TC, 512)
            table = W(W_TAB, NA_HEADS, 6 * GRID_W)

            def na_rows(h):
                return slice(HD * (h % 2), HD * (h % 2) + HD)

            attention(lambda h, t, g: qT[na_rows(h), h // 2, t * P:(t + 1) * P], lambda h: [kT[na_rows(h), h // 2, :]],
                      lambda h, k: v[:, k, h * HD:(h + 1) * HD], 2, HD, 2 * NA_HEADS,
                      bias=lambda h, t: table[:, h, (1 - t) * P:(1 - t) * P + T])
            join(W(NA["o"], TC, 512), W(NA["oT"], 4, T), 4)

            wait_made("joined")
            freed[n] = nat(as_cols(n), xT, DC, 512, "v", "rope"); n += 1
            freed[n] = nat(as_cols(n), xT, DC, 512, "v", "rope"); n += 1
            for half in range(2):
                freed[n] = nat(as_cols(n), xT, DC, 512, "a", "rv"); n += 1
            for half in range(2):
                freed[n] = nat(as_cols(n), xT, DC, 512, "a", "rg"); n += 1
            wait_made("rope")
            turn(W(RET["q"], TC, 512), 4, "rqk")
            turn(W(RET["k"], TC, 512), 4, "rqk")
            wait_made("rqk")
            wait_made("rv")
            qT, kT, v, sd = W(RET["qT"], 4, T), W(RET["kT"], 4, T), W(RET["v"], TC, D), W(RET["sd"], 2, TC, T)
            for h in range(RET_HEADS + 1):
                if h < RET_HEADS:
                    b = bank("v", by=(S("ret_sd"), h + 1))
                    for j in range(TC):
                        ins = pe.matmul(b[:, j * T:(j + 1) * T], lhsT=kT[:, h, j * P:(j + 1) * P], rhs=qT[:, h, :], start=True, stop=True)
                    full("v", ins)
                if h >= 1:
                    g = h - 1
                    pe.wait_ge(S("ret_sd"), g + 1)
                    b = bank("a", "ret_y")
                    for i in range(TC):
                        for j in range(TC):
                            ins = pe.matmul(b[:, i * RET_V:(i + 1) * RET_V], lhsT=sd[:, g % 2, j, i * P:(i + 1) * P],
                                            rhs=v[:, j, g * RET_V:(g + 1) * RET_V], start=(j == 0), stop=(j == TC - 1))
                    full("a", ins)
            pe.wait_ge(S("norm"), NORM_AT["gn"])
            join(W(RET["y"], TC, D), W(RET["yT"], DC, T), DC)
            wait_made("joined")
            turn(W(W_COMB, TC, D), DC, "xT")
            wait_made("xT")
            for half in range(2):
                freed[n] = nat(as_cols(n), xT, DC, 512, "v", "z"); n += 1
            turn(x, DC, "xT", "ffn")
            wait_made("xT")
            pe.wait_ge(S("wr2_in"), 32)
            route(wr2, 20, 3)
            expert_layer(2)

        @block.scalar
        def _(act):
            took = [0]
            counted = {}

            def bank():
                took[0] += 1
                act.wait_ge(S("a_full"), took[0])
                return RB["a"][(took[0] - 1) % BANKS]

            def step(ins):
                counted["act_step"] = counted.get("act_step", 0) + 1
                ins.then_inc(S("act_step"), 1)
                act.wait_ge(S("act_step"), counted["act_step"])

            def empty(dst, product, func=ACT.Copy, n=512, scale=None):
                b = bank()
                src = b[:, 0:n]
                if len(dst.shape) == 3:
                    src = src.rearrange("p (a b) -> p a b", a=dst.shape[1])
                kw = {} if scale is None else {"scale": scale}
                act.activation(dst, src, func, **kw).then_inc(S(product + "_a"), 1)

            def turn(dst, tiles, product):
                for job in range(1, tiles // 2, 2):
                    t, j = divmod(job, tiles // 4)
                    empty(dst[:, 4 * j:4 * j + 4, t * P:(t + 1) * P], product)

            def nat(dst, n, product, func=ACT.Copy, pack=False):
                if pack:
                    empty(dst, product, func)
                else:
                    for t in range(TC):
                        empty(dst[:, t, :], product, func, n)

            att = {"i": 0}

            def attention(nk, n_tasks, scale, p_at, pT_at, tables=False):
                i0 = att["i"]
                att["i"] += n_tasks
                p, pT = W(p_at, 2, nk * P), W(pT_at, 2, nk * P)
                for i in range(n_tasks + 2):
                    if i >= 2:
                        for first in range(0, nk, 4):
                            m = min(4, nk - first) * P
                            empty(pT[:, i % 2, first * P:first * P + m], "att_pT", n=m)
                    if i < n_tasks:
                        act.wait_ge(S("att_nm"), i0 + i + 1)
                        I = i0 + i
                        if tables:
                            src = p[:, i % 2, :]
                        else:
                            src = score_bank(i0 + i)
                        act.activation(p[:, i % 2, :], src, ACT.Exp, bias=att_nm[:, I:I + 1], scale=scale,
                                       accum_out=att_sum[:, I:I + 1]).then_inc(S("att_p"), 1)

            def score_bank(i):
                return RB["v"][score_at[i] % BANKS][:, 0:T]

            score_at = {}
            v_jobs = 0

            def plan(before, i0, n_tasks):
                j = before
                for i in range(n_tasks + 3):
                    if i < n_tasks:
                        score_at[i0 + i] = j
                        j += 1
                    if i >= 3:
                        j += 1
                return j

            def routed(k):
                act.wait_ge(S("logit_max"), k)
                e, lgt, nm, sm = rt[:, 1, :], rt[:, 0, :], rsm[:, 0, :], rsm[:, 1, :]
                if k < 3:
                    for c in range(TC):
                        act.activation(e[:, c * 16:(c + 1) * 16], lgt[:, c * 16:(c + 1) * 16], ACT.Exp, bias=nm[:, c:c + 1],
                                       accum_out=sm[:, c:c + 1]).then_inc(S("logit_exp"), 1)
                else:
                    act.activation(rt[:, 3, :], rt[:, 2, :], ACT.Exp).then_inc(S("logit_exp"), 1)
                    act.activation(rsm[:, 3, :], rsm[:, 2, :], ACT.Exp).then_inc(S("logit_exp"), 1)

            def experts(ph, p, ahead=False):
                sem, B, lead = ph.sem, ph.base(p), ph.lead
                g, u_, silu, h, y = W(MOE["g"], 512), W(MOE["u"], 512), W(MOE["silu"], 256), W(MOE["h"], 4, CAP), W(MOE["y"], 2, 512)
                pickT = W(MOE["pickT"], T)

                def high(it, k, q):
                    ph.landed(act, it, k, q, B)
                    if k is None:
                        r, sl = ph.slot(q), q % SPLIT
                        if q >= SPLIT:
                            act.wait_ge(sem("used"), plus(q - SPLIT + 1, B["used"]))
                    else:
                        r, sl = ph.slot(4 + q), (4 + q) % SPLIT
                        act.wait_ge(sem("used"), plus(it * 24 + (6 * k + 4 + q - SPLIT + 1), B["used"]))
                    act.copy(w_hi[:, sl, :], raw[:, r, :]).then_inc(sem("hi"), 1)

                def gate_up(bank_at, used):
                    for dst, b, d in ((g, psum[bank_at], -2), (u_, psum[2 + bank_at], 0)):
                        act.wait_ge(sem("used"), plus(used, B["used"]) + d)
                        act.copy(dst, b).then_inc(sem("gu"), 1)

                def tokens(e, buf):
                    act.wait_ge(sem("gathered"), plus(e + 1, B["gathered"]))
                    act.copy(xe[:, buf, :, 0:CAP], psum[7].rearrange("p (c s) -> p c s", c=DC)).then_inc(sem("xe_hi"), 1)

                def step(it, k, more1, more2):
                    first, last = ph.first(k), ph.last(k)
                    e = ph.expert(it, k)
                    act.wait_ge(sem("t_full"), plus(it * 4 + (k + 1), B["t_full"]))
                    act.activation(silu, psum[6][:, 0:256], ACT.Silu).then_inc(sem("silu"), 1)
                    if more1:
                        high(it, k, 2)
                    act.wait_ge(sem("h"), plus(it * 4 + (k + 1), B["h"]))
                    act.copy(hT[:, k % 2, :, 0:CAP], h).then_inc(sem("h_hi"), 1)
                    if more1:
                        high(it, k, 3)
                        high(it, k, 4)
                        high(it, k, 5)
                        gate_up((k + 1) % 2, it * 24 + (6 * k + 8))
                    else:
                        high(it, k, 0)
                        high(it, k, 1)
                    if more2:
                        high(it, k + 1, 0)
                    if first:
                        if ph.there_is(e + lead):
                            tokens(e + lead, ph.buffer(k + lead * ph.halves))
                    if more2:
                        high(it, k + 1, 1)
                    if last:
                        act.wait_ge(sem("used"), plus(it * 24 + (6 * k + (10 if more1 else 6)), B["used"]))
                        act.copy(y, psum_all[:, 4:6, :]).then_inc(sem("y"), 1)
                    if first:
                        act.wait_ge(sem("pick_turned"), plus(e + 1, B["pick_turned"]))
                        act.copy(pickT, psum[7][:, 0:T]).then_inc(sem("pickT"), 1)

                if ahead or ph.more:
                    for q in range(AHEAD):
                        high(None, None, q)
                if ahead:
                    return
                tokens(0, 0)
                for q in range(AHEAD, 4):
                    high(None, None, q)
                if lead == 2:
                    tokens(1, 1)
                gate_up(0, 4)
                high(0, 0, 0)
                high(0, 0, 1)
                ph.run(act, step)

            def expert_layer(k):
                phases[k].passes(act, experts)
                act.wait_ge(S("slots"), k + 1)
                fills = act.value_load(fullest[0:1, 0:1])
                with act.If(fills > CAP):
                    extras[k].passes(act, experts)
                with act.Else():
                    extras[k].skip(act, "hi gu silu h_hi xe_hi pickT y")

            turn(W(L0["memT"], DC, T), DC, "memT"); v_jobs += 2
            for l in range(DEPTH):
                nat(mkv[:, l, 1, :], 256, "mkv", pack=True); v_jobs += 1
            turn(xT, DC, "xT"); v_jobs += 2
            gv, u = W(L0["gv"], TC, SGW), W(L0["u"], TC, SGW)
            nat(gv[:, :, 0:512], 512, "gv", ACT.Gelu)
            nat(gv[:, :, 512:SGW], 256, "gv", ACT.Gelu, pack=True); v_jobs += 1
            nat(u[:, :, 0:512], 512, "u", ACT.Gelu)
            nat(u[:, :, 512:SGW], 256, "u", ACT.Gelu, pack=True)
            v_jobs += 4
            v_jobs = plan(v_jobs, att["i"], 8)
            attention(2, 8, HD ** -0.5, W_P, W_PT)
            v_jobs += 3
            turn(xT, DC, "xT"); v_jobs += 2
            v_jobs += 4
            turn(xT, DC, "xT"); v_jobs += 2
            experts(phases[0], None, ahead=True)
            routed(1); v_jobs += 2
            expert_layer(0)
            turn(xT, DC, "xT"); v_jobs += 2
            qT, kT, v = W(L1["qT"], 6, T), W(L1["kT"], 6, T), W(L1["v"], TC, SGW)
            v_jobs += 5
            empty(qT[:, 4:6, :], "qkv")
            empty(W(L1["qmT"], 2, T), "qkv")
            nat(v[:, :, 0:512], 512, "qkv")
            nat(v[:, :, 512:SGW], 256, "qkv", pack=True)
            attention(6, 8, HD ** -0.5, W_P, W_PT, tables=True)
            v_jobs += 3 * 8
            v_jobs = plan(v_jobs, att["i"], 8)
            attention(2, 8, HD ** -0.5, W_P, W_PT)
            turn(xT, 4, "xT"); v_jobs += 1
            v_jobs += 4
            turn(xT, DC, "xT"); v_jobs += 2
            experts(phases[1], None, ahead=True)
            routed(2); v_jobs += 2
            expert_layer(1)
            squares = [0]

            def square(src, junk, n_norm):
                for c in range(TC):
                    act.activation(junk[:, c, :], src[:, c, :], ACT.Square, accum_out=var8[:, c:c + 1]).then_inc(S("var"), 1)

            act.wait_ge(S("norm"), NORM_AT["ln2_1"])
            square(x, W(XA["H"], TC, D), "mix")
            act.wait_ge(S("mem2_in"), 16)
            act.wait_ge(S("rstd"), 1 + NORM_ORDER.index("mix"))
            square(W(W_MEM2, TC, D), W(XA["memT"], TC, D), "mem")
            turn(xT, DC, "xT"); v_jobs += 2
            turn(W(XA["memT"], DC, T), DC, "memT"); v_jobs += 2
            nat(W(XA["mv"], TC, 512), 512, "xa"); v_jobs += 4
            v_jobs = plan(v_jobs, att["i"], 8)
            attention(2, 8, P ** -0.5, W_P2, W_PT2)

            def join(oT, k, gate_at):
                nonlocal v_jobs
                gate = W(gate_at, TC, D)
                for half in range(2):
                    nat(gate[:, :, half * 512:(half + 1) * 512], 512, "gate", ACT.Sigmoid)
                turn(oT, k, "oT")
                v_jobs += k // 4 + 4

            join(W(XA["oT"], 4, T), 4, XA["gate"])
            v_jobs += 2
            kT, v = W(NA["kT"], 4, T), W(NA["v"], TC, 512)
            empty(kT[:, 0:2, :], "na")
            empty(kT[:, 2:4, :], "na")
            nat(v, 512, "na")
            v_jobs = plan(v_jobs, att["i"], 16)
            attention(2, 16, 1.0, W_P2, W_PT2)
            join(W(NA["oT"], 4, T), 4, NA["gate"])
            act.wait_ge(S("dec_in"), 32)
            act.activation(lg[:, 0, :], dec[:], ACT.Abs).then_inc(S("dec_abs"), 1)
            act.wait_ge(S("dec_abs"), 1)
            act.activation(lg[:, 1, :], lg[:, 0, :], ACT.Exp, scale=-1.0).then_inc(S("dec_exp"), 1)
            Dm = W(RET["D"], RET_HEADS, TC * T)
            act.wait_ge(S("ret_e"), RET_HEADS)
            for h in range(RET_HEADS):
                act.activation(Dm[:, h, :], Dm[:, h, :], ACT.Exp).then_inc(S("ret_d"), 1)
            v, rg, y = W(RET["v"], TC, D), W(RET["rg"], TC, D), W(RET["y"], TC, D)
            for half in range(2):
                nat(v[:, :, half * 512:(half + 1) * 512], 512, "rv")
            for half in range(2):
                nat(rg[:, :, half * 512:(half + 1) * 512], 512, "rg", ACT.Silu)
            turn(W(RET["qT"], 4, T), 4, "rqk")
            turn(W(RET["kT"], 4, T), 4, "rqk")
            for h in range(RET_HEADS):
                empty(y[:, :, h * RET_V:(h + 1) * RET_V], "ret_y")
            join(W(RET["yT"], DC, T), DC, RET["gate"])
            turn(xT, DC, "xT")
            act.wait_ge(S("z_v"), 12)
            square(x, W(RET["y"], TC, D), "ffn")
            turn(xT, DC, "xT")
            experts(phases[2], None, ahead=True)
            routed(3)
            expert_layer(2)
            act.wait_ge(S("summed"), 1)
            square(W(MOE["acc"], TC, D), W(0, TC, D), "final")

        @block.vector
        def _(dve):
            took = [0]
            counted = {"dve_step": 0, "rstd": 0, "att": 0, "sc": 0}

            def bank():
                took[0] += 1
                dve.wait_ge(S("v_full"), took[0])
                return RB["v"][(took[0] - 1) % BANKS]

            def step(ins):
                counted["dve_step"] += 1
                ins.then_inc(S("dve_step"), 1)
                dve.wait_ge(S("dve_step"), counted["dve_step"])

            def steps(todo):
                for ins in todo:
                    counted["dve_step"] += 1
                    ins.then_inc(S("dve_step"), 1)
                dve.wait_ge(S("dve_step"), counted["dve_step"])

            def empty(dst, product, n=512):
                b = bank()
                src = b[:, 0:n]
                if len(dst.shape) == 3:
                    src = src.rearrange("p (a b) -> p a b", a=dst.shape[1])
                dve.tensor_copy(dst, src).then_inc(S(product + "_v"), 1)

            def turn(dst, tiles, product):
                for job in range(0, tiles // 2, 2):
                    t, j = divmod(job, tiles // 4)
                    empty(dst[:, 4 * j:4 * j + 4, t * P:(t + 1) * P], product)

            def turned(dst, tiles, product):
                for j in range(tiles // 2):
                    empty(dst[:, 2 * j:2 * j + 2, :], product)

            def wait_rstd():
                counted["rstd"] += 1
                dve.wait_ge(S("rstd"), counted["rstd"])

            def spread_of(n, cuts):
                steps(dve.bn_aggr(mv8[:, i, :], stats[:, i * cuts:(i + 1) * cuts, :]) for i in range(n))
                dve.tensor_copy(var8[:, 0:n], mv8[:, 0:n, 1]).then_inc(S("var"), 2)

            def moments(srcs, cuts):
                w = srcs[0].shape[-1] // cuts
                steps(dve.bn_stats(stats[:, n * cuts + c, :], src[:, c * w:(c + 1) * w]) for n, src in enumerate(srcs) for c in range(cuts))
                spread_of(len(srcs), cuts)

            def layer_norm(src, dst, width, slot, params, measured=False):
                if measured:
                    spread_of(TC, 2)
                else:
                    moments([src[:, c, :] for c in range(TC)], 2)
                g, b = prm[:, slot, 0, 0:width], prm[:, slot, 1, 0:width]
                dve.wait_ge(S(f"prm{slot}_in"), params)
                steps(dve.scalar_tensor_tensor(out=dst[:, c, :], in0=src[:, c, :], scalar=mv8[:, c, 0:1], in1=g,
                                               op0=ALU.subtract, op1=ALU.mult) for c in range(TC))
                wait_rstd()
                for c in range(TC):
                    dve.scalar_tensor_tensor(out=dst[:, c, :], in0=dst[:, c, :], scalar=rstd[:, c:c + 1], in1=b,
                                             op0=ALU.mult, op1=ALU.add).then_inc(S("norm"), 1)

            def rms_norm(src, dst, g):
                wait_rstd()
                for c in range(TC):
                    dve.scalar_tensor_tensor(out=dst[:, c, :], in0=src[:, c, :], scalar=rstd[:, c:c + 1], in1=g,
                                             op0=ALU.mult, op1=ALU.mult).then_inc(S("norm"), 1)

            def attention(nk, dv, n_tasks, scale, outs, p_at=None, t_slopes=None, dist=None):
                i0 = counted["att"]
                counted["att"] += n_tasks

                def peak(i):
                    I = i0 + i
                    if t_slopes is None:
                        src = bank()[:, 0:nk * P]
                    else:
                        h, t = divmod(i, TC)
                        sc = W(p_at, 2, nk * P)[:, i % 2, :]
                        if i >= 2:
                            dve.wait_ge(S("att_pT_a"), counted["pT0"] + 2 * (i - 1))
                        for g in range(3):
                            if g != 1:
                                b = bank()
                            dve.scalar_tensor_tensor(out=sc[:, g * T:(g + 1) * T], in0=dist[:, g, t, :], scalar=t_slopes(g, h),
                                                     in1=b[:, (g % 2) * T:(g % 2 + 1) * T],
                                                     op0=ALU.mult, op1=ALU.add).then_inc(S("att_sc"), 1)
                        counted["sc"] += 3
                        dve.wait_ge(S("att_sc"), counted["sc"])
                        src = sc
                    step(dve.tensor_reduce(att_mx[:, I:I + 1], src, AX.X, ALU.max))
                    dve.tensor_scalar(att_nm[:, I:I + 1], att_mx[:, I:I + 1], -scale, None, ALU.mult).then_inc(S("att_nm"), 1)

                def result(i):
                    I = i0 + i
                    b = bank()
                    step(dve.reciprocal(att_rec[:, I:I + 1], att_sum[:, I:I + 1]))
                    dve.tensor_scalar(outs(i // TC, i % TC), b[:, 0:dv], att_rec[:, I:I + 1], None, ALU.mult).then_inc(S("att_o"), 1)

                for i in range(n_tasks + 3):
                    if i < n_tasks:
                        peak(i)
                    if i >= 3:
                        result(i - 3)

            def residual(half, t):
                b = bank()
                xs = x[:, t, half * 512:(half + 1) * 512]
                return b, xs

            def rank4(v, r):
                step(dve.tensor_copy(r, rank0[:, 0:r.shape[1], :]))
                ge = rt[:, 15, 0:4 * r.shape[1]].rearrange("p (g e) -> p g e", e=4)
                for s in range(1, 4):
                    step(dve.tensor_tensor(ge[:, :, 0:4 - s], v[:, :, 0:4 - s], v[:, :, s:4], ALU.is_ge))
                    step(dve.tensor_tensor(r[:, :, s:4], r[:, :, s:4], ge[:, :, 0:4 - s], ALU.add))
                    step(dve.tensor_tensor(r[:, :, 0:4 - s], r[:, :, 0:4 - s], ge[:, :, 0:4 - s], ALU.subtract))

            def groups(ap, n=8):
                return ap.rearrange("p (g e) -> p g e", e=4)

            def spread(ap):
                return ap.unsqueeze(2).to_broadcast([P, 8, 4])

            selg = sel[:].rearrange("p c (g e) -> p (c g) e", e=4)

            def slots(k):
                b = bank()
                s2 = sel[:].rearrange("p c e -> p (c e)")
                step(dve.scalar_tensor_tensor(out=rt[:, 12, :], in0=b[:, 0:32], scalar=1.0, in1=s2, op0=ALU.add, op1=ALU.mult))
                r = rt[:, 12, :].rearrange("p (c e) -> p c e", c=TC)
                step(dve.tensor_reduce(fullest_f[:], b[:, 32:48], AX.X, ALU.max))
                steps([dve.tensor_scalar(slot_main[:], r, -1.0, None, ALU.add),
                       dve.tensor_scalar(slot_more[:], r, -1.0, None, ALU.add)])
                dve.tensor_copy(fullest[:], fullest_f[:]).then_inc(S("slots"), 1)
                dve.wait_ge(S("slots"), k)

            def route_1(k):
                b = bank()
                lgt, e, nm, sm = rt[:, 0, :], rt[:, 1, :], rsm[:, 0, 0:2], rsm[:, 1, 0:2]
                dve.tensor_copy(lgt, b[:, 0:32]).then_inc(S("logits_read"), 1)
                dve.wait_ge(S("logits_read"), k)
                step(dve.tensor_reduce(rsm[:, 2, 0:2], lgt.rearrange("p (c e) -> p c e", c=TC), AX.X, ALU.max))
                dve.tensor_scalar(nm, rsm[:, 2, 0:2], -1.0, None, ALU.mult).then_inc(S("logit_max"), 1)
                dve.wait_ge(S("logit_exp"), 2 * k)
                step(dve.reciprocal(rsm[:, 3, 0:2], sm))
                probs, score, r, two = rt[:, 2, :], rt[:, 3, :], groups(rt[:, 4, :]), rt[:, 5, :]
                steps(dve.tensor_scalar(probs[:, c * 16:(c + 1) * 16], e[:, c * 16:(c + 1) * 16], rsm[:, 3, c:c + 1], None, ALU.mult)
                      for c in range(TC))
                if k == 1:
                    dve.wait_ge(S("br_in"), 32)
                step(dve.tensor_tensor(score, probs, br[:].rearrange("p c e -> p (c e)"), ALU.add))
                rank4(groups(score), r)
                step(dve.tensor_scalar(groups(two), r, 2.0, None, ALU.is_lt))
                step(dve.tensor_tensor(rt[:, 6, :], score, two, ALU.mult))
                step(dve.tensor_reduce(rsm[:, 4, :], groups(rt[:, 6, :]), AX.X, ALU.add))
                rg = rsm[:, 5, :].rearrange("p (c g) -> p c g", c=TC)
                rank4(rsm[:, 4, :].rearrange("p (c g) -> p c g", c=TC), rg)
                step(dve.tensor_scalar(rsm[:, 6, :], rsm[:, 5, :], 1.0, None, ALU.is_lt))
                dve.tensor_tensor(selg, groups(two), spread(rsm[:, 6, :]), ALU.mult).then_inc(S("chosen"), 1)
                dve.wait_ge(S("chosen"), k)
                s2 = sel[:].rearrange("p c e -> p (c e)")
                step(dve.tensor_tensor(rt[:, 7, :], probs, s2, ALU.mult))
                step(dve.tensor_reduce(rsm[:, 7, 0:2], rt[:, 7, :].rearrange("p (c e) -> p c e", c=TC), AX.X, ALU.add))
                step(dve.reciprocal(rsm[:, 8, 0:2], rsm[:, 7, 0:2]))
                steps(dve.tensor_scalar(gates[:, c, :], rt[:, 7, c * 16:(c + 1) * 16], rsm[:, 8, c:c + 1], None, ALU.mult) for c in range(TC))
                slots(k)

            def route_2(k):
                b = bank()
                full = rt[:, 8:10, 0:20]
                dve.wait_ge(S("br2_in"), 64)
                dve.tensor_tensor(full, b[:, 0:40].rearrange("p (c e) -> p c e", c=TC), br2[:], ALU.add).then_inc(S("logits_read"), 1)
                dve.wait_ge(S("logits_read"), k)
                lgrp, lexp = full[:, :, 0:4], full[:, :, 4:20].rearrange("p c (g e) -> p c g e", e=4)
                steps([dve.tensor_reduce(rsm[:, 0, 0:2], lgrp, AX.X, ALU.max),
                       dve.tensor_reduce(rsm[:, 1, :].rearrange("p (c g) -> p c g", c=TC), lexp, AX.X, ALU.max)])
                todo = []
                for c in range(TC):
                    todo.append(dve.tensor_scalar(rsm[:, 2, 4 * c:4 * c + 4], lgrp[:, c, :], rsm[:, 0, c:c + 1], None, ALU.subtract))
                    todo.append(dve.tensor_tensor(groups(rt[:, 2, 16 * c:16 * c + 16]), lexp[:, c],
                                                  rsm[:, 1, 4 * c:4 * c + 4].unsqueeze(2).to_broadcast([P, 4, 4]), ALU.subtract))
                steps(todo)
                dve.sem_inc(S("logit_max"), 1)
                dve.wait_ge(S("logit_exp"), 6)
                e, r, two = rt[:, 3, :], groups(rt[:, 4, :]), rt[:, 5, :]
                rank4(groups(e), r)
                step(dve.tensor_scalar(groups(two), r, 2.0, None, ALU.is_lt))
                rg = rsm[:, 5, :].rearrange("p (c g) -> p c g", c=TC)
                rank4(rsm[:, 2, :].rearrange("p (c g) -> p c g", c=TC), rg)
                step(dve.tensor_scalar(rsm[:, 6, :], rsm[:, 5, :], 1.0, None, ALU.is_lt))
                dve.tensor_tensor(selg, groups(two), spread(rsm[:, 6, :]), ALU.mult).then_inc(S("chosen"), 1)
                dve.wait_ge(S("chosen"), k)
                s2 = sel[:].rearrange("p c e -> p (c e)")
                step(dve.tensor_tensor(rt[:, 7, :], e, s2, ALU.mult))
                steps([dve.tensor_reduce(rsm[:, 7, 0:2], rt[:, 7, :].rearrange("p (c e) -> p c e", c=TC), AX.X, ALU.add),
                       dve.tensor_reduce(rsm[:, 8, 0:2], rsm[:, 3, :].rearrange("p (c g) -> p c g", c=TC), AX.X, ALU.add)])
                steps([dve.reciprocal(rsm[:, 9, 0:2], rsm[:, 7, 0:2]), dve.reciprocal(rsm[:, 10, 0:2], rsm[:, 8, 0:2])])
                steps(dve.tensor_scalar(gates[:, c, :], rt[:, 7, c * 16:(c + 1) * 16], rsm[:, 9, c:c + 1], rsm[:, 10, c:c + 1],
                                        ALU.mult, ALU.mult) for c in range(TC))
                slots(k)

            def experts(ph, p, ahead=False):
                sem, B, lead = ph.sem, ph.base(p), ph.lead
                silu, h, y = W(MOE["silu"], 256), W(MOE["h"], 256), W(MOE["y"], D)
                pick, pickg, pickT = W(MOE["pick"], TC, CAP), W(MOE["pickg"], TC, P), W(MOE["pickT"], T)
                acc = W(MOE["acc"], TC, 2, 512)

                def column(of, c, e):
                    return of[:, c, e:e + 1] if isinstance(e, int) else of[:, c, bass.ds(e, 1)]

                def mark(e):
                    for c in range(TC):
                        dve.tensor_scalar(pick[:, c, :], iota[:, 0:CAP], column(ph.slots, c, e), None, ALU.is_equal).then_inc(sem("pick"), 1)

                def mark_gated(e):
                    for c in range(TC):
                        dve.tensor_scalar(pickg[:, c, :], iota, column(ph.slots, c, e), column(gates, c, e),
                                          ALU.is_equal, ALU.mult).then_inc(sem("pickg"), 1)

                def low(it, k, q):
                    if k is None:
                        r, sl = ph.slot(q), q % SPLIT
                        dve.wait_ge(sem("hi"), plus(q + 1, B["hi"]))
                    else:
                        r, sl = ph.slot(4 + q), (4 + q) % SPLIT
                        dve.wait_ge(sem("hi"), plus(it * 24 + (6 * k + 4 + q + 1), B["hi"]))
                    dve.tensor_tensor(w_lo[:, sl, :], raw[:, r, :], w_hi[:, sl, :].bitcast(F32), ALU.subtract).then_inc(sem("lo"), 1)

                def tokens(e, buf):
                    dve.wait_ge(sem("xe_hi"), plus(e + 1, B["xe_hi"]))
                    dve.tensor_tensor(xe[:, buf, :, CAP:], psum[7].rearrange("p (c s) -> p c s", c=DC),
                                      xe[:, buf, :, 0:CAP].bitcast(F32), ALU.subtract).then_inc(sem("xe_lo"), 1)

                def add(e, j):
                    dve.wait_ge(sem("scattered"), plus(e * 4 + (j + 1), B["scattered"]))
                    a_ = acc[:, j // 2, j % 2, :]
                    at_end = isinstance(e, int) and e == N_EXP
                    dve.tensor_tensor(a_, a_, psum[j] if at_end and j > 0 else psum[7], ALU.add).then_inc(sem("added"), 1)

                def step(it, k, more1, more2):
                    first, last = ph.first(k), ph.last(k)
                    e = ph.expert(it, k)
                    dve.wait_ge(sem("silu"), plus(it * 4 + (k + 1), B["silu"]))
                    dve.tensor_tensor(h, silu, psum[6][:, 256:512], ALU.mult).then_inc(sem("h"), 1)
                    if first:
                        mark_gated(e)
                        add(e, 0)
                    if more1:
                        low(it, k, 2)
                    if first:
                        add(e, 1)
                    dve.wait_ge(sem("h_hi"), plus(it * 4 + (k + 1), B["h_hi"]))
                    dve.tensor_tensor(hT[:, k % 2, :, CAP:], W(MOE["h"], 4, CAP), hT[:, k % 2, :, 0:CAP].bitcast(F32),
                                      ALU.subtract).then_inc(sem("h_lo"), 1)
                    if more1:
                        low(it, k, 3)
                    if first:
                        add(e, 2)
                    low(it, k, 4 if more1 else 0)
                    if first:
                        add(e, 3)
                    low(it, k, 5 if more1 else 1)
                    if more2:
                        low(it, k + 1, 0)
                    if first and ph.there_is(e + lead):
                        tokens(e + lead, ph.buffer(k + lead * ph.halves))
                        if ph.there_is(e + (lead + 1)):
                            mark(e + (lead + 1))
                    if more2:
                        low(it, k + 1, 1)

                if ahead or ph.more:
                    for q in range(AHEAD):
                        low(None, None, q)
                if ahead:
                    return

                if ph.more:
                    dve.tensor_scalar(slot_more[:], slot_more[:], -float(CAP), None, ALU.add).then_inc(sem("shift"), 1)
                    dve.wait_ge(sem("shift"), plus(1, B["shift"]))
                mark(0)
                dve.memset(y, 0.0).then_inc(sem("y"), 1)
                dve.memset(pickT, 0.0).then_inc(sem("pickT"), 1)
                tokens(0, 0)
                mark(1)
                for q in range(AHEAD, 4):
                    low(None, None, q)
                if lead == 2:
                    tokens(1, 1)
                    mark(2)
                low(0, 0, 0)
                low(0, 0, 1)
                ph.run(dve, step)
                for j in range(4):
                    add(N_EXP, j)
                dve.wait_ge(sem("added"), plus(4 * (N_EXP + 1), B["added"]))

            def expert_layer(k):
                phases[k].passes(dve, experts)
                fills = dve.value_load(fullest[0:1, 0:1])
                with dve.If(fills > CAP):
                    extras[k].passes(dve, experts)
                with dve.Else():
                    extras[k].skip(dve, "lo h h_lo pick xe_lo pickg added shift")

            turn(W(L0["memT"], DC, T), DC, "memT")
            for l in range(DEPTH):
                empty(mkv[:, l, 0, :], "mkv")
            turn(xT, DC, "xT")
            empty(W(L0["qmT"], 2 * T), "qm")
            swT, bsT = W(L0["swT"], N_SG * P), W(L0["bsT"], 16)
            for j in range(3):
                empty(swT[:, j * 512:(j + 1) * 512], "sw")
            empty(bsT[:, 0:N_SG], "sw", N_SG)
            dve.wait_ge(S("gv_a"), 3)
            gv = W(L0["gv"], TC, SGW)
            cat = W(L0["cat"], TC, D)
            attention(2, HD, 8, HD ** -0.5, lambda h, t: cat[:, t, SGW + h * HD:SGW + (h + 1) * HD])
            layer_norm(gv, gv, SGW, 0, 32)
            dve.wait_ge(S("u_a"), 3)
            dve.wait_ge(S("sw_v"), 4)
            u = W(L0["u"], TC, SGW)
            for j in range(3):
                b = bank()
                for g in range(4):
                    hh = 4 * j + g
                    c = slice(hh * HD, (hh + 1) * HD)
                    dve.scalar_tensor_tensor(out=cat[:, :, c], in0=b[:, g * P:(g + 1) * P].rearrange("p (c d) -> p c d", c=2),
                                             scalar=bsT[:, hh:hh + 1], in1=u[:, :, c], op0=ALU.add, op1=ALU.mult).then_inc(S("mix"), 1)
            turn(xT, DC, "xT")
            zs = [0]

            def add_residual(scale):
                for half in range(2):
                    for t in range(TC):
                        b, xs = residual(half, t)
                        if scale == 1.0:
                            ins = dve.tensor_tensor(xs, xs, b[:], ALU.add)
                        else:
                            ins = dve.scalar_tensor_tensor(out=xs, in0=xs, scalar=scale, in1=b[:], op0=ALU.mult, op1=ALU.add)
                        ins.then_inc(S("z_v"), 1)
                        zs[0] += 1
                        dve.wait_ge(S("z_v"), zs[0])
                        if scale != 1.0:
                            step(dve.bn_stats(stats[:, 2 * t + half, :], xs))

            acc = W(MOE["acc"], TC, D)

            def ahead_of_routing(k):
                if k < 2:
                    steps(dve.tensor_scalar(acc[:, c, :], x[:, c, :], ALPHA, None, ALU.mult) for c in range(TC))
                experts(phases[k], None, ahead=True)

            add_residual(ALPHA)
            layer_norm(x, x, D, 1, 32, measured=True)
            turn(xT, DC, "xT")
            ahead_of_routing(0)
            route_1(1)
            expert_layer(0)
            layer_norm(acc, x, D, 0, 64)
            turn(xT, DC, "xT")
            qT, kT = W(L1["qT"], 6, T), W(L1["kT"], 6, T)
            turned(qT[:, 0:4, :], 4, "qkv")
            turned(kT[:, 0:4, :], 4, "qkv")
            empty(kT[:, 4:6, :], "qkv")
            cat = W(L1["cat"], TC, 512)
            dve.wait_ge(S("dist_in"), 16)
            counted["pT0"] = counted["att"]
            attention(6, HD, 8, HD ** -0.5, lambda h, t: cat[:, t, h * HD:(h + 1) * HD], p_at=W_P,
                      t_slopes=lambda g, h: -SLOPES[g * DIL_HEADS + h] * HD ** 0.5, dist=W(L1["dist"], 3, TC * T)
                      .rearrange("p g (t k) -> p g t k", t=TC))
            attention(2, HD, 8, HD ** -0.5, lambda h, t: cat[:, t, 256 + h * HD:256 + (h + 1) * HD])
            turn(xT, 4, "xT")
            add_residual(ALPHA)
            layer_norm(x, x, D, 1, 64, measured=True)
            turn(xT, DC, "xT")
            ahead_of_routing(1)
            route_1(2)
            expert_layer(1)
            layer_norm(acc, x, D, 0, 96)
            dve.wait_ge(S("prm1_in"), 96)
            rms_norm(x, W(XA["H"], TC, D), prm[:, 1, 0, :])
            mem2 = W(W_MEM2, TC, D)
            turn(xT, DC, "xT")
            rms_norm(mem2, mem2, prm[:, 1, 1, :])
            turned(W(XA["qT"], 4, T), 4, "xa")
            turn(W(XA["memT"], DC, T), DC, "memT")
            turned(W(XA["mkT"], 4, T), 4, "xa")
            o = W(XA["o"], TC, 512)
            attention(2, P, 8, P ** -0.5, lambda h, t: o[:, t, h * P:(h + 1) * P])
            comb = W(W_COMB, TC, D)
            joins = [0]

            def join(oT, k, gate_at):
                turn(oT, k, "oT")
                gate = W(gate_at, TC, D)
                joins[0] += 1
                dve.wait_ge(S("gate_a"), 4 * joins[0])
                for half in range(2):
                    for t in range(TC):
                        cs = slice(half * 512, (half + 1) * 512)
                        b = bank()
                        if joins[0] == 1:
                            dve.tensor_tensor(comb[:, t, cs], b[:], gate[:, t, cs], ALU.mult).then_inc(S("joined_v"), 1)
                        else:
                            step(dve.tensor_tensor(gate[:, t, cs], b[:], gate[:, t, cs], ALU.mult))
                            dve.tensor_tensor(comb[:, t, cs], comb[:, t, cs], gate[:, t, cs], ALU.add).then_inc(S("joined_v"), 1)
                dve.wait_ge(S("joined_v"), 4 * joins[0])

            join(W(XA["oT"], 4, T), 4, XA["gate"])
            qT = W(NA["qT"], 4, T)
            for j in range(2):
                b = bank()
                dve.tensor_scalar(qT[:, 2 * j:2 * j + 2, :], b[:].rearrange("p (a b) -> p a b", a=2), HD ** -0.5, None, ALU.mult).then_inc(S("na_v"), 1)
            o = W(NA["o"], TC, 512)
            attention(2, HD, 16, 1.0, lambda h, t: o[:, t, h * HD:(h + 1) * HD])
            join(W(NA["oT"], 4, T), 4, NA["gate"])
            dve.wait_ge(S("dec_exp"), 1)
            z, s, s2, series, ls = lg[:, 1, :], lg[:, 2, :], lg[:, 3, :], lg[:, 4, :], lg[:, 5, :]
            step(dve.tensor_scalar(s2, z, 2.0, None, ALU.add))
            step(dve.reciprocal(series, s2))
            step(dve.tensor_tensor(s, z, series, ALU.mult))
            step(dve.tensor_tensor(s2, s, s, ALU.mult))
            step(dve.tensor_scalar(series, s2, 1.0 / 17, 1.0 / 15, ALU.mult, ALU.add))
            for k in range(13, 0, -2):
                step(dve.tensor_tensor(series, series, s2, ALU.mult))
                step(dve.tensor_scalar(series, series, 1.0 / k, None, ALU.add))
            step(dve.tensor_tensor(series, series, s, ALU.mult))
            step(dve.tensor_scalar(ls, dec[:], 0.0, None, ALU.min))
            step(dve.scalar_tensor_tensor(out=ls, in0=series, scalar=-2.0, in1=ls, op0=ALU.mult, op1=ALU.add))
            Dm = W(RET["D"], RET_HEADS, TC * T)
            AB = W(W_AB, 2, TC * T)
            dve.wait_ge(S("later_in"), 16)
            steps(dve.tensor_scalar(Dm[:, h, :], AB[:, 0, :], ls[:, h:h + 1], None, ALU.mult) for h in range(RET_HEADS))
            for h in range(RET_HEADS):
                dve.scalar_tensor_tensor(out=Dm[:, h, :], in0=AB[:, 1, :], scalar=ls[:, 4 + h:5 + h], in1=Dm[:, h, :],
                                         op0=ALU.mult, op1=ALU.add).then_inc(S("ret_e"), 1)
            rope = W(W_ROPE, 2, TC * 64)
            tmp = W(RET["tmp"], 4, RET_HEADS * 64)
            for name in "qk":
                dst = W(RET[name], TC, 512)
                for t in range(TC):
                    b = bank()[:].rearrange("p (h s d) -> p h s d", h=4, s=2)
                    cos, sin = (rope[:, f, t * 64:(t + 1) * 64].unsqueeze(1).to_broadcast([P, 4, 64]) for f in range(2))
                    ts = [tmp[:, n, :].rearrange("p (h d) -> p h d", h=4) for n in range(4)]
                    steps([dve.tensor_tensor(ts[0], b[:, :, 0, :], cos, ALU.mult), dve.tensor_tensor(ts[1], b[:, :, 1, :], sin, ALU.mult),
                           dve.tensor_tensor(ts[2], b[:, :, 0, :], sin, ALU.mult), dve.tensor_tensor(ts[3], b[:, :, 1, :], cos, ALU.mult)])
                    dd = dst[:, t, :].rearrange("p (h s d) -> p h s d", h=4, s=2)
                    step(dve.tensor_tensor(dd[:, :, 0, :], ts[0], ts[1], ALU.subtract))
                    dve.tensor_tensor(dd[:, :, 1, :], ts[2], ts[3], ALU.add).then_inc(S("rope_v"), 1)
                    counted["rope"] = counted.get("rope", 0) + 1
                    dve.wait_ge(S("rope_v"), counted["rope"])
            turn(W(RET["qT"], 4, T), 4, "rqk")
            turn(W(RET["kT"], 4, T), 4, "rqk")
            sd = W(RET["sd"], 2, TC * T)
            dve.wait_ge(S("ret_d"), RET_HEADS)
            for h in range(RET_HEADS):
                b = bank()
                if h >= 2:
                    dve.wait_ge(S("ret_y_a"), h - 1)
                dve.scalar_tensor_tensor(out=sd[:, h % 2, :], in0=b[:], scalar=RET_QK ** -0.5, in1=Dm[:, h, :],
                                         op0=ALU.mult, op1=ALU.mult).then_inc(S("ret_sd"), 1)
            y, rg = W(RET["y"], TC, D), W(RET["rg"], TC, D)
            dve.wait_ge(S("rg_a"), 4)
            dve.wait_ge(S("prm0_in"), 128)
            steps(dve.tensor_tensor(rg[:, t, :], rg[:, t, :], prm[:, 0, 0, :], ALU.mult) for t in range(TC))
            dve.wait_ge(S("ret_y_a"), RET_HEADS)
            cells = [(t, slice(h * RET_V, (h + 1) * RET_V)) for t in range(TC) for h in range(RET_HEADS)]
            moments([y[:, t, vs] for t, vs in cells], 1)
            steps(dve.scalar_tensor_tensor(out=y[:, t, vs], in0=y[:, t, vs], scalar=mv8[:, n, 0:1], in1=rg[:, t, vs],
                                           op0=ALU.subtract, op1=ALU.mult) for n, (t, vs) in enumerate(cells))
            wait_rstd()
            for n, (t, vs) in enumerate(cells):
                ins = dve.tensor_scalar(y[:, t, vs], y[:, t, vs], rstd[:, n:n + 1], None, ALU.mult)
                ins.then_inc(S("norm" if n % RET_HEADS == RET_HEADS - 1 else "dve_step"), 1)
                if n % RET_HEADS < RET_HEADS - 1:
                    counted["dve_step"] += 1
            join(W(RET["yT"], DC, T), DC, RET["gate"])
            turn(xT, DC, "xT")
            add_residual(1.0)
            steps(dve.tensor_copy(acc[:, c, :], x[:, c, :]) for c in range(TC))
            rms_norm(acc, x, prm[:, 0, 1, :])
            turn(xT, DC, "xT")
            ahead_of_routing(2)
            route_2(3)
            expert_layer(2)
            dve.sem_inc(S("summed"), 1)
            dve.wait_ge(S("prm1_in"), 112)
            rms_norm(acc, x, prm[:, 1, 0, :])

        @block.gpsimd
        def _(pool):
            def bc(v):
                return v.partition_broadcast(P)

            pool.dma_start(wr[:], a["w_router"].rearrange("(c p) n -> p c n", p=P)).then_inc(S("wr_in"), 16)
            pool.dma_start(W(L0["bsN"], P)[0:N_SG, :], a["sg_b"][0]).then_inc(S("sgb_in"), 16)
            loads = [
                [(0, SGW, a["sg_ln_g"][0]), (1, SGW, a["sg_ln_b"][0])],
                [(0, D, a["ln1_g"][0]), (1, D, a["ln1_b"][0])],
                [(0, D, a["ln2_g"][0]), (1, D, a["ln2_b"][0])],
                [(0, D, a["ln1_g"][1]), (1, D, a["ln1_b"][1])],
                [(0, D, a["ln2_g"][1]), (1, D, a["ln2_b"][1])],
                [(0, D, a["g_mix_2"][0]), (1, D, a["g_mem_2"][0])],
                [(0, D, a["ret_norm_gain_2"][0]), (1, D, a["g_ffn_2"][0])],
                [(0, D, a["g_final_2"])],
            ]
            last_use = ["gv", "ln1_0", "ln2_0", "ln1_1", "ln2_1", "mem"]

            def load(k):
                if k >= 2:
                    pool.wait_ge(S("norm"), NORM_AT[last_use[k - 2]])
                for which, width, src in loads[k]:
                    pool.dma_start(prm[:, k % 2, which, 0:width], bc(src)).then_inc(S(f"prm{k % 2}_in"), 16)

            load(0)
            load(1)
            for c in range(TC):
                pool.dma_start(br[:, c, :], bc(a["b_router"])).then_inc(S("br_in"), 16)
                pool.dma_start(br2[:, c, 0:4], bc(a["b_router_group_2"][0])).then_inc(S("br2_in"), 16)
                pool.dma_start(br2[:, c, 4:20], bc(a["b_router_expert_2"][0])).then_inc(S("br2_in"), 16)
            pool.dma_start(wr2[:, :, 0:4], a["w_router_group_2"][0].rearrange("(c p) n -> p c n", p=P)).then_inc(S("wr2_in"), 16)
            pool.dma_start(wr2[:, :, 4:20], a["w_router_expert_2"][0].rearrange("(c p) n -> p c n", p=P)).then_inc(S("wr2_in"), 16)
            pool.dma_start(dec[:, 0:4], bc(a["ret_decay_fwd_2"][0])).then_inc(S("dec_in"), 16)
            pool.dma_start(dec[:, 4:8], bc(a["ret_decay_bwd_2"][0])).then_inc(S("dec_in"), 16)
            pool.dma_start(W(W_AB, W_N - W_AB), a["later"]).then_inc(S("later_in"), 16)
            pool.wait_ge(S("sgw_in"), 16)
            pool.wait_ge(S("sgb_in"), 16)
            sgw = W(L0["sgw"], N_SG, P)
            pool.affine_select(out=sgw, in_=sgw, compare_op=ALU.is_ge, fill=0.0, base=0,
                               pattern=[[0, N_SG], [-1, P]], channel_multiplier=1).then_inc(S("sg_causal"), 1)
            pool.wait_ge(S("con_in"), 16)
            done = [0]

            def root(n, eps, scale=None):
                done[0] += 1
                pool.wait_ge(S("var"), 2 * done[0])
                if scale is None:
                    pool.tensor_scalar(var8[:, 0:n], var8[:, 0:n], eps, None, ALU.add).then_inc(S("var_eps"), 1)
                else:
                    pool.tensor_scalar(var8[:, 0:n], var8[:, 0:n], scale, eps, ALU.mult, ALU.add).then_inc(S("var_eps"), 1)
                pool.wait_ge(S("var_eps"), done[0])
                if done[0] >= 2:
                    pool.wait_ge(S("norm"), 2 * (done[0] - 1))
                pool.tensor_tensor(rstd[:, 0:n], var8[:, 0:n], mhalf[:, 0:n], ALU.pow).then_inc(S("rstd"), 1)

            root(2, LN_EPS)
            root(2, LN_EPS)
            pool.wait_ge(S("norm"), NORM_AT["ln1_0"])
            pool.dma_start(W(L1["dist"], 3 * TC * T), a["dist"]).then_inc(S("dist_in"), 16)
            load(2)
            load(3)
            root(2, LN_EPS)
            root(2, LN_EPS)
            pool.wait_ge(S("norm"), NORM_AT["ln1_1"])
            pool.dma_start(W(W_MEM2, TC, D), a["mem_2"][0].rearrange("(c p) n -> p c n", p=P)).then_inc(S("mem2_in"), 16)
            rpb = a["na_rpb_2"]
            n_r, n_c = 2 * NA_ROWS - 1, 2 * NA_COLS - 1
            table = W(W_TAB, NA_HEADS, 6, GRID_W)
            for r in range(2):
                for h in range(NA_HEADS):
                    src = bass.AP(rpb.tensor, (h * n_r + 5 - r) * n_c + NA_COLS - 1 - (GRID_W - 1),
                                  [[1, GRID_W], [n_c, 6], [1, GRID_W]])
                    pool.dma_start(table[r * GRID_W:(r + 1) * GRID_W, h], src).then_inc(S("rpb_in"), 16)
            load(4)
            load(5)
            pool.wait_ge(S("rpb_in"), 16 * 2 * NA_HEADS)
            flat = W(W_TAB, NA_HEADS * 6, GRID_W)
            pool.tensor_tensor(flat, flat, namask.unsqueeze(1).to_broadcast([P, NA_HEADS * 6, GRID_W]), ALU.add).then_inc(S("na_table"), 1)
            root(2, LN_EPS)
            root(2, RMS_EPS, 1.0 / D)
            load(6)
            root(2, RMS_EPS, 1.0 / D)
            load(7)
            root(8, GN_EPS)
            root(2, RMS_EPS, 1.0 / D)
            root(2, RMS_EPS, 1.0 / D)

        @block.sync
        def _(sp):
            sp.dma_start(con[:], a["const"]).then_inc(S("con_in"), 16)
            sp.dma_start(W(L0["memN"], TC, D), a["mem"][0].rearrange("(c p) n -> p c n", p=P)).then_inc(S("mem_in"), 16)

            def fill(n, parts):
                if n >= RING:
                    sp.wait_ge(*freed[n - RING])
                for at, src in parts:
                    dst = ring[:, n % RING, at:at + src.shape[1] * src.shape[2]].rearrange("p (c n) -> p c n", c=src.shape[1])
                    sp.dma_start(dst, src).then_inc(S(f"slot{n % RING}"), 16)

            def piece(ph, it, k, q):
                which, part = divmod(q, 2)
                e, half = ph.expert(it, k), (k % 2 if ph.halves == 2 else 0)
                if which < 2:
                    w = (ph.wg, ph.wu)[which]
                    return w[e, part * 512:(part + 1) * 512, half * 512:(half + 1) * 512].rearrange("(c p) n -> p c n", p=P)
                return ph.wd[e, half * 512 + part * 256:half * 512 + (part + 1) * 256, :].rearrange("(c p) n -> p c n", p=P)

            def load(ph, slot, src):
                dst = raw[:, slot, :].rearrange("p (c n) -> p c n", c=src.shape[1])
                sp.dma_start(dst, src).then_inc(ph.sem("piece%d" % slot), 16)

            def expert_stream(ph, p):
                B = ph.base(p)

                def room(idx, it, c):
                    if idx is not None and idx < RAW:
                        if not ph.more and ph.n0 + idx // 2 >= RING:
                            sp.wait_ge(*freed[ph.n0 + idx // 2 - RING])
                    else:
                        sp.wait_ge(ph.sem("lo"), plus(it * 24 + c, B["lo"]))

                def unit(it, k, more1):
                    todo = [(k + 1, 0), (k + 1, 1), (k + 1, 2), (k + 1, 3), (k, 4), (k, 5)] if more1 else [(k, 4), (k, 5)]
                    for q, (kk, what) in enumerate(todo):
                        idx = it * 24 + 6 * k + 4 + q if isinstance(it, int) else None
                        src = piece(ph, it, kk, what)
                        room(idx, it, 6 * k + 4 + q - RAW + 1)
                        if idx is None:
                            sp.sem_inc(S("ring_turns"), 1)
                        load(ph, ph.slot(4 + q), src)

                for q in range(4):
                    room(q, 0, 0)
                    load(ph, ph.slot(q), piece(ph, 0, 0, q))
                for k in range(4):
                    unit(0, k, True)
                with sp.Fori(1, ph.iters - 1) as it:
                    for k in range(4):
                        unit(it, k, True)
                for k in range(4):
                    unit(ph.iters - 1, k, k < 3)
                if ph.more:
                    sp.wait_ge(ph.sem("lo"), plus(ph.per["lo"], B["lo"]))
                    sp.sem_inc(ph.sem("loaded"), 1)

            for k, (s0, stream) in enumerate(zip(starts, (stream_0, stream_1, stream_2))):
                for m, parts in enumerate(stream):
                    fill(s0 + m, parts)
                    if k == 0 and m == 1:
                        sp.dma_start(x[:], a["x"][0].rearrange("(c p) n -> p c n", p=P)).then_inc(S("x_in"), 16)
                        sp.dma_start(W(L0["sgw"], N_SG, P), a["sg_w"][0].rearrange("g p q -> p g q")).then_inc(S("sgw_in"), 16)
                ph, more = phases[k], extras[k]
                ph.passes(sp, expert_stream)
                sp.wait_ge(S("slots"), k + 1)
                fills = sp.value_load(fullest[0:1, 0:1])
                with sp.If(fills > CAP):
                    sp.wait_ge(ph.sem("lo"), ph.before["lo"] + ph.per["lo"])
                    more.passes(sp, expert_stream)
                with sp.Else():
                    for m in range(RAW):
                        sp.sem_inc(more.sem(f"piece{m}"), MORE * more.per["piece"])
            for c in range(TC):
                sp.wait_ge(S("norm"), NORM_AT["final"] - TC + 1 + c)
                sp.dma_start(out[0, c * P:(c + 1) * P, :], x[:, c, :]).then_inc(S("stored"), 16)
            sp.wait_ge(S("stored"), 16 * TC)


_INS = ["x", "mem", "w_in_a", "w_out_a", "sg_ln_g", "sg_ln_b", "sg_w", "sg_b", "w_in_b", "w_out_b", "w_k_shared",
        "w_v_shared", "w_mem_k", "w_mem_v", "ln1_g", "ln1_b", "ln2_g", "ln2_b", "w_router", "b_router", "w_gate", "w_up",
        "w_down", "mem_2", "g_mix_2", "w_in_2", "ret_decay_fwd_2", "ret_decay_bwd_2", "ret_norm_gain_2",
        "w_ret_o_2", "na_rpb_2", "w_na_o_2", "g_mem_2", "w_mem_kv_2", "w_xa_o_2", "w_out_2", "g_ffn_2",
        "w_router_group_2", "b_router_group_2", "w_router_expert_2", "b_router_expert_2", "w_exp_gate_2",
        "w_exp_up_2", "w_exp_down_2", "g_final_2"]


def kernel(**inputs):
    import concourse.bacc as _bacc
    from concourse.bass_utils import run_bass_kernel_spmd as _run

    nc = _bacc.Bacc("TRN2", target_bir_lowering=False, num_devices=1)
    arrays, args = {}, {}
    for name, value in [(n, inputs[n]) for n in _INS] + list(constants().items()):
        v = np.ascontiguousarray(value)
        arrays[f"in_{name}_dram"] = v
        args[name] = nc.dram_tensor(f"in_{name}_dram", v.shape, mybir.dt.from_np(v.dtype), kind="ExternalInput").ap()
    out = nc.dram_tensor("out_0_dram", (1, T, D), F32, kind="ExternalOutput").ap()
    build(nc, args, out)
    r = _run(nc, [arrays], core_ids=[0])
    return r.results[0]["out_0_dram"]
```

```python
import numpy as np

import concourse.bass as bass
from concourse import mybir
from concourse.alu_op_type import AluOpType as ALU

F32 = mybir.dt.float32
F32R = mybir.dt.float32r
I32 = mybir.dt.int32
ACT = mybir.ActivationFunctionType
AX = mybir.AxisListType

P = 128
T, D = 256, 1024
TC, DC = T // P, D // P
DEPTH = 2
ALPHA = (2 * DEPTH) ** 0.25
LN_EPS, GN_EPS, RMS_EPS = 1e-5, 1e-5, 1e-6
HD = 64
N_SG, SGW = 12, 768
MEM_HEADS = 4
DILS = (1, 4, 16)
STEPS = 128
DIL_HEADS = 4
N_EXP = 16
RET_HEADS, RET_QK, RET_V = 4, 128, 256
NA_HEADS, NA_ROWS, NA_COLS, GRID_W = 8, 8, 16, 64
XA_HEADS = 4
BIG = 1e30

RING = 3
CHUNK = 4096
PIECE = CHUNK // 2
RAW = 2 * RING
SPLIT = 3
CAP = P // 2
MORE = T // CAP - 1
AHEAD = 2
BANKS = 4

C_IDENT, C_FLIP, C_BEFORE, C_ONES, C_IOTA = 0, 128, 256, 384, 512
C_EARLIER, C_NAMASK, C_MHALF, C_STACK = 640, 656, 720, 728
C_N = 792


def constants():
    c = np.zeros((P, C_N), np.float32)
    c[:, C_IDENT:C_IDENT + P] = np.eye(P)
    flip = np.zeros((P, P))
    for r in range(2):
        for x in range(GRID_W):
            flip[r * GRID_W + x, r * GRID_W + GRID_W - 1 - x] = 1
    c[:, C_FLIP:C_FLIP + P] = flip
    c[:, C_BEFORE:C_BEFORE + P] = np.triu(np.ones((P, P)), 1)
    c[:, C_ONES:C_ONES + P] = 1
    c[:, C_IOTA:C_IOTA + P] = np.arange(P)[None] % CAP
    c[:, C_STACK:C_STACK + CAP] = np.arange(P)[:, None] % CAP == np.arange(CAP)[None]
    c[:, C_EARLIER:C_EARLIER + 16] = np.tril(np.ones((4, 4)), -1).reshape(1, 16)
    col = GRID_W - 1 - np.arange(P) % GRID_W
    start = np.clip(col - NA_COLS // 2, 0, GRID_W - NA_COLS)
    off = np.arange(GRID_W)[None] - start[:, None]
    c[:, C_NAMASK:C_NAMASK + GRID_W] = np.where((off >= 0) & (off < NA_COLS), 0, -BIG)
    c[:, C_MHALF:C_MHALF + 8] = -0.5
    i = np.arange(T)[:, None]
    j = np.arange(T)[None]
    rel = np.stack([np.where((j <= i) & ((i - j) % d == 0) & ((i - j) // d <= STEPS), i - j, BIG) for d in DILS])
    dist = rel.reshape(3, TC, P, T).transpose(2, 0, 1, 3).reshape(P, 3 * TC * T)
    fwd = np.maximum(j - i, 0).reshape(TC, P, T).transpose(1, 0, 2).reshape(P, TC * T)
    bwd = np.maximum(i - j, 0).reshape(TC, P, T).transpose(1, 0, 2).reshape(P, TC * T)
    half = RET_QK // 2
    inv = np.float32(10000.0) ** (-np.arange(half, dtype=np.float32) / np.float32(half))
    ang = np.arange(T, dtype=np.float32)[:, None] * inv[None].astype(np.float32)
    rope = [f(ang).reshape(TC, P, half).transpose(1, 0, 2).reshape(P, TC * half) for f in (np.cos, np.sin)]
    return {
        "const": c,
        "dist": np.ascontiguousarray(dist.astype(np.float32)),
        "later": np.ascontiguousarray(np.concatenate([fwd, bwd] + rope, 1).astype(np.float32)),
    }


SLOPES = [float(np.float32(2.0) ** np.float32(-8.0 * k / 12)) for k in range(1, 13)]

W_N = 15616
L0 = dict(memN=0, cat=0, memT=2048, sgw=4096, swT=5632, bsN=7168, bsT=7296, u=7424, gv=8960, qmT=10496)
W_P, W_PT = 11008, 12544
L1 = dict(dist=8192, qT=1536, kT=3072, v=4608, qmT=6144, cat=6656)
W_MEM2, W_MEMT2, W_MK2 = 0, 11264, 13312
W_TAB = 8192
W_P2, W_PT2, W_COMB = 11264, 11776, 12288
XA = dict(H=0, mv=2048, p=4096, pT=4608, qT=6144, o=7168, oT=0, gate=2048)
NA = dict(qT=4096, kT=5120, v=6144, o=7168, oT=0, gate=2048)
RET = dict(q=0, k=1024, qT=2048, kT=3072, v=4096, rg=6144, D=8192, sd=10240, tmp=11264, y=0, yT=4096, gate=2048)
W_AB, W_ROPE = 14336, 15360
W_RANK = 6912
MOE = dict(hT=0, g=1024, u=1536, silu=2048, h=2304, y=2560, pickg=3712, pickT=3968, acc=4224, pick=6656)

NORM_ORDER = ["gv", "ln1_0", "ln2_0", "mem", "ln1_1", "ln2_1", "mix", "gn", "ffn", "final"]
NORM_AT = {name: 2 * (n + 1) for n, name in enumerate(NORM_ORDER)}


def build(nc, a, out):
    from contextlib import ExitStack
    with ExitStack() as ctx:
        def sb(name, shape, dt=F32):
            return ctx.enter_context(nc.sbuf_tensor(name, shape, dt))

        ring = sb("ring", [P, RING, CHUNK])
        raw = ring[:].rearrange("p r (h n) -> p (r h) n", h=2)
        w_hi_at = nc.sbuf_base
        w_hi = sb("w_hi", [P, SPLIT, PIECE], F32R)
        w_lo_at = nc.sbuf_base
        w_lo = sb("w_lo", [P, SPLIT, PIECE], F32R)
        late = [nc.alloc_sbuf_tensor_at(name, [P, DC, 256], F32, offset=at + 4 * AHEAD * PIECE)
                for name, at in (("late_0", w_hi_at), ("late_1", w_lo_at))]
        x = sb("x", [P, TC, D])
        xT_at = nc.sbuf_base
        xT = sb("xT", [P, DC, T])
        xe = nc.alloc_sbuf_tensor_at("xe", [P, 2, DC, P], F32R, offset=xT_at)
        mkv = sb("mkv", [P, DEPTH, 2, 512])
        prm = sb("prm", [P, 2, 2, D])
        con = sb("con", [P, C_N])
        work_at = nc.sbuf_base
        work = sb("work", [P, W_N])
        hT = nc.alloc_sbuf_tensor_at("hT", [P, 2, 4, P], F32R, offset=work_at + 4 * MOE["hT"])
        wr = sb("wr", [P, DC, 16])
        wr2 = sb("wr2", [P, DC, 20])
        br = sb("br", [P, TC, 16])
        br2 = sb("br2", [P, TC, 20])
        dec = sb("dec", [P, 8])
        stats = sb("stats", [P, 8, 6])
        mv8 = sb("mv8", [P, 8, 2])
        var8 = sb("var8", [P, 8])
        rstd = sb("rstd", [P, 8])
        att_mx = sb("att_mx", [P, 64])
        att_nm = sb("att_nm", [P, 64])
        att_sum = sb("att_sum", [P, 64])
        att_rec = sb("att_rec", [P, 64])
        rt = sb("rt", [P, 13, 32])
        rsm = sb("rsm", [P, 16, 8])
        sel = sb("sel", [P, TC, N_EXP])
        gates = sb("gates", [P, TC, N_EXP])
        slot_main = sb("slot_main", [P, TC, N_EXP])
        slot_more = sb("slot_more", [P, TC, N_EXP])
        fullest = sb("fullest", [P, 1], I32)
        fullest_f = sb("fullest_f", [P, 1])
        lg = sb("lg", [P, 10, 8])

        psum_all = ctx.enter_context(nc.psum_tensor("psum", [P, 8, 512], F32))
        psum = [psum_all[:, i, :] for i in range(8)]
        RB = {"v": psum[0:4], "a": psum[4:8]}

        sems = {}

        def S(name):
            if name not in sems:
                sems[name] = ctx.enter_context(nc.semaphore(name))
            return sems[name]

        def W(at, *shape):
            n = int(np.prod(shape))
            ap = work[:, at:at + n]
            if len(shape) == 1:
                return ap
            names = "abc"[:len(shape)]
            return ap.rearrange(f"p ({' '.join(names)}) -> p {' '.join(names)}", **dict(zip(names, shape)))

        ident = con[:, C_IDENT:C_IDENT + P]
        flip = con[:, C_FLIP:C_FLIP + P]
        before = con[:, C_BEFORE:C_BEFORE + P]
        ones = con[:, C_ONES:C_ONES + P]
        iota = con[:, C_IOTA:C_IOTA + P]
        stack = con[:, C_STACK:C_STACK + CAP]
        earlier = con[:, C_EARLIER:C_EARLIER + 16].rearrange("p (i j) -> p i j", j=4)
        namask = con[:, C_NAMASK:C_NAMASK + GRID_W]
        mhalf = con[:, C_MHALF:C_MHALF + 8]

        block = ctx.enter_context(nc.Block())

        def cols(w, c0, n):
            return w[:, c0:c0 + n].rearrange("(c p) n -> p c n", p=P)

        def rows(w, r0, n):
            return w[r0:r0 + n, :].rearrange("(c p) n -> p c n", p=P)

        w_in_a, w_out_a = a["w_in_a"][0], a["w_out_a"][0]
        w_in_b, w_out_b = a["w_in_b"][0], a["w_out_b"][0]
        w2 = a["w_in_2"][0]
        stream_0 = [[(0, cols(a["w_mem_k"][0], 0, 256)), (2048, cols(a["w_mem_v"][0], 0, 256))], [(0, cols(w_in_a, SGW, 512))], [(0, cols(w_in_a, SGW + 512, 512))],
                     [(0, cols(w_in_a, 0, 512))], [(0, cols(w_in_a, 512, 256))],
                     [(0, cols(w_out_a, 0, 512))], [(0, cols(w_out_a, 512, 512))]]
        late_weights = [[cols(a["w_mem_k"][1], 0, 256), cols(a["w_mem_v"][1], 0, 256)],
                        [cols(a["w_mem_kv_2"][0], 0, 256), cols(a["w_mem_kv_2"][0], 256, 256)]]
        stream_1 = [[(0, cols(w_in_b, 0, 512))], [(0, cols(w_in_b, 512, 512))],
                    [(0, cols(a["w_k_shared"], 0, 512))], [(0, cols(a["w_v_shared"], 0, 512))],
                    [(0, cols(a["w_k_shared"], 512, 256)), (2048, cols(a["w_v_shared"], 512, 256))],
                    [(0, rows(w_out_b, 0, 512))]]
        O_RQ, O_RK, O_RV, O_RG, O_NQ, O_NK, O_NV, O_XQ, O_G = 0, 512, 1024, 2048, 3072, 3584, 4096, 4608, 5120
        stream_2 = [[(0, cols(a["w_mem_kv_2"][0], 512, 512))], [(0, cols(w2, O_XQ, 512))],
                    [(0, cols(w2, O_G + 2048, 512))], [(0, cols(w2, O_G + 2560, 512))],
                    [(0, rows(a["w_xa_o_2"][0], 0, 512))],
                    [(0, cols(w2, O_NQ, 512))], [(0, cols(w2, O_NK, 512))], [(0, cols(w2, O_NV, 512))],
                    [(0, cols(w2, O_G + 1024, 512))], [(0, cols(w2, O_G + 1536, 512))],
                    [(0, rows(a["w_na_o_2"][0], 0, 512))],
                    [(0, cols(w2, O_RQ, 512))], [(0, cols(w2, O_RK, 512))],
                    [(0, cols(w2, O_RV, 512))], [(0, cols(w2, O_RV + 512, 512))],
                    [(0, cols(w2, O_RG, 512))], [(0, cols(w2, O_RG + 512, 512))],
                    [(0, cols(w2, O_G, 512))], [(0, cols(w2, O_G + 512, 512))],
                    [(0, cols(a["w_ret_o_2"][0], 0, 512))], [(0, cols(a["w_ret_o_2"][0], 512, 512))],
                    [(0, cols(a["w_out_2"][0], 0, 512))], [(0, cols(a["w_out_2"][0], 512, 512))]]

        def key_tiles(nk, i, causal):
            return nk // TC if causal and i % TC == 0 else nk

        def plus(a, b):
            return a + b if not isinstance(a, int) else b + a

        class Pass:
            def __init__(self, wg, wu, wd, halves, n0, slots, before, more):
                self.wg, self.wu, self.wd, self.halves, self.n0 = wg, wu, wd, halves, n0
                self.slots, self.more = slots, more
                self.units = N_EXP * halves
                self.iters = self.units // 4
                self.group = 2 // halves
                self.gathers = N_EXP // self.group
                U, E, G = self.units, N_EXP, self.gathers
                self.per = dict(hi=6 * U, lo=6 * U, used=6 * U, gu=2 * U, t_full=U, silu=U, h=U, h_hi=U, h_lo=U,
                                pick=2 * E, gathered=G, xe_hi=G, xe_lo=G, pickg=2 * E, pick_turned=E,
                                pickT=E + 1, y=E + 1, scattered=4 * (E + 1), added=4 * (E + 1), shift=1, piece=16 * U)
                times = MORE if more else 1
                self.before = {k: sum(o.per[k] for o in before) * times for k in self.per}

            def sem(self, name):
                return S(("more_" if self.more else "moe_") + name)

            def base(self, p):
                return {k: self.before[k] if p is None else p * self.per[k] + self.before[k] for k in self.per}

            def skip(self, eng, names):
                for name in names.split():
                    eng.sem_inc(self.sem(name), MORE * self.per[name])

            def expert(self, it, k):
                return it * 2 + k // 2 if self.halves == 2 else it * 4 + k

            def next_gather(self, it, k):
                return it * 2 + (k // 2 + 1)

            def there_is(self, g):
                return not isinstance(g, int) or g < self.gathers

            def gathered(self, g):
                n = self.group
                return psum_all[:, 8 - n:8, :].rearrange("p b n -> p (b n)").rearrange("p (c g s) -> p g c s", c=DC, g=n)

            def tokens_of(self, g):
                return xe[:] if self.group == 2 else xe[:, g % 2:g % 2 + 1]

            def first(self, k):
                return self.halves == 1 or k % 2 == 0

            def last(self, k):
                return self.halves == 1 or k % 2 == 1

            def buffer(self, k):
                return (k // 2 if self.halves == 2 else k) % 2

            def slot(self, idx):
                return (2 * self.n0 + idx) % RAW

            def landed(self, eng, it, k, q, B):
                if k is None:
                    eng.wait_ge(self.sem("piece%d" % self.slot(q)), plus(16, B["piece"]))
                else:
                    eng.wait_ge(self.sem("piece%d" % self.slot(4 + q)), plus(it * 64 + 16 * (k + (4 + q) // 6 + 1), B["piece"]))

            def run(self, eng, step):
                with eng.Fori(0, self.iters - 1) as it:
                    for k in range(4):
                        step(it, k, True)
                for k in range(4):
                    step(self.iters - 1, k, k < 3)

            def passes(self, eng, one):
                if not self.more:
                    one(self, None)
                else:
                    with eng.Fori(0, MORE) as p:
                        one(self, p)

        phases, extras = [], []
        n_at = 0
        starts = []
        for tag, stream, halves in (("0", stream_0, 2), ("1", stream_1, 2), ("2", stream_2, 1)):
            starts.append(n_at)
            n_at += len(stream)
            if halves == 2:
                wg, wu, wd = (a[k][int(tag)] for k in ("w_gate", "w_up", "w_down"))
            else:
                wg, wu, wd = (a[k][0].rearrange("g e r c -> (g e) r c") for k in ("w_exp_gate_2", "w_exp_up_2", "w_exp_down_2"))
            ph = Pass(wg, wu, wd, halves, n_at, slot_main, phases, False)
            extras.append(Pass(wg, wu, wd, halves, 0, slot_more, extras, True))
            phases.append(ph)
            n_at += 3 * ph.units

        landed, count = {}, [0] * RING

        def note(n, parts):
            count[n % RING] += 16 * parts
            landed[n] = count[n % RING]

        for s0, stream in zip(starts, (stream_0, stream_1, stream_2)):
            for k, parts in enumerate(stream):
                note(s0 + k, len(parts) if s0 + k > 0 else 0)

        freed = {}

        @block.tensor
        def _(pe):
            taken = {"v": 0, "a": 0}
            emptied = {"v": [], "a": []}
            made = {}

            def bank(r, product=None, by=None):
                j = taken[r]
                taken[r] += 1
                if j >= BANKS:
                    pe.wait_ge(*emptied[r][j - BANKS])
                if by is None:
                    key = product + "_" + r
                    made[key] = made.get(key, 0) + 1
                    by = (S(key), made[key])
                emptied[r].append(by)
                return RB[r][j % BANKS]

            def full(r, ins):
                ins.then_inc(S(r + "_full"), 1)
                return (S(r + "_full"), taken[r])

            def wait_made(product):
                for r in "va":
                    if product + "_" + r in made:
                        pe.wait_ge(S(product + "_" + r), made[product + "_" + r])

            def chunk(n):
                pe.wait_ge(S(f"slot{n % RING}"), landed[n])
                return ring[:, n % RING, :]

            def turn(src, tiles, product, norm=None, rings="va", loaded=None):
                for t in range(TC):
                    if loaded is not None:
                        pe.wait_ge(S(loaded[t]), 16)
                    if norm is not None:
                        pe.wait_ge(S("norm"), NORM_AT[norm] - TC + 1 + t)
                    for j in range(tiles // 4):
                        r = rings[(t * (tiles // 4) + j) % len(rings)]
                        b = bank(r, product)
                        for c in range(4):
                            ins = pe.transpose(b[:, c * P:(c + 1) * P], src[:, t, (4 * j + c) * P:(4 * j + c + 1) * P], ident)
                        full(r, ins)

            def gemm(b, cols_at, lhsT, rhs, k):
                for c in range(k):
                    ins = pe.matmul(b[:, cols_at[0]:cols_at[1]], lhsT=lhsT(c), rhs=rhs(c), start=(c == 0), stop=(c == k - 1))
                return ins

            def nat(w, act, k, n, r, product, pack=False):
                for t in range(TC):
                    if t == 0 or not pack:
                        b = bank(r, product)
                    at = (t * n, (t + 1) * n) if pack else (0, n)
                    ins = gemm(b, at, lambda c: act[:, c, t * P:(t + 1) * P], lambda c: w[:, c, :], k)
                    if not pack or t == TC - 1:
                        done = full(r, ins)
                return done

            def turned(w, act, k, tiles, r, product):
                for j in range(tiles // 2):
                    b = bank(r, product)
                    for cc in range(2):
                        f = (2 * j + cc) * P
                        ins = gemm(b, (cc * T, (cc + 1) * T), lambda c: w[:, c, f:f + P], lambda c: act[:, c, :], k)
                    done = full(r, ins)
                return done

            def as_cols(n, at=0, width=512):
                return chunk(n)[:, at:at + 8 * width].rearrange("p (c n) -> p c n", c=8)

            def as_rows(n):
                return chunk(n).rearrange("p (c n) -> p c n", c=4)

            att = {"i": 0, "sc": 0}

            def attention(q, keys, v, nk, dv, n_tasks, bias=None, tables=False):
                i0 = att["i"]
                att["i"] += n_tasks

                def scores(i):
                    h, t = divmod(i, TC)
                    ks = keys(h)
                    width = T
                    if tables:
                        width = key_tiles(nk, i, True) * P // len(ks)
                        ks = [kk[:, 0:width] for kk in ks]
                    together = 512 // width
                    for first in range(0, len(ks), together):
                        mine = ks[first:first + together]
                        if tables:
                            att["sc"] += len(mine)
                            b = bank("v", by=(S("att_sc"), att["sc"]))
                        else:
                            b = bank("v", by=(S("att_p"), i0 + i + 1))
                        for g, kk in enumerate(mine):
                            o = b[:, g * width:(g + 1) * width]
                            if bias is not None:
                                pe.matmul(o, lhsT=flip, rhs=bias(h, t), start=True, stop=False)
                            ins = pe.matmul(o, lhsT=q(h, t, first + g), rhs=kk, start=(bias is None), stop=True)
                        full("v", ins)

                def turn_weights(i):
                    pe.wait_ge(S("att_p"), i0 + i + 1)
                    p = W(p_at, 2, nk * P)
                    mine = key_tiles(nk, i, tables)
                    for first in range(0, mine, 4):
                        m = min(4, mine - first)
                        b = bank("a", "att_pT")
                        for k in range(m):
                            ins = pe.transpose(b[:, k * P:(k + 1) * P], p[:, i % 2, (first + k) * P:(first + k + 1) * P], ident)
                        full("a", ins)
                    upto[i] = made["att_pT_a"]

                def values(i):
                    h = i // TC
                    pe.wait_ge(S("att_pT_a"), upto[i])
                    pT = W(pT_at, 2, nk * P)
                    b = bank("v", by=(S("att_o"), i0 + i + 1))
                    mine = key_tiles(nk, i, tables)
                    for k in range(mine):
                        ins = pe.matmul(b[:, 0:dv], lhsT=pT[:, i % 2, k * P:(k + 1) * P], rhs=v(h, k * nk // mine),
                                        start=(k == 0), stop=(k == mine - 1))
                    full("v", ins)

                upto = {}
                for i in range(n_tasks + 3):
                    if i < n_tasks:
                        scores(i)
                    if 2 <= i < n_tasks + 2:
                        turn_weights(i - 2)
                    if i >= 3:
                        values(i - 3)

            def route(w, n, k, meanwhile=None):
                b = bank("v", by=(S("logits_read"), k))
                for t in range(TC):
                    for r in "va":
                        pe.wait_ge(S("xT_" + r), made["xT_" + r] - (TC - 1 - t))
                    ins = gemm(b, (t * n, (t + 1) * n), lambda c: xT[:, c, t * P:(t + 1) * P], lambda c: w[:, c, :], DC)
                full("v", ins)
                if meanwhile:
                    meanwhile()
                pe.wait_ge(S("chosen"), k)
                b = bank("v", by=(S("slots"), k))
                pe.matmul(b[:, 0:16], lhsT=before, rhs=sel[:, 0, :], start=True, stop=True)
                pe.matmul(b[:, 16:32], lhsT=ones, rhs=sel[:, 0, :], start=True, stop=False)
                pe.matmul(b[:, 16:32], lhsT=before, rhs=sel[:, 1, :], start=False, stop=True)
                pe.matmul(b[:, 32:48], lhsT=ones, rhs=sel[:, 0, :], start=True, stop=False)
                ins = pe.matmul(b[:, 32:48], lhsT=ones, rhs=sel[:, 1, :], start=False, stop=True)
                full("v", ins)

            def drain():
                for r in "va":
                    for by in emptied[r][-BANKS:]:
                        pe.wait_ge(*by)

            def experts(ph, p):
                sem, B = ph.sem, ph.base(p)
                g_bank, u_bank, y_bank, t_bank, x_bank = psum[0:2], psum[2:4], psum[4:6], psum[6], psum[7]
                g, u_, y = W(MOE["g"], 4, P), W(MOE["u"], 4, P), W(MOE["y"], 2, 512)
                pick, pickg, pickT = W(MOE["pick"], TC, ph.group * CAP), W(MOE["pickg"], TC, P), W(MOE["pickT"], TC, P)

                def gather(g):
                    pe.wait_ge(sem("pick"), plus(g * (2 * ph.group) + 2 * ph.group, B["pick"]))
                    width = ph.group * CAP
                    per_bank = 512 // width
                    for c in range(DC):
                        to = psum[8 - ph.group + c // per_bank][:, c % per_bank * width:(c % per_bank + 1) * width]
                        for t in range(TC):
                            ins = pe.matmul(to, lhsT=x[:, t, c * P:(c + 1) * P], rhs=pick[:, t, :], start=(t == 0), stop=(t == TC - 1))
                    ins.then_inc(sem("gathered"), 1)

                def scatter(e, j, spread_out):
                    if j == 0:
                        pe.wait_ge(sem("y"), plus(e + 1, B["y"]))
                        pe.wait_ge(sem("pickT"), plus(e + 1, B["pickT"]))
                        to = x_bank
                    elif spread_out:
                        to = psum[j]
                    else:
                        pe.wait_ge(sem("added"), plus(e * 4 + j, B["added"]))
                        to = x_bank
                    pe.matmul(to, lhsT=pickT[:, j // 2, :], rhs=y[:, j % 2, :], start=True, stop=True).then_inc(sem("scattered"), 1)

                def split_wait(it, k, q):
                    if k is None:
                        pe.wait_ge(sem("lo"), plus(q + 1, B["lo"]))
                        return q % SPLIT
                    pe.wait_ge(sem("lo"), plus(it * 24 + (6 * k + 4 + q + 1), B["lo"]))
                    return (4 + q) % SPLIT

                def up(it, k, q, to, buf, half):
                    sl = split_wait(it, k, q)
                    for c in range(4):
                        for part in (w_hi, w_lo):
                            ins = pe.matmul(to, lhsT=xe[:, buf, 4 * half + c, :], rhs=part[:, sl, c * 512:(c + 1) * 512],
                                            start=(half == 0 and c == 0 and part is w_hi), stop=(half == 1 and c == 3 and part is w_lo))
                    ins.then_inc(sem("used"), 1)

                def step(it, k, more):
                    first, last = ph.first(k), ph.last(k)
                    e = ph.expert(it, k)
                    gathers = k % 2 == 0 and ph.there_is(ph.next_gather(it, k))
                    pe.wait_ge(sem("gu"), plus(it * 8 + (2 * k + 2), B["gu"]))
                    for i, src in enumerate((g, u_)):
                        for c in range(4):
                            at = (4 * i + c) * CAP
                            ins = pe.matmul(t_bank[:, at:at + CAP], lhsT=src[:, c, :], rhs=stack, start=True, stop=True)
                    ins.then_inc(sem("t_full"), 1)
                    nk = (k + 1) % 2
                    buf = ph.buffer(k + 1)
                    for q in range(4):
                        if first:
                            scatter(e, q, not more)
                        if more:
                            if q == 0 and ph.first(k + 1):
                                pe.wait_ge(sem("xe_lo"), plus(it * 2 + ((k + 1) // 2 + 1), B["xe_lo"]))
                            up(it, k, q, (g_bank if q < 2 else u_bank)[nk], buf, q % 2)
                    if first:
                        pe.wait_ge(sem("added"), plus(e * 4 + 4, B["added"]))
                    if gathers:
                        if ph.group == 2:
                            pe.wait_ge(sem("h"), plus(it * 4 + (k + 1), B["h"]))
                        gather(ph.next_gather(it, k))
                    pe.wait_ge(sem("h_lo"), plus(it * 4 + (k + 1), B["h_lo"]))
                    for half in range(2):
                        sl = split_wait(it, k, (4 if more else 0) + half)
                        for c in range(2):
                            for part in (w_hi, w_lo):
                                for n2 in range(2):
                                    ins = pe.matmul(y_bank[n2], lhsT=hT[:, k % 2, 2 * half + c, :],
                                                    rhs=part[:, sl, c * D + n2 * 512:c * D + (n2 + 1) * 512],
                                                    start=(first and half == 0 and c == 0 and part is w_hi),
                                                    stop=(last and half == 1 and c == 1 and part is w_lo))
                        ins.then_inc(sem("used"), 1)
                    if first:
                        pe.wait_ge(sem("pickg"), plus(e * 2 + 2, B["pickg"]))
                        if gathers:
                            pe.wait_ge(sem("xe_lo"), plus(ph.next_gather(it, k) + 1, B["xe_lo"]))
                        for t in range(TC):
                            ins = pe.transpose(x_bank[:, t * P:(t + 1) * P], pickg[:, t, :], ident)
                        ins.then_inc(sem("pick_turned"), 1)

                gather(0)
                pe.wait_ge(sem("xe_lo"), plus(1, B["xe_lo"]))
                for q in range(4):
                    up(None, None, q, (g_bank if q < 2 else u_bank)[0], 0, q % 2)
                ph.run(pe, step)
                for j in range(4):
                    scatter(N_EXP, j, True)
                pe.wait_ge(sem("added"), plus(4 * (N_EXP + 1), B["added"]))

            def expert_layer(k):
                drain()
                ph = phases[k]
                ph.passes(pe, experts)
                for m in range(RING):
                    freed[ph.n0 + 3 * ph.units - RING + m] = (ph.sem("lo"), ph.before["lo"] + ph.per["lo"] - RAW + 2 * m + 2)
                fills = pe.value_load(fullest[0:1, 0:1])
                with pe.If(fills > CAP):
                    extras[k].passes(pe, experts)
                with pe.Else():
                    extras[k].skip(pe, "used t_full gathered pick_turned scattered")

            n = 0
            pe.wait_ge(S("ident_in"), 16)
            turn(W(L0["memN"], TC, D), DC, "memT", loaded=("mem0_in", "mem1_in"))
            wait_made("memT")
            memT = W(L0["memT"], DC, T)
            pe.wait_ge(S("first_k_in"), 16)
            turned(ring[:, 0, 0:2048].rearrange("p (c n) -> p c n", c=DC), memT, DC, 2, "v", "mkv")
            pe.wait_ge(S("first_v_in"), 16)
            freed[n] = nat(ring[:, 0, 2048:].rearrange("p (c n) -> p c n", c=DC), memT, DC, 256, "a", "mkv", pack=True); n += 1
            pe.wait_ge(S("con_in"), 16)
            pe.wait_ge(S("x_in"), 16)
            turn(x, DC, "xT")
            wait_made("xT")
            freed[n] = nat(as_cols(n), xT, DC, 512, "a", "gv"); n += 1
            w = as_cols(n)
            nat(w[:, :, 0:256], xT, DC, 256, "a", "gv", pack=True)
            freed[n] = turned(w[:, :, 256:512], xT, DC, 2, "v", "qm"); n += 1
            freed[n] = nat(as_cols(n), xT, DC, 512, "a", "u"); n += 1
            freed[n] = nat(as_cols(n, 0, 256), xT, DC, 256, "a", "u", pack=True); n += 1
            pe.wait_ge(S("sg_causal"), 1)
            sgw = W(L0["sgw"], N_SG, P)
            for j in range(3):
                b = bank("v", "sw")
                for g in range(4):
                    ins = pe.transpose(b[:, g * P:(g + 1) * P], sgw[:, 4 * j + g, :], ident)
                full("v", ins)
            b = bank("v", "sw")
            full("v", pe.transpose(b[:, 0:N_SG], W(L0["bsN"], P)[0:N_SG, :], ident[0:N_SG, 0:N_SG]))
            qmT = W(L0["qmT"], 2, T)
            wait_made("qm")
            wait_made("mkv")

            def mem_attention(qT, l):
                mk = mkv[:, l, 0, :].rearrange("p (c m) -> p c m", c=2)
                mv = mkv[:, l, 1, :].rearrange("p (c n) -> p c n", c=2)

                def hp(h):
                    return slice(HD * (h % 2), HD * (h % 2) + HD)
                attention(lambda h, t, g: qT[hp(h), h // 2, t * P:(t + 1) * P], lambda h: [mk[hp(h), h // 2, :]],
                          lambda h, k: mv[:, k, h * HD:(h + 1) * HD], 2, HD, 2 * MEM_HEADS)

            p_at, pT_at = W_P, W_PT
            mem_attention(qmT, 0)
            pe.wait_ge(S("att_o"), att["i"])
            gv, swT = W(L0["gv"], TC, SGW), W(L0["swT"], N_SG, P)
            wait_made("sw")
            pe.wait_ge(S("norm"), NORM_AT["gv"])
            for j in range(3):
                b = bank("v", by=(S("mix"), 4 * (j + 1)))
                for g in range(4):
                    hh = 4 * j + g
                    ins = pe.matmul(b[:, g * P:(g + 1) * P].rearrange("p (c d) -> p c d", c=2), lhsT=swT[:, hh, :],
                                    rhs=gv[:, :, hh * HD:(hh + 1) * HD], start=True, stop=True)
                full("v", ins)
            pe.wait_ge(S("mix"), N_SG)
            turn(W(L0["cat"], TC, D), DC, "xT")
            wait_made("xT")
            for half in range(2):
                freed[n] = nat(as_cols(n), xT, DC, 512, "v", "z"); n += 1
            pe.wait_ge(S("late_in"), 32)
            turned(late[0], memT, DC, 2, "a", "mkv")
            turn(x, DC, "xT", "ln1_0")
            pe.wait_ge(S("wr_in"), 16)

            route(wr, 16, 1, lambda: nat(late[1], memT, DC, 256, "a", "mkv", pack=True))
            expert_layer(0)
            n += 3 * phases[0].units

            turn(x, DC, "xT", "ln2_0")
            wait_made("xT")
            freed[n] = turned(as_cols(n), xT, DC, 4, "v", "qkv"); n += 1
            w = as_cols(n)
            turned(w[:, :, 0:256], xT, DC, 2, "a", "qkv")
            freed[n] = turned(w[:, :, 256:512], xT, DC, 2, "a", "qkv"); n += 1
            freed[n] = turned(as_cols(n), xT, DC, 4, "v", "qkv"); n += 1
            freed[n] = nat(as_cols(n), xT, DC, 512, "a", "qkv"); n += 1
            turned(as_cols(n, 0, 256), xT, DC, 2, "v", "qkv")
            freed[n] = nat(as_cols(n, 2048, 256), xT, DC, 256, "a", "qkv", pack=True); n += 1
            wait_made("qkv")
            qT, kT, v = W(L1["qT"], 6, T), W(L1["kT"], 6, T), W(L1["v"], TC, SGW)

            def pair(g, h):
                hh = g * DIL_HEADS + h
                return slice(HD * (hh % 2), HD * (hh % 2) + HD), hh // 2

            def dil_q(h, t, g):
                r, tile = pair(g, h)
                return qT[r, tile, t * P:(t + 1) * P]

            def dil_k(h):
                return [kT[pair(g, h)[0], pair(g, h)[1], :] for g in range(3)]

            def dil_v(h, k):
                hh = (k // 2) * DIL_HEADS + h
                return v[:, k % 2, hh * HD:(hh + 1) * HD]

            attention(dil_q, dil_k, dil_v, 6, HD, 2 * DIL_HEADS, tables=True)
            wait_made("mkv")
            mem_attention(W(L1["qmT"], 2, T), 1)
            pe.wait_ge(S("att_o"), att["i"])
            turn(W(L1["cat"], TC, 512), 4, "xT")
            wait_made("xT")
            w = as_rows(n)
            for half in range(2):
                freed[n] = nat(w[:, :, half * 512:(half + 1) * 512], xT, 4, 512, "v", "z")
            n += 1
            turn(W(W_MEM2, TC, D), DC, "memT", "mem", rings="a")
            wait_made("memT")
            memT = W(W_MEMT2, DC, T)
            pe.wait_ge(S("late_in"), 64)
            turned(late[0], memT, DC, 2, "a", "xa")
            turn(x, DC, "xT", "ln1_1")

            route(wr, 16, 2, lambda: turned(late[1], memT, DC, 2, "a", "xa"))
            expert_layer(1)
            n += 3 * phases[1].units

            freed[n] = nat(as_cols(n), memT, DC, 512, "a", "xa"); n += 1
            turn(W(XA["H"], TC, D), DC, "xT", "mix")
            wait_made("xT")
            freed[n] = turned(as_cols(n), xT, DC, 4, "v", "xa"); n += 1
            wait_made("xa")
            qT, kT, v = W(XA["qT"], 4, T), W(W_MK2, 4, T), W(XA["mv"], TC, 512)
            p_at, pT_at = XA["p"], XA["pT"]
            attention(lambda h, t, g: qT[:, h, t * P:(t + 1) * P], lambda h: [kT[:, h, :]],
                      lambda h, k: v[:, k, h * P:(h + 1) * P], 2, P, 2 * XA_HEADS)

            def join(o, oT, k, norm=None):
                nonlocal n
                for half in range(2):
                    freed[n] = nat(as_cols(n), xT, DC, 512, "a", "gate"); n += 1
                pe.wait_ge(S("att_o"), att["i"])
                turn(o, k, "oT", norm)
                wait_made("oT")
                wait_made("gate")
                if k == 4:
                    w = as_rows(n)
                    for half in range(2):
                        freed[n] = nat(w[:, :, half * 512:(half + 1) * 512], oT, 4, 512, "v", "joined")
                    n += 1
                else:
                    for half in range(2):
                        freed[n] = nat(as_cols(n), oT, DC, 512, "v", "joined"); n += 1

            join(W(XA["o"], TC, 512), W(XA["oT"], 4, T), 4)

            p_at, pT_at = W_P2, W_PT2
            freed[n] = turned(as_cols(n), xT, DC, 4, "v", "na"); n += 1
            freed[n] = turned(as_cols(n), xT, DC, 4, "a", "na"); n += 1
            freed[n] = nat(as_cols(n), xT, DC, 512, "a", "na"); n += 1
            wait_made("na")
            pe.wait_ge(S("na_table"), 1)
            qT, kT, v = W(NA["qT"], 4, T), W(NA["kT"], 4, T), W(NA["v"], TC, 512)
            table = W(W_TAB, NA_HEADS, 6 * GRID_W)

            def na_rows(h):
                return slice(HD * (h % 2), HD * (h % 2) + HD)

            attention(lambda h, t, g: qT[na_rows(h), h // 2, t * P:(t + 1) * P], lambda h: [kT[na_rows(h), h // 2, :]],
                      lambda h, k: v[:, k, h * HD:(h + 1) * HD], 2, HD, 2 * NA_HEADS,
                      bias=lambda h, t: table[:, h, (1 - t) * P:(1 - t) * P + T])
            join(W(NA["o"], TC, 512), W(NA["oT"], 4, T), 4)

            wait_made("joined")
            freed[n] = nat(as_cols(n), xT, DC, 512, "v", "rope"); n += 1
            freed[n] = nat(as_cols(n), xT, DC, 512, "v", "rope"); n += 1
            for half in range(2):
                freed[n] = nat(as_cols(n), xT, DC, 512, "a", "rv"); n += 1
            for half in range(2):
                freed[n] = nat(as_cols(n), xT, DC, 512, "a", "rg"); n += 1
            wait_made("rope")
            turn(W(RET["q"], TC, 512), 4, "rqk")
            turn(W(RET["k"], TC, 512), 4, "rqk")
            wait_made("rqk")
            wait_made("rv")
            qT, kT, v, sd = W(RET["qT"], 4, T), W(RET["kT"], 4, T), W(RET["v"], TC, D), W(RET["sd"], 2, TC, T)
            for h in range(RET_HEADS + 1):
                if h < RET_HEADS:
                    b = bank("v", by=(S("ret_sd"), h + 1))
                    for j in range(TC):
                        ins = pe.matmul(b[:, j * T:(j + 1) * T], lhsT=kT[:, h, j * P:(j + 1) * P], rhs=qT[:, h, :], start=True, stop=True)
                    full("v", ins)
                if h >= 1:
                    g = h - 1
                    pe.wait_ge(S("ret_sd"), g + 1)
                    b = bank("a", "ret_y")
                    for i in range(TC):
                        for j in range(TC):
                            ins = pe.matmul(b[:, i * RET_V:(i + 1) * RET_V], lhsT=sd[:, g % 2, j, i * P:(i + 1) * P],
                                            rhs=v[:, j, g * RET_V:(g + 1) * RET_V], start=(j == 0), stop=(j == TC - 1))
                    full("a", ins)
            join(W(RET["y"], TC, D), W(RET["yT"], DC, T), DC, "gn")
            wait_made("joined")
            turn(W(W_COMB, TC, D), DC, "xT")
            wait_made("xT")
            for half in range(2):
                freed[n] = nat(as_cols(n), xT, DC, 512, "v", "z"); n += 1
            turn(x, DC, "xT", "ffn")
            pe.wait_ge(S("wr2_in"), 32)
            route(wr2, 20, 3)
            expert_layer(2)

        @block.scalar
        def _(act):
            took = [0]
            counted = {}

            def bank():
                took[0] += 1
                act.wait_ge(S("a_full"), took[0])
                return RB["a"][(took[0] - 1) % BANKS]

            def step(ins):
                counted["act_step"] = counted.get("act_step", 0) + 1
                ins.then_inc(S("act_step"), 1)
                act.wait_ge(S("act_step"), counted["act_step"])

            def empty(dst, product, func=ACT.Copy, n=512, scale=None):
                b = bank()
                src = b[:, 0:n]
                if len(dst.shape) == 3:
                    src = src.rearrange("p (a b) -> p a b", a=dst.shape[1])
                kw = {} if scale is None else {"scale": scale}
                act.activation(dst, src, func, **kw).then_inc(S(product + "_a"), 1)

            def turn(dst, tiles, product):
                for job in range(1, tiles // 2, 2):
                    t, j = divmod(job, tiles // 4)
                    empty(dst[:, 4 * j:4 * j + 4, t * P:(t + 1) * P], product)

            def nat(dst, n, product, func=ACT.Copy, pack=False):
                if pack:
                    empty(dst, product, func)
                else:
                    for t in range(TC):
                        empty(dst[:, t, :], product, func, n)

            att = {"i": 0}

            def attention(nk, n_tasks, scale, p_at, pT_at, tables=False):
                i0 = att["i"]
                att["i"] += n_tasks
                p, pT = W(p_at, 2, nk * P), W(pT_at, 2, nk * P)
                for i in range(n_tasks + 2):
                    if i >= 2:
                        mine = key_tiles(nk, i, tables)
                        for first in range(0, mine, 4):
                            m = min(4, mine - first) * P
                            empty(pT[:, i % 2, first * P:first * P + m], "att_pT", n=m)
                    if i < n_tasks:
                        act.wait_ge(S("att_nm"), i0 + i + 1)
                        I = i0 + i
                        mine = key_tiles(nk, i, tables) * P
                        if tables:
                            src = p[:, i % 2, 0:mine]
                        else:
                            src = score_bank(i0 + i)
                        act.activation(p[:, i % 2, 0:mine], src, ACT.Exp, bias=att_nm[:, I:I + 1], scale=scale,
                                       accum_out=att_sum[:, I:I + 1]).then_inc(S("att_p"), 1)

            def score_bank(i):
                return RB["v"][score_at[i] % BANKS][:, 0:T]

            score_at = {}
            v_jobs = 0

            def plan(before, i0, n_tasks):
                j = before
                for i in range(n_tasks + 3):
                    if i < n_tasks:
                        score_at[i0 + i] = j
                        j += 1
                    if i >= 3:
                        j += 1
                return j

            def routed(k):
                act.wait_ge(S("logit_max"), k)
                e, lgt, nm, sm = rt[:, 1, :], rt[:, 0, :], rsm[:, 0, :], rsm[:, 1, :]
                if k < 3:
                    for c in range(TC):
                        act.activation(e[:, c * 16:(c + 1) * 16], lgt[:, c * 16:(c + 1) * 16], ACT.Exp, bias=nm[:, c:c + 1],
                                       accum_out=sm[:, c:c + 1]).then_inc(S("logit_exp"), 1)
                else:
                    act.activation(rt[:, 3, :], rt[:, 2, :], ACT.Exp).then_inc(S("logit_exp"), 1)
                    act.activation(rsm[:, 3, :], rsm[:, 2, :], ACT.Exp).then_inc(S("logit_exp"), 1)

            def experts(ph, p, ahead=False):
                sem, B = ph.sem, ph.base(p)
                g, u_, silu, h, y = W(MOE["g"], 512), W(MOE["u"], 512), W(MOE["silu"], 256), W(MOE["h"], 4, CAP), W(MOE["y"], 2, 512)
                pickT = W(MOE["pickT"], T)

                def high(it, k, q):
                    ph.landed(act, it, k, q, B)
                    if k is None:
                        r, sl = ph.slot(q), q % SPLIT
                        if q >= SPLIT:
                            act.wait_ge(sem("used"), plus(q - SPLIT + 1, B["used"]))
                    else:
                        r, sl = ph.slot(4 + q), (4 + q) % SPLIT
                        act.wait_ge(sem("used"), plus(it * 24 + (6 * k + 4 + q - SPLIT + 1), B["used"]))
                    act.copy(w_hi[:, sl, :], raw[:, r, :]).then_inc(sem("hi"), 1)

                def gate_up(bank_at, used):
                    for dst, b, d in ((g, psum[bank_at], -2), (u_, psum[2 + bank_at], 0)):
                        act.wait_ge(sem("used"), plus(used, B["used"]) + d)
                        act.copy(dst, b).then_inc(sem("gu"), 1)

                def tokens(g, k):
                    act.wait_ge(sem("gathered"), plus(g + 1, B["gathered"]))
                    act.copy(ph.tokens_of(k)[:, :, :, 0:CAP], ph.gathered(k)).then_inc(sem("xe_hi"), 1)

                def step(it, k, more):
                    first, last = ph.first(k), ph.last(k)
                    e = ph.expert(it, k)
                    gathers = k % 2 == 0 and ph.there_is(ph.next_gather(it, k))
                    act.wait_ge(sem("t_full"), plus(it * 4 + (k + 1), B["t_full"]))
                    act.activation(silu, psum[6][:, 0:256], ACT.Silu).then_inc(sem("silu"), 1)
                    if more:
                        high(it, k, 2)
                    act.wait_ge(sem("h"), plus(it * 4 + (k + 1), B["h"]))
                    act.copy(hT[:, k % 2, :, 0:CAP], h).then_inc(sem("h_hi"), 1)
                    if more:
                        high(it, k, 3)
                        high(it, k, 4)
                        high(it, k, 5)
                        gate_up((k + 1) % 2, it * 24 + (6 * k + 8))
                        high(it, k + 1, 0)
                    if gathers:
                        tokens(ph.next_gather(it, k), k // 2 + 1)
                    if more:
                        high(it, k + 1, 1)
                    if last:
                        act.wait_ge(sem("used"), plus(it * 24 + (6 * k + (10 if more else 6)), B["used"]))
                        act.copy(y, psum_all[:, 4:6, :]).then_inc(sem("y"), 1)
                    if first:
                        act.wait_ge(sem("pick_turned"), plus(e + 1, B["pick_turned"]))
                        act.copy(pickT, psum[7][:, 0:T]).then_inc(sem("pickT"), 1)

                if ahead or ph.more:
                    for q in range(AHEAD):
                        high(None, None, q)
                if ahead:
                    return
                high(None, None, AHEAD)
                tokens(0, 0)
                for q in range(AHEAD + 1, 4):
                    high(None, None, q)
                high(0, 0, 0)
                high(0, 0, 1)
                gate_up(0, 4)
                ph.run(act, step)

            def expert_layer(k):
                phases[k].passes(act, experts)
                act.wait_ge(S("slots"), k + 1)
                fills = act.value_load(fullest[0:1, 0:1])
                with act.If(fills > CAP):
                    extras[k].passes(act, experts)
                with act.Else():
                    extras[k].skip(act, "hi gu silu h_hi xe_hi pickT y")

            def square(src, junk, ready=None):
                for c in range(TC):
                    if ready is not None:
                        act.wait_ge(S(ready[0]), ready[1] + c)
                    act.activation(junk[:, c, :], src[:, c, :], ACT.Square, accum_out=var8[:, c:c + 1]).then_inc(S("var"), 1)

            turn(W(L0["memT"], DC, T), DC, "memT"); v_jobs += 2
            nat(mkv[:, 0, 1, :], 256, "mkv", pack=True); v_jobs += 1
            turn(xT, DC, "xT"); v_jobs += 2
            gv, u = W(L0["gv"], TC, SGW), W(L0["u"], TC, SGW)
            nat(gv[:, :, 0:512], 512, "gv", ACT.Gelu)
            nat(gv[:, :, 512:SGW], 256, "gv", ACT.Gelu, pack=True); v_jobs += 1
            nat(u[:, :, 0:512], 512, "u", ACT.Gelu)
            nat(u[:, :, 512:SGW], 256, "u", ACT.Gelu, pack=True)
            v_jobs += 4
            v_jobs = plan(v_jobs, att["i"], 8)
            attention(2, 8, HD ** -0.5, W_P, W_PT)
            v_jobs += 3
            turn(xT, DC, "xT"); v_jobs += 2
            v_jobs += 4
            empty(mkv[:, 1, 0, :], "mkv")
            turn(xT, DC, "xT"); v_jobs += 2
            experts(phases[0], None, ahead=True)
            routed(1); v_jobs += 2
            empty(mkv[:, 1, 1, :], "mkv")
            expert_layer(0)
            turn(xT, DC, "xT"); v_jobs += 2
            qT, kT, v = W(L1["qT"], 6, T), W(L1["kT"], 6, T), W(L1["v"], TC, SGW)
            v_jobs += 5
            empty(qT[:, 4:6, :], "qkv")
            empty(W(L1["qmT"], 2, T), "qkv")
            nat(v[:, :, 0:512], 512, "qkv")
            nat(v[:, :, 512:SGW], 256, "qkv", pack=True)
            attention(6, 8, HD ** -0.5, W_P, W_PT, tables=True)
            v_jobs += (2 + 3) * DIL_HEADS
            v_jobs = plan(v_jobs, att["i"], 8)
            attention(2, 8, HD ** -0.5, W_P, W_PT)
            turn(xT, 4, "xT"); v_jobs += 1
            v_jobs += 4
            act.wait_ge(S("mem2_in"), 16)
            square(W(W_MEM2, TC, D), W(W_MEM2 + TC * D, TC, D))
            memT, mk = W(W_MEMT2, DC, T), W(W_MK2, 4, T)
            for t in range(TC):
                for j in range(0, DC, 4):
                    empty(memT[:, j:j + 4, t * P:(t + 1) * P], "memT")
            empty(mk[:, 0:2, :], "xa")
            turn(xT, DC, "xT"); v_jobs += 2
            experts(phases[1], None, ahead=True)
            routed(2); v_jobs += 2
            empty(mk[:, 2:4, :], "xa")
            expert_layer(1)
            empty(W(XA["mv"], TC, 512)[:, 0, :], "xa")
            act.wait_ge(S("norm"), NORM_AT["ln2_1"])
            square(x, W(XA["H"], TC, D))
            empty(W(XA["mv"], TC, 512)[:, 1, :], "xa")
            turn(xT, DC, "xT"); v_jobs += 2
            v_jobs += 2
            v_jobs = plan(v_jobs, att["i"], 8)
            attention(2, 8, P ** -0.5, XA["p"], XA["pT"])

            def join(oT, k, gate_at):
                nonlocal v_jobs
                gate = W(gate_at, TC, D)
                for half in range(2):
                    nat(gate[:, :, half * 512:(half + 1) * 512], 512, "gate", ACT.Sigmoid)
                turn(oT, k, "oT")
                v_jobs += k // 4 + 4

            join(W(XA["oT"], 4, T), 4, XA["gate"])
            v_jobs += 2
            kT, v = W(NA["kT"], 4, T), W(NA["v"], TC, 512)
            empty(kT[:, 0:2, :], "na")
            empty(kT[:, 2:4, :], "na")
            nat(v, 512, "na")
            v_jobs = plan(v_jobs, att["i"], 16)
            attention(2, 16, 1.0, W_P2, W_PT2)
            join(W(NA["oT"], 4, T), 4, NA["gate"])
            act.wait_ge(S("dec_in"), 32)
            act.activation(lg[:, 0, :], dec[:], ACT.Abs).then_inc(S("dec_abs"), 1)
            act.wait_ge(S("dec_abs"), 1)
            act.activation(lg[:, 1, :], lg[:, 0, :], ACT.Exp, scale=-1.0).then_inc(S("dec_exp"), 1)
            Dm = W(RET["D"], RET_HEADS, TC * T)
            act.wait_ge(S("ret_e"), RET_HEADS)
            for h in range(RET_HEADS):
                act.activation(Dm[:, h, :], Dm[:, h, :], ACT.Exp).then_inc(S("ret_d"), 1)
            v, rg, y = W(RET["v"], TC, D), W(RET["rg"], TC, D), W(RET["y"], TC, D)
            for half in range(2):
                nat(v[:, :, half * 512:(half + 1) * 512], 512, "rv")
            for half in range(2):
                nat(rg[:, :, half * 512:(half + 1) * 512], 512, "rg", ACT.Silu)
            turn(W(RET["qT"], 4, T), 4, "rqk")
            turn(W(RET["kT"], 4, T), 4, "rqk")
            for h in range(RET_HEADS):
                empty(y[:, :, h * RET_V:(h + 1) * RET_V], "ret_y")
            join(W(RET["yT"], DC, T), DC, RET["gate"])
            turn(xT, DC, "xT")
            square(x, W(RET["y"], TC, D), ("z_v", 11))
            turn(xT, DC, "xT")
            experts(phases[2], None, ahead=True)
            routed(3)
            expert_layer(2)
            act.wait_ge(S("summed"), 1)
            square(W(MOE["acc"], TC, D), W(0, TC, D))

        @block.vector
        def _(dve):
            took = [0]
            counted = {"dve_step": 0, "rstd": 0, "att": 0, "sc": 0}

            def bank():
                took[0] += 1
                dve.wait_ge(S("v_full"), took[0])
                return RB["v"][(took[0] - 1) % BANKS]

            def step(ins):
                counted["dve_step"] += 1
                ins.then_inc(S("dve_step"), 1)
                dve.wait_ge(S("dve_step"), counted["dve_step"])

            def steps(todo):
                for ins in todo:
                    counted["dve_step"] += 1
                    ins.then_inc(S("dve_step"), 1)
                dve.wait_ge(S("dve_step"), counted["dve_step"])

            def empty(dst, product, n=512):
                b = bank()
                src = b[:, 0:n]
                if len(dst.shape) == 3:
                    src = src.rearrange("p (a b) -> p a b", a=dst.shape[1])
                dve.tensor_copy(dst, src).then_inc(S(product + "_v"), 1)

            def turn(dst, tiles, product):
                for job in range(0, tiles // 2, 2):
                    t, j = divmod(job, tiles // 4)
                    empty(dst[:, 4 * j:4 * j + 4, t * P:(t + 1) * P], product)

            def turned(dst, tiles, product):
                for j in range(tiles // 2):
                    empty(dst[:, 2 * j:2 * j + 2, :], product)

            def wait_rstd():
                counted["rstd"] += 1
                dve.wait_ge(S("rstd"), counted["rstd"])

            def spread_of(n, cuts):
                steps(dve.bn_aggr(mv8[:, i, :], stats[:, i * cuts:(i + 1) * cuts, :]) for i in range(n))
                dve.tensor_copy(var8[:, 0:n], mv8[:, 0:n, 1]).then_inc(S("var"), 2)

            def moments(srcs, cuts):
                w = srcs[0].shape[-1] // cuts
                steps(dve.bn_stats(stats[:, n * cuts + c, :], src[:, c * w:(c + 1) * w]) for n, src in enumerate(srcs) for c in range(cuts))
                spread_of(len(srcs), cuts)

            def layer_norm(src, dst, width, slot, params, measured=False):
                if measured:
                    spread_of(TC, 2)
                else:
                    moments([src[:, c, :] for c in range(TC)], 2)
                g, b = prm[:, slot, 0, 0:width], prm[:, slot, 1, 0:width]
                dve.wait_ge(S(f"prm{slot}_in"), params)
                steps(dve.scalar_tensor_tensor(out=dst[:, c, :], in0=src[:, c, :], scalar=mv8[:, c, 0:1], in1=g,
                                               op0=ALU.subtract, op1=ALU.mult) for c in range(TC))
                wait_rstd()
                for c in range(TC):
                    dve.scalar_tensor_tensor(out=dst[:, c, :], in0=dst[:, c, :], scalar=rstd[:, c:c + 1], in1=b,
                                             op0=ALU.mult, op1=ALU.add).then_inc(S("norm"), 1)

            def rms_norm(src, dst, g):
                wait_rstd()
                for c in range(TC):
                    dve.scalar_tensor_tensor(out=dst[:, c, :], in0=src[:, c, :], scalar=rstd[:, c:c + 1], in1=g,
                                             op0=ALU.mult, op1=ALU.mult).then_inc(S("norm"), 1)

            def attention(nk, dv, n_tasks, scale, outs, p_at=None, t_slopes=None, dist=None):
                i0 = counted["att"]
                counted["att"] += n_tasks

                def peak(i):
                    I = i0 + i
                    if t_slopes is None:
                        src = bank()[:, 0:nk * P]
                    else:
                        h, t = divmod(i, TC)
                        mine = key_tiles(nk, i, True)
                        width = mine * P // 3
                        together = 512 // width
                        sc = W(p_at, 2, nk * P)[:, i % 2, 0:mine * P]
                        if i >= 2:
                            dve.wait_ge(S("att_pT_a"), counted["pT0"] + sum(-(-key_tiles(nk, j, True) // 4) for j in range(i - 1)))
                        for g in range(3):
                            if g % together == 0:
                                b = bank()
                            dve.scalar_tensor_tensor(out=sc[:, g * width:(g + 1) * width], in0=dist[:, g, t, 0:width], scalar=t_slopes(g, h),
                                                     in1=b[:, (g % together) * width:(g % together + 1) * width],
                                                     op0=ALU.mult, op1=ALU.add).then_inc(S("att_sc"), 1)
                        counted["sc"] += 3
                        dve.wait_ge(S("att_sc"), counted["sc"])
                        src = sc
                    step(dve.tensor_reduce(att_mx[:, I:I + 1], src, AX.X, ALU.max))
                    dve.tensor_scalar(att_nm[:, I:I + 1], att_mx[:, I:I + 1], -scale, None, ALU.mult).then_inc(S("att_nm"), 1)

                def result(i):
                    I = i0 + i
                    b = bank()
                    step(dve.reciprocal(att_rec[:, I:I + 1], att_sum[:, I:I + 1]))
                    dve.tensor_scalar(outs(i // TC, i % TC), b[:, 0:dv], att_rec[:, I:I + 1], None, ALU.mult).then_inc(S("att_o"), 1)

                for i in range(n_tasks + 3):
                    if i < n_tasks:
                        peak(i)
                    if i >= 3:
                        result(i - 3)

            def residual(half, t):
                b = bank()
                xs = x[:, t, half * 512:(half + 1) * 512]
                return b, xs

            def rank4(*pairs):
                todo, at = [], W_RANK
                for v, r in pairs:
                    shape = [P, v.shape[1], 4, 4]
                    n = 16 * shape[1]
                    vi, vj = v.unsqueeze(3).to_broadcast(shape), v.unsqueeze(2).to_broadcast(shape)
                    not_less, more = (W(at + k * n, n).rearrange("p (g i j) -> p g i j", i=4, j=4) for k in range(2))
                    at += 2 * n
                    todo.append((vi, vj, not_less, more, earlier.unsqueeze(1).to_broadcast(shape), r))
                steps([dve.tensor_tensor(ge, vj, vi, ALU.is_ge) for vi, vj, ge, gt, e, r in todo]
                      + [dve.tensor_tensor(gt, vj, vi, ALU.is_gt) for vi, vj, ge, gt, e, r in todo])
                steps(dve.tensor_tensor(ge, ge, e, ALU.mult) for vi, vj, ge, gt, e, r in todo)
                steps(dve.tensor_tensor(gt, gt, ge, ALU.max) for vi, vj, ge, gt, e, r in todo)
                steps(dve.tensor_reduce(r, gt, AX.X, ALU.add) for vi, vj, ge, gt, e, r in todo)

            def groups(ap, n=8):
                return ap.rearrange("p (g e) -> p g e", e=4)

            def spread(ap):
                return ap.unsqueeze(2).to_broadcast([P, 8, 4])

            selg = sel[:].rearrange("p c (g e) -> p (c g) e", e=4)

            def slots(k):
                b = bank()
                s2 = sel[:].rearrange("p c e -> p (c e)")
                step(dve.scalar_tensor_tensor(out=rt[:, 12, :], in0=b[:, 0:32], scalar=1.0, in1=s2, op0=ALU.add, op1=ALU.mult))
                r = rt[:, 12, :].rearrange("p (c e) -> p c e", c=TC)
                steps([dve.tensor_scalar(slot_main[:], r, -1.0, None, ALU.add),
                       dve.tensor_scalar(slot_more[:], r, -1.0, None, ALU.add),
                       dve.tensor_reduce(fullest_f[:], b[:, 32:48], AX.X, ALU.max)])
                dve.tensor_copy(fullest[:], fullest_f[:]).then_inc(S("slots"), 1)

            acc = W(MOE["acc"], TC, D)

            def route_1(k):
                b = bank()
                lgt, e, nm, sm = rt[:, 0, :], rt[:, 1, :], rsm[:, 0, 0:2], rsm[:, 1, 0:2]
                dve.tensor_copy(lgt, b[:, 0:32]).then_inc(S("logits_read"), 1)
                dve.wait_ge(S("logits_read"), k)
                step(dve.tensor_reduce(rsm[:, 2, 0:2], lgt.rearrange("p (c e) -> p c e", c=TC), AX.X, ALU.max))
                dve.tensor_scalar(nm, rsm[:, 2, 0:2], -1.0, None, ALU.mult).then_inc(S("logit_max"), 1)
                dve.wait_ge(S("logit_exp"), 2 * k)
                step(dve.reciprocal(rsm[:, 3, 0:2], sm))
                probs, score, r, two = rt[:, 2, :], rt[:, 3, :], groups(rt[:, 4, :]), rt[:, 5, :]
                steps(dve.tensor_scalar(probs[:, c * 16:(c + 1) * 16], e[:, c * 16:(c + 1) * 16], rsm[:, 3, c:c + 1], None, ALU.mult)
                      for c in range(TC))
                if k == 1:
                    dve.wait_ge(S("br_in"), 32)
                step(dve.tensor_tensor(score, probs, br[:].rearrange("p c e -> p (c e)"), ALU.add))
                rank4((groups(score), r))
                step(dve.tensor_scalar(groups(two), r, 2.0, None, ALU.is_lt))
                step(dve.tensor_tensor(rt[:, 6, :], score, two, ALU.mult))
                step(dve.tensor_reduce(rsm[:, 4, :], groups(rt[:, 6, :]), AX.X, ALU.add))
                rg = rsm[:, 5, :].rearrange("p (c g) -> p c g", c=TC)
                rank4((rsm[:, 4, :].rearrange("p (c g) -> p c g", c=TC), rg))
                step(dve.tensor_scalar(rsm[:, 6, :], rsm[:, 5, :], 1.0, None, ALU.is_lt))
                dve.tensor_tensor(selg, groups(two), spread(rsm[:, 6, :]), ALU.mult).then_inc(S("chosen"), 1)
                dve.wait_ge(S("chosen"), k)
                s2 = sel[:].rearrange("p c e -> p (c e)")
                step(dve.tensor_tensor(rt[:, 7, :], probs, s2, ALU.mult))
                step(dve.tensor_reduce(rsm[:, 7, 0:2], rt[:, 7, :].rearrange("p (c e) -> p c e", c=TC), AX.X, ALU.add))
                step(dve.reciprocal(rsm[:, 8, 0:2], rsm[:, 7, 0:2]))
                steps(dve.tensor_scalar(gates[:, c, :], rt[:, 7, c * 16:(c + 1) * 16], rsm[:, 8, c:c + 1], None, ALU.mult) for c in range(TC))
                steps(dve.tensor_scalar(acc[:, c, :], x[:, c, :], ALPHA, None, ALU.mult) for c in range(TC))
                slots(k)

            def route_2(k):
                b = bank()
                full = rt[:, 8:10, 0:20]
                dve.wait_ge(S("br2_in"), 64)
                dve.tensor_tensor(full, b[:, 0:40].rearrange("p (c e) -> p c e", c=TC), br2[:], ALU.add).then_inc(S("logits_read"), 1)
                dve.wait_ge(S("logits_read"), k)
                lgrp, lexp = full[:, :, 0:4], full[:, :, 4:20].rearrange("p c (g e) -> p c g e", e=4)
                steps([dve.tensor_reduce(rsm[:, 0, 0:2], lgrp, AX.X, ALU.max),
                       dve.tensor_reduce(rsm[:, 1, :].rearrange("p (c g) -> p c g", c=TC), lexp, AX.X, ALU.max)])
                todo = []
                for c in range(TC):
                    todo.append(dve.tensor_scalar(rsm[:, 2, 4 * c:4 * c + 4], lgrp[:, c, :], rsm[:, 0, c:c + 1], None, ALU.subtract))
                    todo.append(dve.tensor_tensor(groups(rt[:, 2, 16 * c:16 * c + 16]), lexp[:, c],
                                                  rsm[:, 1, 4 * c:4 * c + 4].unsqueeze(2).to_broadcast([P, 4, 4]), ALU.subtract))
                steps(todo)
                dve.sem_inc(S("logit_max"), 1)
                dve.wait_ge(S("logit_exp"), 6)
                e, r, two = rt[:, 3, :], groups(rt[:, 4, :]), rt[:, 5, :]
                rg = rsm[:, 5, :].rearrange("p (c g) -> p c g", c=TC)
                rank4((groups(e), r), (rsm[:, 2, :].rearrange("p (c g) -> p c g", c=TC), rg))
                steps([dve.tensor_scalar(groups(two), r, 2.0, None, ALU.is_lt), dve.tensor_scalar(rsm[:, 6, :], rsm[:, 5, :], 1.0, None, ALU.is_lt)])
                dve.tensor_tensor(selg, groups(two), spread(rsm[:, 6, :]), ALU.mult).then_inc(S("chosen"), 1)
                dve.wait_ge(S("chosen"), k)
                s2 = sel[:].rearrange("p c e -> p (c e)")
                step(dve.tensor_tensor(rt[:, 7, :], e, s2, ALU.mult))
                steps([dve.tensor_reduce(rsm[:, 7, 0:2], rt[:, 7, :].rearrange("p (c e) -> p c e", c=TC), AX.X, ALU.add),
                       dve.tensor_reduce(rsm[:, 8, 0:2], rsm[:, 3, :].rearrange("p (c g) -> p c g", c=TC), AX.X, ALU.add)])
                steps([dve.reciprocal(rsm[:, 9, 0:2], rsm[:, 7, 0:2]), dve.reciprocal(rsm[:, 10, 0:2], rsm[:, 8, 0:2])])
                steps(dve.tensor_scalar(gates[:, c, :], rt[:, 7, c * 16:(c + 1) * 16], rsm[:, 9, c:c + 1], rsm[:, 10, c:c + 1],
                                        ALU.mult, ALU.mult) for c in range(TC))
                slots(k)

            def experts(ph, p, ahead=False):
                sem, B = ph.sem, ph.base(p)
                silu, h, y = W(MOE["silu"], 256), W(MOE["h"], 256), W(MOE["y"], D)
                pick, pickg, pickT = W(MOE["pick"], TC, ph.group * CAP), W(MOE["pickg"], TC, P), W(MOE["pickT"], T)
                acc = W(MOE["acc"], TC, 2, 512)

                def column(of, c, e):
                    return of[:, c, e:e + 1] if isinstance(e, int) else of[:, c, bass.ds(e, 1)]

                def mark(g):
                    for n in range(ph.group):
                        for c in range(TC):
                            dve.tensor_scalar(pick[:, c, n * CAP:(n + 1) * CAP], iota[:, 0:CAP], column(ph.slots, c, g * ph.group + n),
                                              None, ALU.is_equal).then_inc(sem("pick"), 1)

                def mark_gated(e):
                    for c in range(TC):
                        dve.tensor_scalar(pickg[:, c, :], iota, column(ph.slots, c, e), column(gates, c, e),
                                          ALU.is_equal, ALU.mult).then_inc(sem("pickg"), 1)

                def low(it, k, q):
                    if k is None:
                        r, sl = ph.slot(q), q % SPLIT
                        dve.wait_ge(sem("hi"), plus(q + 1, B["hi"]))
                    else:
                        r, sl = ph.slot(4 + q), (4 + q) % SPLIT
                        dve.wait_ge(sem("hi"), plus(it * 24 + (6 * k + 4 + q + 1), B["hi"]))
                    dve.tensor_tensor(w_lo[:, sl, :], raw[:, r, :], w_hi[:, sl, :].bitcast(F32), ALU.subtract).then_inc(sem("lo"), 1)

                def tokens(g, k):
                    to = ph.tokens_of(k)
                    dve.wait_ge(sem("xe_hi"), plus(g + 1, B["xe_hi"]))
                    dve.tensor_tensor(to[:, :, :, CAP:], ph.gathered(k), to[:, :, :, 0:CAP].bitcast(F32),
                                      ALU.subtract).then_inc(sem("xe_lo"), 1)

                def add(e, j, spread_out):
                    dve.wait_ge(sem("scattered"), plus(e * 4 + (j + 1), B["scattered"]))
                    a_ = acc[:, j // 2, j % 2, :]
                    dve.tensor_tensor(a_, a_, psum[j] if spread_out and j > 0 else psum[7], ALU.add).then_inc(sem("added"), 1)

                def step(it, k, more):
                    first, last = ph.first(k), ph.last(k)
                    e = ph.expert(it, k)
                    gathers = k % 2 == 0 and ph.there_is(ph.next_gather(it, k))
                    dve.wait_ge(sem("silu"), plus(it * 4 + (k + 1), B["silu"]))
                    dve.tensor_tensor(h, silu, psum[6][:, 256:512], ALU.mult).then_inc(sem("h"), 1)
                    if first:
                        mark_gated(e)
                        add(e, 0, not more)
                    if more:
                        low(it, k, 2)
                    if first:
                        add(e, 1, not more)
                    dve.wait_ge(sem("h_hi"), plus(it * 4 + (k + 1), B["h_hi"]))
                    dve.tensor_tensor(hT[:, k % 2, :, CAP:], W(MOE["h"], 4, CAP), hT[:, k % 2, :, 0:CAP].bitcast(F32),
                                      ALU.subtract).then_inc(sem("h_lo"), 1)
                    if more:
                        low(it, k, 3)
                    if first:
                        add(e, 2, not more)
                    if more:
                        low(it, k, 4)
                    if first:
                        add(e, 3, not more)
                    if more:
                        low(it, k, 5)
                        low(it, k + 1, 0)
                    if gathers:
                        tokens(ph.next_gather(it, k), k // 2 + 1)
                        if ph.there_is(ph.next_gather(it, k) + 1):
                            mark(ph.next_gather(it, k) + 1)
                    if more:
                        low(it, k + 1, 1)

                if ahead or ph.more:
                    low(None, None, 0)
                if ahead:
                    return

                if ph.more:
                    dve.tensor_scalar(slot_more[:], slot_more[:], -float(CAP), None, ALU.add).then_inc(sem("shift"), 1)
                    dve.wait_ge(sem("shift"), plus(1, B["shift"]))
                mark(0)
                low(None, None, 1)
                tokens(0, 0)
                mark(1)
                low(None, None, 2)
                low(None, None, 3)
                dve.memset(y, 0.0).then_inc(sem("y"), 1)
                dve.memset(pickT, 0.0).then_inc(sem("pickT"), 1)
                low(0, 0, 0)
                low(0, 0, 1)
                ph.run(dve, step)
                for j in range(4):
                    add(N_EXP, j, True)
                dve.wait_ge(sem("added"), plus(4 * (N_EXP + 1), B["added"]))

            def expert_layer(k):
                phases[k].passes(dve, experts)
                dve.wait_ge(S("slots"), k + 1)
                fills = dve.value_load(fullest[0:1, 0:1])
                with dve.If(fills > CAP):
                    extras[k].passes(dve, experts)
                with dve.Else():
                    extras[k].skip(dve, "lo h h_lo pick xe_lo pickg added shift")

            turn(W(L0["memT"], DC, T), DC, "memT")
            empty(mkv[:, 0, 0, :], "mkv")
            turn(xT, DC, "xT")
            empty(W(L0["qmT"], 2 * T), "qm")
            dve.wait_ge(S("gv_a"), 3)
            gv = W(L0["gv"], TC, SGW)
            layer_norm(gv, gv, SGW, 0, 32)
            swT, bsT = W(L0["swT"], N_SG * P), W(L0["bsT"], 16)
            for j in range(3):
                empty(swT[:, j * 512:(j + 1) * 512], "sw")
            empty(bsT[:, 0:N_SG], "sw", N_SG)
            cat = W(L0["cat"], TC, D)
            attention(2, HD, 8, HD ** -0.5, lambda h, t: cat[:, t, SGW + h * HD:SGW + (h + 1) * HD])
            dve.wait_ge(S("u_a"), 3)
            dve.wait_ge(S("sw_v"), 4)
            u = W(L0["u"], TC, SGW)
            for j in range(3):
                b = bank()
                for g in range(4):
                    hh = 4 * j + g
                    c = slice(hh * HD, (hh + 1) * HD)
                    dve.scalar_tensor_tensor(out=cat[:, :, c], in0=b[:, g * P:(g + 1) * P].rearrange("p (c d) -> p c d", c=2),
                                             scalar=bsT[:, hh:hh + 1], in1=u[:, :, c], op0=ALU.add, op1=ALU.mult).then_inc(S("mix"), 1)
            turn(xT, DC, "xT")
            zs = [0]

            def add_residual(scale):
                for half in range(2):
                    for t in range(TC):
                        b, xs = residual(half, t)
                        if scale == 1.0:
                            ins = dve.tensor_tensor(xs, xs, b[:], ALU.add)
                        else:
                            ins = dve.scalar_tensor_tensor(out=xs, in0=xs, scalar=scale, in1=b[:], op0=ALU.mult, op1=ALU.add)
                        ins.then_inc(S("z_v"), 1)
                        zs[0] += 1
                        dve.wait_ge(S("z_v"), zs[0])
                        if scale != 1.0:
                            step(dve.bn_stats(stats[:, 2 * t + half, :], xs))

            add_residual(ALPHA)
            layer_norm(x, x, D, 1, 32, measured=True)
            turn(xT, DC, "xT")
            experts(phases[0], None, ahead=True)
            route_1(1)
            expert_layer(0)
            layer_norm(acc, x, D, 0, 64)
            turn(xT, DC, "xT")
            qT, kT = W(L1["qT"], 6, T), W(L1["kT"], 6, T)
            turned(qT[:, 0:4, :], 4, "qkv")
            turned(kT[:, 0:4, :], 4, "qkv")
            empty(kT[:, 4:6, :], "qkv")
            cat = W(L1["cat"], TC, 512)
            dve.wait_ge(S("dist_in"), 16)
            counted["pT0"] = counted["att"]
            attention(6, HD, 8, HD ** -0.5, lambda h, t: cat[:, t, h * HD:(h + 1) * HD], p_at=W_P,
                      t_slopes=lambda g, h: -SLOPES[g * DIL_HEADS + h] * HD ** 0.5, dist=W(L1["dist"], 3, TC * T)
                      .rearrange("p g (t k) -> p g t k", t=TC))
            attention(2, HD, 8, HD ** -0.5, lambda h, t: cat[:, t, 256 + h * HD:256 + (h + 1) * HD])
            turn(xT, 4, "xT")
            mem2 = W(W_MEM2, TC, D)
            dve.wait_ge(S("prm0_in"), 80)
            rms_norm(mem2, mem2, prm[:, 0, 0, :])
            add_residual(ALPHA)
            layer_norm(x, x, D, 1, 64, measured=True)
            turn(xT, DC, "xT")
            experts(phases[1], None, ahead=True)
            route_1(2)
            expert_layer(1)
            layer_norm(acc, x, D, 1, 96)
            dve.wait_ge(S("prm0_in"), 96)
            rms_norm(x, W(XA["H"], TC, D), prm[:, 0, 0, :])
            turn(xT, DC, "xT")
            turned(W(XA["qT"], 4, T), 4, "xa")
            o = W(XA["o"], TC, 512)
            attention(2, P, 8, P ** -0.5, lambda h, t: o[:, t, h * P:(h + 1) * P])
            comb = W(W_COMB, TC, D)
            joins = [0]

            def join(oT, k, gate_at):
                turn(oT, k, "oT")
                gate = W(gate_at, TC, D)
                joins[0] += 1
                dve.wait_ge(S("gate_a"), 4 * joins[0])
                for half in range(2):
                    for t in range(TC):
                        cs = slice(half * 512, (half + 1) * 512)
                        b = bank()
                        if joins[0] == 1:
                            dve.tensor_tensor(comb[:, t, cs], b[:], gate[:, t, cs], ALU.mult).then_inc(S("joined_v"), 1)
                        else:
                            step(dve.tensor_tensor(gate[:, t, cs], b[:], gate[:, t, cs], ALU.mult))
                            dve.tensor_tensor(comb[:, t, cs], comb[:, t, cs], gate[:, t, cs], ALU.add).then_inc(S("joined_v"), 1)
                dve.wait_ge(S("joined_v"), 4 * joins[0])

            join(W(XA["oT"], 4, T), 4, XA["gate"])
            qT = W(NA["qT"], 4, T)
            for j in range(2):
                b = bank()
                dve.tensor_scalar(qT[:, 2 * j:2 * j + 2, :], b[:].rearrange("p (a b) -> p a b", a=2), HD ** -0.5, None, ALU.mult).then_inc(S("na_v"), 1)
            o = W(NA["o"], TC, 512)
            attention(2, HD, 16, 1.0, lambda h, t: o[:, t, h * HD:(h + 1) * HD])
            join(W(NA["oT"], 4, T), 4, NA["gate"])
            dve.wait_ge(S("dec_exp"), 1)
            z, s, s2, series, ls = lg[:, 1, :], lg[:, 2, :], lg[:, 3, :], lg[:, 4, :], lg[:, 5, :]
            step(dve.tensor_scalar(s2, z, 2.0, None, ALU.add))
            step(dve.reciprocal(series, s2))
            step(dve.tensor_tensor(s, z, series, ALU.mult))
            step(dve.tensor_tensor(s2, s, s, ALU.mult))
            step(dve.tensor_scalar(series, s2, 1.0 / 17, 1.0 / 15, ALU.mult, ALU.add))
            for k in range(13, 0, -2):
                step(dve.tensor_tensor(series, series, s2, ALU.mult))
                step(dve.tensor_scalar(series, series, 1.0 / k, None, ALU.add))
            step(dve.tensor_tensor(series, series, s, ALU.mult))
            step(dve.tensor_scalar(ls, dec[:], 0.0, None, ALU.min))
            step(dve.scalar_tensor_tensor(out=ls, in0=series, scalar=-2.0, in1=ls, op0=ALU.mult, op1=ALU.add))
            Dm = W(RET["D"], RET_HEADS, TC * T)
            AB = W(W_AB, 2, TC * T)
            dve.wait_ge(S("later_in"), 16)
            steps(dve.tensor_scalar(Dm[:, h, :], AB[:, 0, :], ls[:, h:h + 1], None, ALU.mult) for h in range(RET_HEADS))
            for h in range(RET_HEADS):
                dve.scalar_tensor_tensor(out=Dm[:, h, :], in0=AB[:, 1, :], scalar=ls[:, 4 + h:5 + h], in1=Dm[:, h, :],
                                         op0=ALU.mult, op1=ALU.add).then_inc(S("ret_e"), 1)
            rope = W(W_ROPE, 2, TC * 64)
            tmp = W(RET["tmp"], 4, RET_HEADS * 64)
            for name in "qk":
                dst = W(RET[name], TC, 512)
                for t in range(TC):
                    b = bank()[:].rearrange("p (h s d) -> p h s d", h=4, s=2)
                    cos, sin = (rope[:, f, t * 64:(t + 1) * 64].unsqueeze(1).to_broadcast([P, 4, 64]) for f in range(2))
                    ts = [tmp[:, n, :].rearrange("p (h d) -> p h d", h=4) for n in range(4)]
                    steps([dve.tensor_tensor(ts[0], b[:, :, 0, :], cos, ALU.mult), dve.tensor_tensor(ts[1], b[:, :, 1, :], sin, ALU.mult),
                           dve.tensor_tensor(ts[2], b[:, :, 0, :], sin, ALU.mult), dve.tensor_tensor(ts[3], b[:, :, 1, :], cos, ALU.mult)])
                    dd = dst[:, t, :].rearrange("p (h s d) -> p h s d", h=4, s=2)
                    step(dve.tensor_tensor(dd[:, :, 0, :], ts[0], ts[1], ALU.subtract))
                    dve.tensor_tensor(dd[:, :, 1, :], ts[2], ts[3], ALU.add).then_inc(S("rope_v"), 1)
                    counted["rope"] = counted.get("rope", 0) + 1
                    dve.wait_ge(S("rope_v"), counted["rope"])
            turn(W(RET["qT"], 4, T), 4, "rqk")
            turn(W(RET["kT"], 4, T), 4, "rqk")
            sd = W(RET["sd"], 2, TC * T)
            dve.wait_ge(S("ret_d"), RET_HEADS)
            for h in range(RET_HEADS):
                b = bank()
                if h >= 2:
                    dve.wait_ge(S("ret_y_a"), h - 1)
                dve.scalar_tensor_tensor(out=sd[:, h % 2, :], in0=b[:], scalar=RET_QK ** -0.5, in1=Dm[:, h, :],
                                         op0=ALU.mult, op1=ALU.mult).then_inc(S("ret_sd"), 1)
            y, rg = W(RET["y"], TC, D), W(RET["rg"], TC, D)
            dve.wait_ge(S("rg_a"), 4)
            dve.wait_ge(S("prm1_in"), 128)
            steps(dve.tensor_tensor(rg[:, t, :], rg[:, t, :], prm[:, 1, 0, :], ALU.mult) for t in range(TC))
            dve.wait_ge(S("ret_y_a"), RET_HEADS)
            cells = [(t, slice(h * RET_V, (h + 1) * RET_V)) for t in range(TC) for h in range(RET_HEADS)]
            moments([y[:, t, vs] for t, vs in cells], 1)
            steps(dve.scalar_tensor_tensor(out=y[:, t, vs], in0=y[:, t, vs], scalar=mv8[:, n, 0:1], in1=rg[:, t, vs],
                                           op0=ALU.subtract, op1=ALU.mult) for n, (t, vs) in enumerate(cells))
            wait_rstd()
            for n, (t, vs) in enumerate(cells):
                ins = dve.tensor_scalar(y[:, t, vs], y[:, t, vs], rstd[:, n:n + 1], None, ALU.mult)
                ins.then_inc(S("norm" if n % RET_HEADS == RET_HEADS - 1 else "dve_step"), 1)
                if n % RET_HEADS < RET_HEADS - 1:
                    counted["dve_step"] += 1
            join(W(RET["yT"], DC, T), DC, RET["gate"])
            turn(xT, DC, "xT")
            add_residual(1.0)
            steps(dve.tensor_copy(acc[:, c, :], x[:, c, :]) for c in range(TC))
            rms_norm(acc, x, prm[:, 1, 1, :])
            turn(xT, DC, "xT")
            experts(phases[2], None, ahead=True)
            route_2(3)
            expert_layer(2)
            dve.sem_inc(S("summed"), 1)
            dve.wait_ge(S("prm0_in"), 112)
            rms_norm(acc, x, prm[:, 0, 0, :])

        @block.gpsimd
        def _(pool):
            def bc(v):
                return v.partition_broadcast(P)

            pool.dma_start(wr[:], a["w_router"].rearrange("(c p) n -> p c n", p=P)).then_inc(S("wr_in"), 16)
            pool.dma_start(W(L0["bsN"], P)[0:N_SG, :], a["sg_b"][0]).then_inc(S("sgb_in"), 16)
            loads = [
                [(0, SGW, a["sg_ln_g"][0]), (1, SGW, a["sg_ln_b"][0])],
                [(0, D, a["ln1_g"][0]), (1, D, a["ln1_b"][0])],
                [(0, D, a["ln2_g"][0]), (1, D, a["ln2_b"][0])],
                [(0, D, a["ln1_g"][1]), (1, D, a["ln1_b"][1])],
                [(0, D, a["g_mem_2"][0])],
                [(0, D, a["ln2_g"][1]), (1, D, a["ln2_b"][1])],
                [(0, D, a["g_mix_2"][0])],
                [(0, D, a["ret_norm_gain_2"][0]), (1, D, a["g_ffn_2"][0])],
                [(0, D, a["g_final_2"])],
            ]
            last_use = ["gv", "ln1_0", "ln2_0", "ln1_1", "mem", "ln2_1", "mix"]

            def load(k):
                if k >= 2:
                    pool.wait_ge(S("norm"), NORM_AT[last_use[k - 2]])
                for which, width, src in loads[k]:
                    pool.dma_start(prm[:, k % 2, which, 0:width], bc(src)).then_inc(S(f"prm{k % 2}_in"), 16)

            pool.wait_ge(S("first_v_in"), 16)
            load(0)
            load(1)
            for c in range(TC):
                pool.dma_start(br[:, c, :], bc(a["b_router"])).then_inc(S("br_in"), 16)
                pool.dma_start(br2[:, c, 0:4], bc(a["b_router_group_2"][0])).then_inc(S("br2_in"), 16)
                pool.dma_start(br2[:, c, 4:20], bc(a["b_router_expert_2"][0])).then_inc(S("br2_in"), 16)
            pool.dma_start(wr2[:, :, 0:4], a["w_router_group_2"][0].rearrange("(c p) n -> p c n", p=P)).then_inc(S("wr2_in"), 16)
            pool.dma_start(wr2[:, :, 4:20], a["w_router_expert_2"][0].rearrange("(c p) n -> p c n", p=P)).then_inc(S("wr2_in"), 16)
            pool.dma_start(dec[:, 0:4], bc(a["ret_decay_fwd_2"][0])).then_inc(S("dec_in"), 16)
            pool.dma_start(dec[:, 4:8], bc(a["ret_decay_bwd_2"][0])).then_inc(S("dec_in"), 16)
            pool.dma_start(W(W_AB, W_N - W_AB), a["later"]).then_inc(S("later_in"), 16)
            pool.wait_ge(S("sgw_in"), 16)
            pool.wait_ge(S("sgb_in"), 16)
            sgw = W(L0["sgw"], N_SG, P)
            pool.affine_select(out=sgw, in_=sgw, compare_op=ALU.is_ge, fill=0.0, base=0,
                               pattern=[[0, N_SG], [-1, P]], channel_multiplier=1).then_inc(S("sg_causal"), 1)
            pool.wait_ge(S("con_in"), 16)
            done = [0]

            def root(n, eps, scale=None):
                done[0] += 1
                pool.wait_ge(S("var"), 2 * done[0])
                if scale is None:
                    pool.tensor_scalar(var8[:, 0:n], var8[:, 0:n], eps, None, ALU.add).then_inc(S("var_eps"), 1)
                else:
                    pool.tensor_scalar(var8[:, 0:n], var8[:, 0:n], scale, eps, ALU.mult, ALU.add).then_inc(S("var_eps"), 1)
                pool.wait_ge(S("var_eps"), done[0])
                if done[0] >= 2:
                    pool.wait_ge(S("norm"), 2 * (done[0] - 1))
                pool.tensor_tensor(rstd[:, 0:n], var8[:, 0:n], mhalf[:, 0:n], ALU.pow).then_inc(S("rstd"), 1)

            root(2, LN_EPS)
            root(2, LN_EPS)
            pool.wait_ge(S("norm"), NORM_AT["ln1_0"])
            pool.dma_start(W(L1["dist"], 3 * TC * T), a["dist"]).then_inc(S("dist_in"), 16)
            load(2)
            load(3)
            root(2, LN_EPS)
            load(4)
            pool.wait_ge(S("att_o"), 3 * TC * MEM_HEADS)
            pool.dma_start(W(W_MEM2, TC, D), a["mem_2"][0].rearrange("(c p) n -> p c n", p=P)).then_inc(S("mem2_in"), 16)
            root(2, RMS_EPS, 1.0 / D)
            root(2, LN_EPS)
            pool.wait_ge(S("norm"), NORM_AT["ln1_1"])
            rpb = a["na_rpb_2"]
            n_r, n_c = 2 * NA_ROWS - 1, 2 * NA_COLS - 1
            table = W(W_TAB, NA_HEADS, 6, GRID_W)
            for r in range(2):
                for h in range(NA_HEADS):
                    src = bass.AP(rpb.tensor, (h * n_r + 5 - r) * n_c + NA_COLS - 1 - (GRID_W - 1),
                                  [[1, GRID_W], [n_c, 6], [1, GRID_W]])
                    pool.dma_start(table[r * GRID_W:(r + 1) * GRID_W, h], src).then_inc(S("rpb_in"), 16)
            load(5)
            load(6)
            pool.wait_ge(S("rpb_in"), 16 * 2 * NA_HEADS)
            flat = W(W_TAB, NA_HEADS * 6, GRID_W)
            pool.tensor_tensor(flat, flat, namask.unsqueeze(1).to_broadcast([P, NA_HEADS * 6, GRID_W]), ALU.add).then_inc(S("na_table"), 1)
            root(2, LN_EPS)
            load(7)
            root(2, RMS_EPS, 1.0 / D)
            load(8)
            root(8, GN_EPS)
            root(2, RMS_EPS, 1.0 / D)
            root(2, RMS_EPS, 1.0 / D)

        @block.sync
        def _(sp):
            sp.dma_start(ident, a["const"][:, C_IDENT:C_IDENT + P]).then_inc(S("ident_in"), 16)
            for t in range(TC):
                sp.dma_start(W(L0["memN"], TC, D)[:, t, :], a["mem"][0, t * P:(t + 1) * P, :]).then_inc(S(f"mem{t}_in"), 16)

            def fill(n, parts):
                if n >= RING:
                    sp.wait_ge(*freed[n - RING])
                for (at, src), sem in zip(parts, ("first_k_in", "first_v_in") if n == 0 else [f"slot{n % RING}"] * 2):
                    dst = ring[:, n % RING, at:at + src.shape[1] * src.shape[2]].rearrange("p (c n) -> p c n", c=src.shape[1])
                    sp.dma_start(dst, src).then_inc(S(sem), 16)

            def piece(ph, it, k, q):
                which, part = divmod(q, 2)
                e, half = ph.expert(it, k), (k % 2 if ph.halves == 2 else 0)
                if which < 2:
                    w = (ph.wg, ph.wu)[which]
                    return w[e, part * 512:(part + 1) * 512, half * 512:(half + 1) * 512].rearrange("(c p) n -> p c n", p=P)
                return ph.wd[e, half * 512 + part * 256:half * 512 + (part + 1) * 256, :].rearrange("(c p) n -> p c n", p=P)

            def load(ph, slot, src):
                dst = raw[:, slot, :].rearrange("p (c n) -> p c n", c=src.shape[1])
                sp.dma_start(dst, src).then_inc(ph.sem("piece%d" % slot), 16)

            def expert_stream(ph, p):
                B = ph.base(p)

                def room(idx, it, c):
                    if idx is not None and idx < RAW:
                        if not ph.more and ph.n0 + idx // 2 >= RING:
                            sp.wait_ge(*freed[ph.n0 + idx // 2 - RING])
                    else:
                        sp.wait_ge(ph.sem("lo"), plus(it * 24 + c, B["lo"]))

                def unit(it, k, more1):
                    todo = [(k + 1, 0), (k + 1, 1), (k + 1, 2), (k + 1, 3), (k, 4), (k, 5)] if more1 else [(k, 4), (k, 5)]
                    for q, (kk, what) in enumerate(todo):
                        idx = it * 24 + 6 * k + 4 + q if isinstance(it, int) else None
                        src = piece(ph, it, kk, what)
                        room(idx, it, 6 * k + 4 + q - RAW + 1)
                        if idx is None:
                            sp.sem_inc(S("ring_turns"), 1)
                        load(ph, ph.slot(4 + q), src)

                for q in range(4):
                    room(q, 0, 0)
                    load(ph, ph.slot(q), piece(ph, 0, 0, q))
                for k in range(4):
                    unit(0, k, True)
                with sp.Fori(1, ph.iters - 1) as it:
                    for k in range(4):
                        unit(it, k, True)
                for k in range(4):
                    unit(ph.iters - 1, k, k < 3)
                if ph.more:
                    sp.wait_ge(ph.sem("lo"), plus(ph.per["lo"], B["lo"]))
                    sp.sem_inc(ph.sem("loaded"), 1)

            for k, (s0, stream) in enumerate(zip(starts, (stream_0, stream_1, stream_2))):
                for m, parts in enumerate(stream):
                    fill(s0 + m, parts)
                    if k == 0 and m == 0:
                        sp.dma_start(con[:, P:], a["const"][:, P:]).then_inc(S("con_in"), 16)
                        sp.dma_start(x[:], a["x"][0].rearrange("(c p) n -> p c n", p=P)).then_inc(S("x_in"), 16)
                        sp.dma_start(W(L0["sgw"], N_SG, P), a["sg_w"][0].rearrange("g p q -> p g q")).then_inc(S("sgw_in"), 16)
                if k < 2:
                    if k == 1:
                        sp.wait_ge(S("norm"), NORM_AT["ln2_0"])
                    for dst, src in zip(late, late_weights[k]):
                        sp.dma_start(dst[:], src).then_inc(S("late_in"), 16)
                ph, more = phases[k], extras[k]
                ph.passes(sp, expert_stream)
                sp.wait_ge(S("slots"), k + 1)
                fills = sp.value_load(fullest[0:1, 0:1])
                with sp.If(fills > CAP):
                    sp.wait_ge(ph.sem("lo"), ph.before["lo"] + ph.per["lo"])
                    more.passes(sp, expert_stream)
                with sp.Else():
                    for m in range(RAW):
                        sp.sem_inc(more.sem(f"piece{m}"), MORE * more.per["piece"])
            for c in range(TC):
                sp.wait_ge(S("norm"), NORM_AT["final"] - TC + 1 + c)
                sp.dma_start(out[0, c * P:(c + 1) * P, :], x[:, c, :]).then_inc(S("stored"), 16)
            sp.wait_ge(S("stored"), 16 * TC)


_INS = ["x", "mem", "w_in_a", "w_out_a", "sg_ln_g", "sg_ln_b", "sg_w", "sg_b", "w_in_b", "w_out_b", "w_k_shared",
        "w_v_shared", "w_mem_k", "w_mem_v", "ln1_g", "ln1_b", "ln2_g", "ln2_b", "w_router", "b_router", "w_gate", "w_up",
        "w_down", "mem_2", "g_mix_2", "w_in_2", "ret_decay_fwd_2", "ret_decay_bwd_2", "ret_norm_gain_2",
        "w_ret_o_2", "na_rpb_2", "w_na_o_2", "g_mem_2", "w_mem_kv_2", "w_xa_o_2", "w_out_2", "g_ffn_2",
        "w_router_group_2", "b_router_group_2", "w_router_expert_2", "b_router_expert_2", "w_exp_gate_2",
        "w_exp_up_2", "w_exp_down_2", "g_final_2"]


def kernel(**inputs):
    import concourse.bacc as _bacc
    from concourse.bass_utils import run_bass_kernel_spmd as _run

    nc = _bacc.Bacc("TRN2", target_bir_lowering=False, num_devices=1)
    arrays, args = {}, {}
    for name, value in [(n, inputs[n]) for n in _INS] + list(constants().items()):
        v = np.ascontiguousarray(value)
        arrays[f"in_{name}_dram"] = v
        args[name] = nc.dram_tensor(f"in_{name}_dram", v.shape, mybir.dt.from_np(v.dtype), kind="ExternalInput").ap()
    out = nc.dram_tensor("out_0_dram", (1, T, D), F32, kind="ExternalOutput").ap()
    build(nc, args, out)
    r = _run(nc, [arrays], core_ids=[0])
    return r.results[0]["out_0_dram"]
```
